# Optimizing a Trainium2 kernel written in Bass

```python
import jax, jax.numpy as jnp
from jax import lax
import numpy as np

D_MODEL = 1024
BATCH = 1
SEQ = 512
DEPTH = 1

N_META = 16
DN_HEADS = 8
DN_HEAD_DIM = 128
DN_WIDTH = DN_HEADS * DN_HEAD_DIM
DN_CONV = 4
CHUNK = 64
SC_WIDTH = D_MODEL
SC_CONV = 3
D_FF = -(-8 * D_MODEL // (3 * 256)) * 256
EPS = 1e-6
PROJ_WIDTHS = (DN_WIDTH, DN_WIDTH, DN_WIDTH, DN_WIDTH, DN_HEADS, DN_HEADS,
               SC_WIDTH, SC_WIDTH, SC_WIDTH, D_MODEL, D_MODEL)
IN_WIDTH = sum(PROJ_WIDTHS)

kernel_name = "hybrid_gdn_shortconv_meta_block"

def rms_norm(x, w):
    xf = x.astype(jnp.float32)
    y = xf * lax.rsqrt(jnp.mean(xf * xf, axis=-1, keepdims=True) + EPS)
    return (y * w.astype(jnp.float32)).astype(x.dtype)

def l2_normalize(x):
    xf = x.astype(jnp.float32)
    return xf * lax.rsqrt(jnp.sum(xf * xf, axis=-1, keepdims=True) + EPS)

def split_columns(t, widths):
    offs = np.cumsum(np.array(widths))[:-1].tolist()
    return jnp.split(t, offs, axis=-1)

def causal_depthwise_conv(x, w):
    k_len, ch = w.shape
    return lax.conv_general_dilated(
        x, w[:, None, :].astype(x.dtype), window_strides=(1,), padding=[(k_len - 1, 0)],
        dimension_numbers=('NWC', 'WIO', 'NWC'), feature_group_count=ch)

def chunk_gated_delta_rule(q, k, v, g, beta):
    bsz, seq_len, n_heads, dk = q.shape
    dv = v.shape[-1]
    pad = (-seq_len) % CHUNK
    n_chunks = (seq_len + pad) // CHUNK

    def front_pad(t):
        return jnp.pad(t, [(0, 0), (pad, 0)] + [(0, 0)] * (t.ndim - 2))

    def to_chunks(t):
        t = jnp.swapaxes(front_pad(t), 1, 2)
        return t.reshape(t.shape[:2] + (n_chunks, CHUNK) + t.shape[3:])

    q = to_chunks(q) * (dk ** -0.5)
    k = to_chunks(k)
    v = to_chunks(v)
    g = to_chunks(g)
    beta = to_chunks(beta)

    gc = jnp.cumsum(g, axis=-1)
    causal = jnp.tril(jnp.ones((CHUNK, CHUNK), dtype=bool))
    strict = jnp.tril(jnp.ones((CHUNK, CHUNK), dtype=bool), -1)
    decay = jnp.exp(jnp.where(causal, gc[..., :, None] - gc[..., None, :], -jnp.inf))

    k_beta = k * beta[..., None]
    v_beta = v * beta[..., None]
    a_mat = jnp.where(strict, jnp.einsum('bhncd,bhnsd->bhncs', k_beta, k) * decay, 0.0)
    eye = jnp.eye(CHUNK, dtype=a_mat.dtype)
    rhs = jnp.concatenate([v_beta, k_beta * jnp.exp(gc)[..., None]], axis=-1)
    sol = lax.linalg.triangular_solve(a_mat + eye, rhs, left_side=True, lower=True)
    u_val, w_cum = sol[..., :dv], sol[..., dv:]

    qk = jnp.einsum('bhncd,bhnsd->bhncs', q, k) * decay
    q_dec = q * jnp.exp(gc)[..., None]
    k_dec = k * jnp.exp(gc[..., -1:] - gc)[..., None]
    g_last = jnp.exp(gc[..., -1])

    def step(state, xs):
        q_i, k_i, u_i, w_i, qk_i, gl_i = xs
        v_new = u_i - jnp.einsum('bhcd,bhde->bhce', w_i, state)
        o_i = jnp.einsum('bhcd,bhde->bhce', q_i, state) + jnp.einsum('bhcs,bhse->bhce', qk_i, v_new)
        state = state * gl_i[..., None, None] + jnp.einsum('bhcd,bhce->bhde', k_i, v_new)
        return state, o_i

    xs = tuple(jnp.moveaxis(t, 2, 0) for t in (q_dec, k_dec, u_val, w_cum, qk, g_last))
    state0 = jnp.zeros((bsz, n_heads, dk, dv), dtype=jnp.float32)
    _, o = lax.scan(step, state0, xs)
    o = jnp.transpose(o, (1, 0, 3, 2, 4)).reshape(bsz, n_chunks * CHUNK, n_heads, dv)
    return o[:, pad:]

def hybrid_layer(h, norm1, w_in, conv_qkv, a_log, dt_bias, o_norm, w_dn_out, conv_sc,
                 w_sc_out, w_o, norm2, w_gate_up, w_down):
    bsz, seq_len, _ = h.shape
    xn = rms_norm(h, norm1)
    proj = xn @ w_in
    q, k, v, z, b_raw, a_raw, sc_c, sc_u, sc_b, gate_a, gate_b = split_columns(proj, PROJ_WIDTHS)

    qkv = jax.nn.silu(causal_depthwise_conv(jnp.concatenate([q, k, v], axis=-1), conv_qkv))
    q, k, v = jnp.split(qkv, 3, axis=-1)
    hd = (bsz, seq_len, DN_HEADS, DN_HEAD_DIM)
    q = l2_normalize(q.reshape(hd))
    k = l2_normalize(k.reshape(hd))
    v = v.reshape(hd).astype(jnp.float32)
    beta = jax.nn.sigmoid(b_raw.astype(jnp.float32))
    g = -jnp.exp(a_log.astype(jnp.float32)) * jax.nn.softplus(
        a_raw.astype(jnp.float32) + dt_bias.astype(jnp.float32))
    o = chunk_gated_delta_rule(q, k, v, g, beta)
    o = rms_norm(o, o_norm) * jax.nn.silu(z.reshape(hd).astype(jnp.float32))
    y_a = o.reshape(bsz, seq_len, DN_WIDTH).astype(h.dtype) @ w_dn_out

    y_b = (sc_b * causal_depthwise_conv(sc_c * sc_u, conv_sc)) @ w_sc_out

    mixed = jax.nn.sigmoid(gate_a) * y_a + jax.nn.sigmoid(gate_b) * y_b
    h = h + mixed @ w_o

    gt, up = jnp.split(rms_norm(h, norm2) @ w_gate_up, 2, axis=-1)
    return h + (jax.nn.silu(gt) * up) @ w_down

def setup_inputs(seed: int = 0) -> dict:
    key = jax.random.key(seed)
    ks = jax.random.split(key, 20)
    f32 = jnp.float32

    def nrm(k, shape, scale):
        return jax.random.normal(k, shape, f32) * scale

    def gain(k, shape):
        return 1.0 + 0.02 * jax.random.normal(k, shape, f32)

    dt = jnp.exp(jax.random.uniform(ks[5], (DEPTH, DN_HEADS), f32, np.log(1e-3), np.log(1e-1)))
    return {
        "x": nrm(ks[0], (BATCH, SEQ, D_MODEL), 1.0),
        "meta_tokens": nrm(ks[1], (N_META, D_MODEL), 1.0),
        "norm1": gain(ks[2], (DEPTH, D_MODEL)),
        "w_in": nrm(ks[3], (DEPTH, D_MODEL, IN_WIDTH), D_MODEL ** -0.5),
        "conv_qkv": nrm(ks[4], (DEPTH, DN_CONV, 3 * DN_WIDTH), DN_CONV ** -0.5),
        "a_log": jnp.log(jax.random.uniform(ks[6], (DEPTH, DN_HEADS), f32, 1.0, 16.0)),
        "dt_bias": dt + jnp.log(-jnp.expm1(-dt)),
        "o_norm": gain(ks[7], (DEPTH, DN_HEAD_DIM)),
        "w_dn_out": nrm(ks[8], (DEPTH, DN_WIDTH, D_MODEL), DN_WIDTH ** -0.5),
        "conv_sc": nrm(ks[9], (DEPTH, SC_CONV, SC_WIDTH), SC_CONV ** -0.5),
        "w_sc_out": nrm(ks[10], (DEPTH, SC_WIDTH, D_MODEL), SC_WIDTH ** -0.5),
        "w_o": nrm(ks[11], (DEPTH, D_MODEL, D_MODEL), D_MODEL ** -0.5),
        "norm2": gain(ks[12], (DEPTH, D_MODEL)),
        "w_gate_up": nrm(ks[13], (DEPTH, D_MODEL, 2 * D_FF), D_MODEL ** -0.5),
        "w_down": nrm(ks[14], (DEPTH, D_FF, D_MODEL), D_FF ** -0.5),
        "final_norm": gain(ks[15], (D_MODEL,)),
    }

def reference(x, meta_tokens, norm1, w_in, conv_qkv, a_log, dt_bias, o_norm, w_dn_out, conv_sc,
              w_sc_out, w_o, norm2, w_gate_up, w_down, final_norm):
    bsz = x.shape[0]
    meta = jnp.broadcast_to(meta_tokens[None].astype(x.dtype), (bsz, N_META, D_MODEL))
    h = jnp.concatenate([meta, x], axis=1)
    for layer in range(DEPTH):
        h = hybrid_layer(h, norm1[layer], w_in[layer], conv_qkv[layer], a_log[layer],
                         dt_bias[layer], o_norm[layer], w_dn_out[layer], conv_sc[layer],
                         w_sc_out[layer], w_o[layer], norm2[layer], w_gate_up[layer],
                         w_down[layer])
    return rms_norm(h, final_norm)[:, N_META:]


_drawn_inputs = setup_inputs


def setup_inputs(seed=0):
    import zlib

    import numpy as np

    out = dict(_drawn_inputs(seed))
    spreads = {}
    factors = {'norm1': 2.668, 'o_norm': 28.74, 'norm2': 13.072, 'final_norm': 8.188}
    for name, (base, spread) in spreads.items():
        noise = np.random.default_rng([zlib.crc32(name.encode()), seed]).standard_normal(out[name].shape)
        drawn = base * np.exp(spread * noise) if base else spread * noise
        out[name] = __import__('jax').numpy.asarray(drawn.astype(out[name].dtype))
    for name, factor in factors.items():
        out[name] = (out[name] * factor).astype(out[name].dtype)
    return out
```

```python
from contextlib import ExitStack

import concourse.bass as bass
from concourse import mybir

D = 1024
T = 512
META = 16
L = META + T
HALF = L // 2
HEADS = 8
FF = 2816
KT = D // 128
FT = FF // 128
NJ = T // 128
EPS = 1e-6
LEVELS = [2, 4, 8, 16, 32, 64]
META_LEVELS = 3

BLOCKS = [(kind, h) for h in range(HEADS) for kind in ("q", "k", "v", "z", "c", "u", "b")]
BLOCKS += [(kind, m) for m in range(KT) for kind in ("gb", "sc")]
BLOCKS += [("ga", 0)] + [x for m in range(KT - 1) for x in (("ga", m + 1), ("dn", m))] + [("dn", KT - 1)]
BLOCKS += [("wo", m) for m in range(KT)]
BLOCKS += [(kind, m) for m in range(FT) for kind in ("gate", "up")]
MAIN = len(BLOCKS)
DOWN = FT * KT // 8
STREAM = MAIN + DOWN
AT = {b: n for n, b in enumerate(BLOCKS)}
WIDE = ("q", "k", "v", "c", "u")
CONV = ("q", "k", "v", "u")
DELTA_FROM = 5
NORM1, NORM2, NORMF = 0, 8, 16
CQKV = 24
CSC = CQKV + 24 * 4
ONORM = CSC + 8 * 3
ALOG = ONORM + 1
DTB = ALOG + 8
NSMALL = DTB + 8
CI, CONE, CTRI, CREV, CLEV = 0, 1, 2, 3, 4
NCONST = CLEV + 1 + len(LEVELS)


GATES = [b for b in BLOCKS if b[0] in ("z", "gb", "ga")]
DOWN_ENDS = {MAIN + (FT * m + FT - 1) // 8 + 1: m for m in range(KT)}


def conv_number(kind, h):
    return 4 * h + CONV.index(kind)


def gate_number(kind, m):
    return GATES.index((kind, m))


def hybrid_block_kernel(nc, h_t, w_stream, w_ba, small, consts, out):
    f32 = mybir.dt.float32
    f32r = mybir.dt.float32r
    ALU = mybir.AluOpType
    ACT = mybir.ActivationFunctionType

    ctx = ExitStack()
    with ctx:
        def sem(name):
            return ctx.enter_context(nc.semaphore(name))

        def sb(name, shape, dt=f32, where=ctx):
            return where.enter_context(nc.sbuf_tensor(name, shape, dt))

        bank = [ctx.enter_context(nc.psum_tensor(f"bank{i}", [128, 512], f32)) for i in range(8)]
        big = [bank[0:2], bank[2:4]]
        dbank = bank[4:8]

        cst = sb("cst", [128, NCONST, 128])
        ident, ones, tri, rev = (cst[:, c, :] for c in (CI, CONE, CTRI, CREV))
        sm = sb("sm", [128, NSMALL])
        w_raw = sb("w_raw", [128, 3, 1024])
        w_hi = sb("w_hi", [128, 2, 1024], f32r)
        w_lo = sb("w_lo", [128, 2, 1024], f32r)
        eps = sb("eps", [128, 2])
        og_hi = sb("og_hi", [128, KT, T], f32r)
        og_lo = sb("og_lo", [128, KT, T], f32r)

        mix_mem = ExitStack()
        x_hi = sb("x_hi", [128, KT, L], f32r, mix_mem)
        x_lo = sb("x_lo", [128, KT, L], f32r, mix_mem)
        yb_hi = sb("yb_hi", [128, KT, T], f32r, mix_mem)
        yb_lo = sb("yb_lo", [128, KT, T], f32r, mix_mem)
        h_in = sb("h_in", [128, KT, L], f32, mix_mem)
        raw = sb("raw", [128, 2, 3 + L], f32, mix_mem)
        cv = sb("cv", [128, 2, L], f32, mix_mem)
        cbuf = sb("cbuf", [128, L], f32, mix_mem)
        ebuf = sb("ebuf", [128, L], f32, mix_mem)
        egate = sb("egate", [128, 2, T], f32, mix_mem)
        qkv = sb("qkv", [128, 3, L], f32, mix_mem)
        zs = sb("zs", [128, 2, T], f32, mix_mem)
        ybf = cbuf[:, 0:T]
        tile4 = [128, NJ, 128]
        sqk = sb("sqk", [128, L], f32, mix_mem)
        xd = sb("xd", tile4, f32, mix_mem)
        xt = sb("xt", tile4, f32, mix_mem)
        am = sb("am", tile4, f32, mix_mem)
        alev = sb("alev", [128, 2, NJ, 128], f32, mix_mem)
        tm = sb("tm", tile4, f32, mix_mem)
        um = sb("um", tile4, f32, mix_mem)
        pb = sb("pb", [128, 2, NJ, 128], f32, mix_mem)
        kbe = sb("kbe", tile4, f32, mix_mem)
        kdec = sb("kdec", tile4, f32, mix_mem)
        dg = kdec
        vb = sb("vb", tile4, f32, mix_mem)
        qdec = sb("qdec", tile4, f32, mix_mem)
        nwt = sqk[:, 0:T].rearrange("p (j c) -> p j c", c=128)
        vnew = sb("vnew", [128, 128], f32, mix_mem)
        state = sb("state", [128, 128], f32, mix_mem)
        g = sb("g", [128, NJ + 1, HEADS], f32, mix_mem)
        ga1 = sb("ga1", [128, NJ + 1, HEADS], f32, mix_mem)
        ga2 = sb("ga2", [128, NJ + 1, HEADS], f32, mix_mem)
        beta = sb("beta", [128, NJ + 1, HEADS], f32, mix_mem)
        gc = sb("gc", [128, NJ + 1, HEADS], f32, mix_mem)
        erev = sb("erev", [128, NJ + 1, HEADS], f32, mix_mem)
        etot = sb("etot", [128, NJ, HEADS], f32, mix_mem)
        be = sb("be", [128, NJ, HEADS], f32, mix_mem)
        nea = sb("nea", [128, HEADS], f32, mix_mem)
        on_scaled = sb("on_scaled", [128, 1], f32, mix_mem)
        wba = sb("wba", [128, KT * 16], f32, mix_mem)
        wba_hi = sb("wba_hi", [128, KT, 16], f32r, mix_mem)
        wba_lo = sb("wba_lo", [128, KT, 16], f32r, mix_mem)
        mdg = sb("mdg", [META, META], f32, mix_mem)
        mx = sb("mx", [META, META], f32, mix_mem)
        ma = sb("ma", [META, META], f32, mix_mem)
        malev = sb("malev", [META, META_LEVELS, META], f32, mix_mem)
        mt = sb("mt", [META, META], f32, mix_mem)
        mu = sb("mu", [META, META], f32, mix_mem)
        mpb = sb("mpb", [META, META_LEVELS, META], f32, mix_mem)
        mkdec = sb("mkdec", [META, 128], f32, mix_mem)
        mvb = sb("mvb", [META, 128], f32, mix_mem)
        mvnew = wba[0:META, :]
        sq1, xnf = qkv, cv
        rs1 = cbuf
        mixb = h_in
        mix_mem.close()

        ffn_mem = ctx.enter_context(ExitStack())
        h1 = sb("h1", [128, KT, T], f32, ffn_mem)
        sqa = sb("sqa", [128, T], f32, ffn_mem)
        sqt = sb("sqt", [128, 2, T], f32, ffn_mem)
        rs2 = sb("rs2", [128, T], f32, ffn_mem)
        tg = sb("tg", [128, T], f32, ffn_mem)
        sg = sb("sg", [128, T], f32, ffn_mem)
        ff = sb("ff", [128, T], f32, ffn_mem)
        f_hi = sb("f_hi", [128, FT, T], f32r, ffn_mem)
        f_lo = sb("f_lo", [128, FT, T], f32r, ffn_mem)

        const_in, small_in, ba_in = sem("const_in"), sem("small_in"), sem("ba_in")
        h_loaded = [sem(f"h_loaded{k}") for k in range(4)]
        h_again = sem("h_again")
        w_in = [sem(f"w_in{i}") for i in range(3)]
        stored = sem("stored")
        rs1_ready, k_root, q_root, o_root = (sem(n) for n in ("rs1_ready", "k_root", "q_root", "o_root"))
        zs_ready, down_done, gr_ready, mixb_ready, dn_gated = (sem(n) for n in ("zs_ready", "down_done", "gr_ready", "mixb_ready", "dn_gated"))
        act_chain, dve_chain, pool_chain = sem("act_chain"), sem("dve_chain"), sem("pool_chain")
        whi_ready, wlo_ready = sem("whi_ready"), sem("wlo_ready")
        block_done = sem("block_done")
        x_squared, x_sums, xn_ready, xhi_ready, xlo_ready = (
            sem(n) for n in ("x_squared", "x_sums", "xn_ready", "xhi_ready", "xlo_ready"))
        zeroed = sem("zeroed")
        wba_hi_ready, wba_ready, ba_done, eb_ready, az_ready, ln_ready, g_ready, cums_done, exps_ready, tokens_ready = (
            sem(n) for n in ("wba_hi_ready", "wba_ready", "ba_done", "eb_ready", "az_ready", "ln_ready", "g_ready",
                             "cums_done", "exps_ready", "tokens_ready"))
        raw_ready, conv_ready, ce_ready, cr_ready, qkv_ready = (
            sem(n) for n in ("raw_ready", "conv_ready", "ce_ready", "cr_ready", "qkv_ready"))
        ge_ready, c_ready, c_used = sem("ge_ready"), sem("c_ready"), sem("c_used")
        yb_ready, ybhi_ready, yblo_ready = sem("yb_ready"), sem("ybhi_ready"), sem("yblo_ready")
        qk_squared, v_turned, diag_ready, vb_ready, qk_sums, gc_spread = (
            sem(n) for n in ("qk_squared", "v_turned", "diag_ready", "vb_ready", "qk_sums", "gc_spread"))
        q_ready, k_ready, egc_ready, dif_ready, xd_ready = (
            sem(n) for n in ("q_ready", "k_ready", "egc_ready", "dif_ready", "xd_ready"))
        k_turned, kk_done, mpre_done, mdif_ready, mx_ready, ma_ready, mkv_ready = (
            sem(n) for n in ("k_turned", "kk_done", "mpre_done", "mdif_ready", "mx_ready", "ma_ready", "mkv_ready"))
        kd_ready, xt_ready, xb_ready, a_ready, t_ready, alev_ready = (
            sem(n) for n in ("kd_ready", "xt_ready", "xb_ready", "a_ready", "t_ready", "alev_ready"))
        qk_done, qkt_ready, qdec_ready, u_turned, u_ready = (
            sem(n) for n in ("qk_done", "qkt_ready", "qdec_ready", "u_turned", "u_ready"))
        p_done, pb_cleared, pb_ready, du_done, ut_ready = (
            sem(n) for n in ("p_done", "pb_cleared", "pb_ready", "du_done", "ut_ready"))
        mv_done, mv_ready, ms_done, w_done, nwt_ready = (
            sem(n) for n in ("mv_done", "mv_ready", "ms_done", "w_done", "nwt_ready"))
        vn_done, vn_ready, ds_done, state_ready, o_done = (
            sem(n) for n in ("vn_done", "vn_ready", "ds_done", "state_ready", "o_done"))
        o_squared, o_sums, on_ready, ogf_ready, oghi_ready, oglo_ready = (
            sem(n) for n in ("o_squared", "o_sums", "on_ready", "ogf_ready", "oghi_ready", "oglo_ready"))
        h1_ready, hnhi_ready, hnlo_ready, sqt_ready, sqa_ready, h_sums, rs2_ready = (
            sem(n) for n in ("h1_ready", "hnhi_ready", "hnlo_ready", "sqt_ready", "sqa_ready", "h_sums", "rs2_ready"))
        tg_ready, sg_ready, sg2_ready, f_ready, fhi_ready, flo_ready = (
            sem(n) for n in ("tg_ready", "sg_ready", "sg2_ready", "f_ready", "fhi_ready", "flo_ready"))
        h2_ready, h2_squared, sqf_ready, last_sums, y_ready = (
            sem(n) for n in ("h2_ready", "h2_squared", "sqf_ready", "last_sums", "y_ready"))

        def cols(ap, b, which):
            return ap.rearrange("p (g two b) -> p g two b", two=2, b=b)[:, :, which, :]

        def flat(t):
            return t[:, :, :].rearrange("p j c -> p (j c)")

        def per_chunk(t, h, first=0, n=NJ):
            return t[:, first:first + n, h].unsqueeze(2).broadcast_to([128, n, 128])

        def all_chunks(m):
            return m.unsqueeze(1).broadcast_to([128, NJ, 128])

        def wait_result_read(engine, kind, m):
            if kind in ("q", "k", "v"):
                engine.wait_ge(raw_ready, 3 * m + ("q", "k", "v").index(kind) + 1)
            elif kind in ("gb", "ga"):
                engine.wait_ge(ge_ready, gate_number(kind, m) + 1)
            else:
                engine.wait_ge({"z": zs_ready, "c": c_ready, "u": c_used, "b": yb_ready, "sc": mixb_ready, "dn": dn_gated,
                                "wo": h1_ready, "gate": tg_ready, "up": f_ready}[kind], m + 1)

        def wait_gate_used(engine, i):
            kind, m = GATES[i]
            engine.wait_ge({"z": zs_ready, "gb": mixb_ready, "ga": dn_gated}[kind], m + 1)

        block = ctx.enter_context(nc.Block())

        @block.sync
        def _(sp):
            for part in range(4):
                sp.dma_start(h_in[:, 2 * part:2 * part + 2, :], h_t[:, 2 * part:2 * part + 2, :]).then_inc(h_loaded[part], 16)
            for n in range(STREAM):
                if n >= 3:
                    sp.wait_ge(wlo_ready, n - 2)
                sp.dma_start(w_raw[:, n % 3, :], w_stream[n, :, :]).then_inc(w_in[n % 3], 16)
            for m in range(KT):
                sp.wait_ge(y_ready, m + 1)
                sp.dma_start(out[:, m, :], h1[:, m, :]).then_inc(stored, 16)
            sp.wait_ge(stored, 16 * KT)

        @block.gpsimd
        def _(pool):
            chain = [0]

            def link(ins):
                chain[0] += 1
                ins.then_inc(pool_chain, 1)
                pool.wait_ge(pool_chain, chain[0])

            nc.gpsimd.memset(raw[:, :, 0:3], 0.0)
            nc.gpsimd.memset(eps[:, 0:1], EPS)
            nc.gpsimd.memset(eps[:, 1:2], 128 * EPS)
            nc.gpsimd.memset(mpb[:, :, :], 0.0).then_inc(zeroed, 1)

            def split_weights(n):
                pool.wait_ge(whi_ready, n + 1)
                if n >= 2:
                    pool.wait_ge(block_done, n - 1)
                nc.gpsimd.tensor_tensor(w_lo[:, n % 2, :], w_raw[:, n % 3, :], w_hi[:, n % 2, :].bitcast(f32),
                                        ALU.subtract).then_inc(wlo_ready, 1)

            split_weights(0)
            for k in range(KT):
                pool.wait_ge(xhi_ready, k + 1)
                nc.gpsimd.tensor_tensor(x_lo[:, k, :], xnf[:, k % 2, 0:L], x_hi[:, k, :].bitcast(f32),
                                        ALU.subtract).then_inc(xlo_ready, 1)

            def delta_steps():
                for h in range(HEADS):
                    pool.wait_ge(tokens_ready, 1)
                    if h:
                        pool.wait_ge(oglo_ready, h)
                    nc.gpsimd.tensor_tensor(dg[:, :, :], all_chunks(ident), per_chunk(gc, h, 1), ALU.mult)
                    nc.gpsimd.tensor_tensor(mdg[:, :], ident[0:META, 0:META], gc[0:META, 0, h:h + 1].broadcast_to([META, META]),
                                            ALU.mult).then_inc(diag_ready, 1)
                    yield
                    yield
                    pool.wait_ge(xd_ready, h + 1)
                    pool.wait_ge(q_ready, h + 1)
                    nc.gpsimd.tensor_tensor(am[:, :, :], xd[:, :, :], per_chunk(beta, h, 1), ALU.mult).then_inc(xb_ready, 1)
                    nc.gpsimd.tensor_tensor(xt[:, :, :], xd[:, :, :], all_chunks(tri), ALU.mult).then_inc(xt_ready, 1)
                    pool.wait_ge(a_ready, h + 1)
                    link(nc.gpsimd.tensor_tensor(tm[:, :, :], am[:, :, :], all_chunks(cst[:, CLEV, :]), ALU.mult))
                    nc.gpsimd.tensor_tensor(tm[:, :, :], all_chunks(ident), tm[:, :, :], ALU.subtract).then_inc(t_ready, 1)
                    yield
                    nc.gpsimd.tensor_tensor(alev[:, 0, :, :], am[:, :, :], all_chunks(cst[:, CLEV + 1, :]),
                                            ALU.mult).then_inc(alev_ready, 1)
                    pool.wait_ge(ma_ready, h + 1)
                    for l in range(META_LEVELS):
                        nc.gpsimd.tensor_tensor(malev[:, l, :], ma[:, :], cst[0:META, CLEV + 1 + l, 0:META], ALU.mult)
                    link(nc.gpsimd.tensor_tensor(mt[:, :], ma[:, :], cst[0:META, CLEV, 0:META], ALU.mult))
                    nc.gpsimd.tensor_tensor(mt[:, :], ident[0:META, 0:META], mt[:, :], ALU.subtract).then_inc(t_ready, 1)
                    pool.wait_ge(q_ready, h + 1)
                    pool.wait_ge(egc_ready, h + 1)
                    nc.gpsimd.tensor_tensor(flat(qdec), flat(qdec), qkv[:, 0, META:L], ALU.mult).then_inc(qdec_ready, 1)
                    yield
                    for l in range(2):
                        if l == 1:
                            nc.gpsimd.tensor_tensor(alev[:, 1, :, :], am[:, :, :], all_chunks(cst[:, CLEV + 2, :]),
                                                    ALU.mult).then_inc(alev_ready, 1)
                        nc.gpsimd.memset(cols(pb[:, l, :, :].rearrange("p j c -> p (j c)"), LEVELS[l], 0), 0.0).then_inc(pb_cleared, 1)
                    yield
                    for l in range(len(LEVELS)):
                        yield
                        if l + 2 < len(LEVELS):
                            pool.wait_ge(du_done, len(LEVELS) * h + l + 1)
                            nc.gpsimd.memset(cols(pb[:, l % 2, :, :].rearrange("p j c -> p (j c)"), LEVELS[l + 2], 0), 0.0).then_inc(pb_cleared, 1)
                            nc.gpsimd.tensor_tensor(alev[:, l % 2, :, :], am[:, :, :], all_chunks(cst[:, CLEV + 3 + l, :]),
                                                    ALU.mult).then_inc(alev_ready, 1)
                        yield
                    for s in range(17, 27):
                        yield
                    pool.wait_ge(on_ready, h + 1)
                    pool.wait_ge(zs_ready, h + 1)
                    nc.gpsimd.tensor_tensor(flat(xd), flat(xd), zs[:, h % 2, :], ALU.mult).then_inc(ogf_ready, 1)
                    pool.wait_ge(oghi_ready, h + 1)
                    nc.gpsimd.tensor_tensor(og_lo[:, h, :], flat(xd), og_hi[:, h, :].bitcast(f32), ALU.subtract).then_inc(oglo_ready, 1)
                    yield

            def evacuate(n, kind, m):
                if kind == "wo":
                    pool.wait_ge(sqt_ready, m + 1)
                    if m == 0:
                        nc.gpsimd.tensor_copy(sqa[:, :], sqt[:, 0, :]).then_inc(sqa_ready, 1)
                    else:
                        pool.wait_ge(sqa_ready, m)
                        nc.gpsimd.tensor_tensor(sqa[:, :], sqa[:, :], sqt[:, m % 2, :], ALU.add).then_inc(sqa_ready, 1)
                if kind == "dn":
                    pool.wait_ge(ybhi_ready, KT + m + 1)
                    nc.gpsimd.tensor_tensor(yb_lo[:, m, :], ybf, yb_hi[:, m, :].bitcast(f32), ALU.subtract).then_inc(yblo_ready, 1)
                if kind == "b":
                    pool.wait_ge(ybhi_ready, m + 1)
                    nc.gpsimd.tensor_tensor(yb_lo[:, m, :], ybf, yb_hi[:, m, :].bitcast(f32), ALU.subtract).then_inc(yblo_ready, 1)
                if kind == "gate":
                    pool.wait_ge(sg_ready, m + 1)
                    nc.gpsimd.tensor_tensor(sg[:, :], sg[:, :], rs2[:, :], ALU.mult).then_inc(sg2_ready, 1)
                if kind == "up":
                    pool.wait_ge(fhi_ready, m + 1)
                    nc.gpsimd.tensor_tensor(f_lo[:, m, :], ff[:, :], f_hi[:, m, :].bitcast(f32), ALU.subtract).then_inc(flo_ready, 1)

            def silu_product(kind, h):
                i = ("q", "k", "v").index(kind)
                pool.wait_ge(cr_ready, 3 * h + i + 1)
                if h:
                    pool.wait_ge(qk_done, h)
                nc.gpsimd.tensor_tensor(qkv[:, i, :], cv[:, conv_number(kind, h) % 2, :], ebuf[:, :], ALU.mult).then_inc(qkv_ready, 1)

            delta = delta_steps()
            for n in range(STREAM + 1):
                if 1 <= n <= MAIN:
                    evacuate(n - 1, *BLOCKS[n - 1])
                for q in range(4):
                    if n >= DELTA_FROM:
                        next(delta, None)
                    if q == 0 and n + 1 < STREAM:
                        split_weights(n + 1)
                    if q == 1 and 2 <= n and n - 2 < MAIN and BLOCKS[n - 2][0] in ("q", "k", "v"):
                        silu_product(*BLOCKS[n - 2])
                if n not in DOWN_ENDS:
                    continue
                m = DOWN_ENDS[n]
                pool.wait_ge(h2_squared, m + 1)
                if m == 0:
                    nc.gpsimd.tensor_copy(sqa[:, :], sqt[:, 0, :]).then_inc(sqf_ready, 1)
                else:
                    pool.wait_ge(sqf_ready, m)
                    nc.gpsimd.tensor_tensor(sqa[:, :], sqa[:, :], sqt[:, m % 2, :], ALU.add).then_inc(sqf_ready, 1)

        @block.scalar
        def _(act):
            chain = [0]

            def link(ins):
                chain[0] += 1
                ins.then_inc(act_chain, 1)
                act.wait_ge(act_chain, chain[0])

            def inverse_root(to, sums, scale, eps_column):
                link(nc.scalar.activation(to, sums, ACT.Ln, scale=scale, bias=eps[:, eps_column:eps_column + 1]))
                return nc.scalar.activation(to, to, ACT.Exp, scale=-0.5)

            nc.scalar.preload_act_table_set("natural_log_exp_and_others")
            act.dma_start(sm[:, :], small[:, :]).then_inc(small_in, 16)
            act.dma_start(cst[:, :, :], consts[:, :, :]).then_inc(const_in, 16)
            act.dma_start(wba[:, :], w_ba[:, :]).then_inc(ba_in, 16)
            for k in range(KT):
                act.wait_ge(h_loaded[k // 2], 16)
                if k >= 2:
                    act.wait_ge(x_sums, k - 1)
                nc.scalar.activation(sq1[:, k % 2, :], h_in[:, k, :], ACT.Square).then_inc(x_squared, 1)
            act.wait_ge(x_sums, KT)
            act.wait_ge(zeroed, 1)
            for s in range(2):
                ins = inverse_root(rs1[:, s * HALF:(s + 1) * HALF], big[0][s][:, 0:HALF], 1.0 / D, 0)
            ins.then_inc(rs1_ready, 1)

            def split_weights(n):
                act.wait_ge(w_in[n % 3], 16 * (n // 3 + 1))
                if n >= 2:
                    act.wait_ge(block_done, n - 1)
                nc.scalar.activation(w_hi[:, n % 2, :], w_raw[:, n % 3, :], ACT.Copy).then_inc(whi_ready, 1)

            split_weights(0)
            act.wait_ge(ba_in, 16)
            nc.scalar.activation(wba_hi[:, :, :].rearrange("p k c -> p (k c)"), wba[:, :], ACT.Copy).then_inc(wba_hi_ready, 1)
            for k in range(KT):
                act.wait_ge(xn_ready, k + 1)
                nc.scalar.activation(x_hi[:, k, :], xnf[:, k % 2, 0:L], ACT.Copy).then_inc(xhi_ready, 1)
            def token_factors():
                act.wait_ge(ba_done, 1)
                ba = dbank[0][:, 0:16 * (NJ + 1)].rearrange("p (j c) -> p j c", c=16)
                nc.scalar.activation(beta[:, :, :], ba[:, :, 0:HEADS], ACT.Exp, scale=-1.0).then_inc(eb_ready, 1)
                act.wait_ge(small_in, 16)
                nc.scalar.activation(nea[:, :], sm[:, ALOG:ALOG + HEADS], ACT.Exp).then_inc(eb_ready, 1)
                act.wait_ge(az_ready, 1)
                link(nc.scalar.activation(ga2[:, :, :], ga1[:, :, :], ACT.Abs))
                link(nc.scalar.activation(ga2[:, :, :], ga2[:, :, :], ACT.Exp, scale=-1.0))
                nc.scalar.activation(ga2[:, :, :], ga2[:, :, :], ACT.Ln, bias=1.0).then_inc(ln_ready, 1)

            def token_decays():
                act.wait_ge(cums_done, 1)
                cums = dbank[1]
                nc.scalar.activation(be[:, :, :], cums[:, 0:32].rearrange("p (j c) -> p j c", c=HEADS), ACT.Exp)
                nc.scalar.activation(erev[:, 1:, :], cums[:, 32:64].rearrange("p (j c) -> p j c", c=HEADS), ACT.Exp)
                nc.scalar.activation(etot[:, :, :], cums[:, 64:96].rearrange("p (j c) -> p j c", c=HEADS), ACT.Exp)
                nc.scalar.activation(gc[:, 1:, :], cums[:, 0:32].rearrange("p (j c) -> p j c", c=HEADS), ACT.Copy)
                nc.scalar.activation(gc[0:META, 0, :], cums[0:META, 96:104], ACT.Copy)
                nc.scalar.activation(erev[0:META, 0, :], cums[0:META, 104:112], ACT.Exp).then_inc(exps_ready, 1)

            def delta_steps():
                for h in range(HEADS):
                    act.wait_ge(qkv_ready, 3 * h + 3)
                    if h:
                        act.wait_ge(oglo_ready, h)
                    nc.scalar.activation(flat(xt), qkv[:, 0, META:L], ACT.Square)
                    nc.scalar.activation(sqk[:, :], qkv[:, 1, :], ACT.Square).then_inc(qk_squared, 1)
                    yield
                    act.wait_ge(qk_sums, h + 1)
                    inverse_root(sqk[:, 0:META], dbank[2][:, 0:META], 1.0, 0)
                    inverse_root(sqk[:, META:L], dbank[1][:, :], 1.0, 0).then_inc(k_root, 1)
                    inverse_root(flat(xt), dbank[0][:, :], 1.0, 0).then_inc(q_root, 1)
                    act.wait_ge(dif_ready, h + 1)
                    nc.scalar.activation(flat(qdec), dbank[3][:, :], ACT.Exp).then_inc(egc_ready, 1)
                    link(nc.scalar.activation(flat(xd), flat(xd), ACT.Abs))
                    nc.scalar.activation(flat(xd), flat(xd), ACT.Exp, scale=-1.0).then_inc(xd_ready, 1)
                    yield
                    act.wait_ge(mdif_ready, h + 1)
                    link(nc.scalar.activation(mx[:, :], mx[:, :], ACT.Abs))
                    nc.scalar.activation(mx[:, :], mx[:, :], ACT.Exp, scale=-1.0).then_inc(mx_ready, 1)
                    yield
                    yield
                    act.wait_ge(u_turned, h + 1)
                    nc.scalar.activation(mu[:, :], dbank[1][0:META, 0:META], ACT.Copy)
                    nc.scalar.activation(flat(um), dbank[0][:, :], ACT.Copy).then_inc(u_ready, 1)
                    yield
                    for l, b in enumerate(LEVELS):
                        done = len(LEVELS) * h + l + 1
                        act.wait_ge(p_done, done)
                        act.wait_ge(pb_cleared, done)
                        if l < META_LEVELS:
                            nc.scalar.activation(cols(mpb[:, l, :], b, 1), dbank[1][0:META, 256:264], ACT.Copy)
                        nc.scalar.activation(cols(pb[:, l % 2, :, :].rearrange("p j c -> p (j c)"), b, 1),
                                             dbank[1][:, 0:256].rearrange("p (g b) -> p g b", b=b), ACT.Copy).then_inc(pb_ready, 1)
                        if l == META_LEVELS:
                            act.wait_ge(mv_done, h + 1)
                            nc.scalar.activation(mvnew, dbank[1][0:META, 256:384], ACT.Copy).then_inc(mv_ready, 1)
                        yield
                        yield
                    act.wait_ge(w_done, h + 1)
                    nc.scalar.activation(sqk[:, 0:T], dbank[0][:, :], ACT.Copy, scale=-1.0).then_inc(nwt_ready, 1)
                    yield
                    for j in range(NJ):
                        act.wait_ge(vn_done, NJ * h + j + 1)
                        nc.scalar.activation(vnew[:, :], dbank[1][:, 0:128], ACT.Copy).then_inc(vn_ready, 1)
                        yield
                        yield
                    act.wait_ge(o_done, h + 1)
                    nc.scalar.activation(flat(dg), dbank[3][:, :], ACT.Square).then_inc(o_squared, 1)
                    yield
                    act.wait_ge(o_sums, h + 1)
                    inverse_root(flat(dg), dbank[0][:, :], 1.0, 1).then_inc(o_root, 1)
                    act.wait_ge(ogf_ready, h + 1)
                    nc.scalar.activation(og_hi[:, h, :], flat(xd), ACT.Copy).then_inc(oghi_ready, 1)
                    yield

            def evacuate(n, kind, m):
                p = big[n % 2]
                act.wait_ge(block_done, n + 1)
                if kind in ("q", "k", "v"):
                    c = conv_number(kind, m)
                    if c >= 2:
                        act.wait_ge(conv_ready, c - 1)
                    else:
                        act.wait_ge(zeroed, 1)
                    nc.scalar.activation(raw[:, c % 2, 3:3 + HALF], p[0][:, 0:HALF], ACT.Copy)
                    nc.scalar.activation(raw[:, c % 2, 3 + HALF:3 + L], p[1][:, 0:HALF],
                                         ACT.Copy).then_inc(raw_ready, 1)
                if kind == "c":
                    if m:
                        act.wait_ge(yblo_ready, m)
                    nc.scalar.activation(cbuf[:, 0:HALF], p[0][:, 0:HALF], ACT.Copy)
                    nc.scalar.activation(cbuf[:, HALF:L], p[1][:, 0:HALF],
                                         ACT.Copy).then_inc(c_ready, 1)
                if kind in ("z", "gb", "ga"):
                    i = gate_number(kind, m)
                    if i >= 2:
                        wait_gate_used(act, i - 2)
                    nc.scalar.activation(egate[:, i % 2, :], p[0][:, :], ACT.Exp, scale=-1.0).then_inc(ge_ready, 1)
                if kind in ("b", "dn"):
                    i = m if kind == "b" else KT + m
                    act.wait_ge(yb_ready, i + 1)
                    nc.scalar.activation(yb_hi[:, m, :], ybf, ACT.Copy).then_inc(ybhi_ready, 1)
                if kind == "wo":
                    act.wait_ge(h1_ready, m + 1)
                    if m >= 2:
                        act.wait_ge(sqa_ready, m - 1)
                    nc.scalar.activation(sqt[:, m % 2, :], h1[:, m, :], ACT.Square).then_inc(sqt_ready, 1)
                    nc.scalar.activation(og_hi[:, m, :], h1[:, m, :], ACT.Copy,
                                         scale=sm[:, NORM2 + m:NORM2 + m + 1]).then_inc(hnhi_ready, 1)
                if kind == "gate":
                    if m == 0:
                        act.wait_ge(h_sums, 1)
                        inverse_root(rs2[:, :], dbank[0][:, :], 1.0 / D, 0).then_inc(rs2_ready, 1)
                    act.wait_ge(tg_ready, m + 1)
                    if m:
                        act.wait_ge(f_ready, m)
                    nc.scalar.activation(sg[:, :], tg[:, :], ACT.Silu).then_inc(sg_ready, 1)
                if kind == "up":
                    act.wait_ge(f_ready, m + 1)
                    nc.scalar.activation(f_hi[:, m, :], ff[:, :], ACT.Copy).then_inc(fhi_ready, 1)

            def silu_exp(kind, h):
                c = conv_number(kind, h)
                i = 3 * h + ("q", "k", "v").index(kind)
                act.wait_ge(conv_ready, c + 1)
                if i:
                    act.wait_ge(qkv_ready, i)
                nc.scalar.activation(ebuf[:, :], cv[:, c % 2, :], ACT.Exp, scale=-1.0).then_inc(ce_ready, 1)

            delta = delta_steps()
            for n in range(STREAM + 1):
                if 1 <= n <= MAIN:
                    evacuate(n - 1, *BLOCKS[n - 1])
                if AT["dn", KT - 2] == n:
                    act.wait_ge(block_done, AT["ga", KT - 1] + 1)
                    act.dma_start(h1[:, :, :], h_t[:, :, META:L]).then_inc(h_again, 16)
                for q in range(4):
                    if n >= DELTA_FROM:
                        next(delta, None)
                    if q == 0 and n + 1 < STREAM:
                        split_weights(n + 1)
                    if q == 1 and 2 <= n and n - 2 < MAIN and BLOCKS[n - 2][0] in ("q", "k", "v"):
                        silu_exp(*BLOCKS[n - 2])
                if n == 1:
                    token_factors()
                if n == 2:
                    token_decays()
                if n in DOWN_ENDS:
                    m = DOWN_ENDS[n]
                    act.wait_ge(h2_ready, m + 1)
                    if m >= 2:
                        act.wait_ge(sqf_ready, m - 1)
                    nc.scalar.activation(sqt[:, m % 2, :], h1[:, m, :], ACT.Square).then_inc(h2_squared, 1)

            act.wait_ge(last_sums, 1)
            inverse_root(rs2[:, :], dbank[0][:, :], 1.0 / D, 0).then_inc(rs2_ready, 1)

        @block.vector
        def _(dve):
            chain = [0]

            def link(ins):
                chain[0] += 1
                ins.then_inc(dve_chain, 1)
                dve.wait_ge(dve_chain, chain[0])

            def inverse_of_one_more(e):
                link(nc.vector.tensor_scalar(e, e, 1.0, None, ALU.add))
                return nc.vector.reciprocal(e, e)

            def mult(to, a, b):
                return nc.vector.tensor_tensor(to, a, b, ALU.mult)

            dve.wait_ge(small_in, 16)
            link(nc.vector.tensor_scalar(on_scaled[:, :], sm[:, ONORM:ONORM + 1], float(128) ** 0.5, None, ALU.mult))
            dve.wait_ge(rs1_ready, 1)
            for k in range(KT):
                if k >= 2:
                    dve.wait_ge(xlo_ready, k - 1)
                nc.vector.scalar_tensor_tensor(xnf[:, k % 2, :], h_in[:, k, :], sm[:, NORM1 + k:NORM1 + k + 1], rs1[:, :],
                                               ALU.mult, ALU.mult).then_inc(xn_ready, 1)
            dve.wait_ge(wba_hi_ready, 1)
            nc.vector.tensor_tensor(wba_lo[:, :, :].rearrange("p k c -> p (k c)"), wba[:, :],
                                    wba_hi[:, :, :].rearrange("p k c -> p (k c)").bitcast(f32), ALU.subtract).then_inc(wba_ready, 1)

            def token_factors():
                dve.wait_ge(ba_done, 1)
                dve.wait_ge(eb_ready, 1)
                ba = dbank[0][:, 0:16 * (NJ + 1)].rearrange("p (j c) -> p j c", c=16)
                dtb = sm[:, DTB:DTB + HEADS].unsqueeze(1).broadcast_to([128, NJ + 1, HEADS])
                nc.vector.tensor_tensor(ga1[:, :, :], ba[:, :, HEADS:16], dtb, ALU.add).then_inc(az_ready, 1)
                dve.wait_ge(eb_ready, 2)
                link(inverse_of_one_more(beta[:, :, :]))
                link(nc.vector.tensor_scalar(nea[:, :], nea[:, :], -1.0, None, ALU.mult))
                dve.wait_ge(ln_ready, 1)
                link(nc.vector.tensor_scalar(ga1[:, :, :], ga1[:, :, :], 0.0, None, ALU.max))
                link(nc.vector.tensor_tensor(ga1[:, :, :], ga1[:, :, :], ga2[:, :, :], ALU.add))
                mult(g[:, :, :], ga1[:, :, :], nea[:, :].unsqueeze(1).broadcast_to([128, NJ + 1, HEADS])).then_inc(g_ready, 1)

            def token_decays():
                dve.wait_ge(exps_ready, 1)
                mult(be[:, :, :], be[:, :, :], beta[:, 1:, :]).then_inc(tokens_ready, 1)

            def delta_steps():
                for h in range(HEADS):
                    dve.wait_ge(tokens_ready, 1)
                    dve.wait_ge(v_turned, h + 1)
                    if h:
                        dve.wait_ge(oglo_ready, h)
                    mult(vb[:, :, :], dbank[0][:, :].rearrange("p (j c) -> p j c", c=128), per_chunk(beta, h, 1)).then_inc(vb_ready, 1)
                    yield
                    dve.wait_ge(gc_spread, h + 1)
                    nc.vector.tensor_tensor(xd[:, :, :], dbank[3][:, :].rearrange("p (j c) -> p j c", c=128),
                                            per_chunk(gc, h, 1), ALU.subtract).then_inc(dif_ready, 1)
                    dve.wait_ge(k_root, h + 1)
                    mult(qkv[:, 1, :], qkv[:, 1, :], sqk[:, :]).then_inc(k_ready, 1)
                    dve.wait_ge(q_root, h + 1)
                    nc.vector.scalar_tensor_tensor(qkv[:, 0, META:L], qkv[:, 0, META:L], float(128) ** -0.5, flat(xt),
                                                   ALU.mult, ALU.mult).then_inc(q_ready, 1)
                    yield
                    dve.wait_ge(mpre_done, h + 1)
                    mbank = dbank[2]
                    nc.vector.tensor_tensor(mx[:, :], mbank[0:META, 272:288], gc[0:META, 0, h:h + 1].broadcast_to([META, META]),
                                            ALU.subtract).then_inc(mdif_ready, 1)
                    dve.wait_ge(k_turned, h + 1)
                    kt = dbank[0][:, :].rearrange("p (j c) -> p j c", c=128)
                    mult(kbe[:, :, :], kt, per_chunk(be, h))
                    mult(kdec[:, :, :], kt, per_chunk(erev, h, 1)).then_inc(kd_ready, 1)
                    dve.wait_ge(kk_done, h + 1)
                    dve.wait_ge(xb_ready, h + 1)
                    mult(flat(am), dbank[1][:, :], flat(am)).then_inc(a_ready, 1)
                    nc.vector.tensor_scalar(mkdec[:, :], mbank[0:META, 0:128], erev[0:META, 0, h:h + 1], None, ALU.mult)
                    nc.vector.tensor_scalar(mvb[:, :], mbank[0:META, 128:256], beta[0:META, 0, h:h + 1], None,
                                            ALU.mult).then_inc(mkv_ready, 1)
                    dve.wait_ge(mx_ready, h + 1)
                    nc.vector.scalar_tensor_tensor(ma[:, :], mbank[0:META, 256:272], beta[0:META, 0, h:h + 1], mx[:, :],
                                                   ALU.mult, ALU.mult).then_inc(ma_ready, 1)
                    yield
                    dve.wait_ge(qk_done, h + 1)
                    dve.wait_ge(xt_ready, h + 1)
                    mult(flat(xt), dbank[3][:, :], flat(xt)).then_inc(qkt_ready, 1)
                    yield
                    yield
                    for l, b in enumerate(LEVELS):
                        yield
                        dve.wait_ge(du_done, len(LEVELS) * h + l + 1)
                        if l == META_LEVELS:
                            dve.wait_ge(ms_done, h + 1)
                            nc.vector.tensor_copy(state[:, :], dbank[2][:, 256:384]).then_inc(state_ready, 1)
                        if l < META_LEVELS:
                            u = cols(mu[:, :], b, 1)
                            nc.vector.tensor_tensor(u, u, dbank[2][0:META, 256:264].rearrange("p (g b) -> p g b", b=b), ALU.subtract)
                        if l < META_LEVELS - 1:
                            t = cols(mt[:, :], b, 0)
                            nc.vector.tensor_tensor(t, t, dbank[3][0:META, 256:264].rearrange("p (g b) -> p g b", b=b), ALU.subtract)
                        if l < len(LEVELS) - 1:
                            t = cols(flat(tm), b, 0)
                            nc.vector.tensor_tensor(t, t, dbank[3][:, 0:256].rearrange("p (g b) -> p g b", b=b), ALU.subtract)
                        u = cols(flat(um), b, 1)
                        nc.vector.tensor_tensor(u, u, dbank[2][:, 0:256].rearrange("p (g b) -> p g b", b=b),
                                                ALU.subtract).then_inc(ut_ready, 1)
                        yield
                    yield
                    for j in range(NJ):
                        yield
                        if j < NJ - 1:
                            dve.wait_ge(ds_done, (NJ - 1) * h + j + 1)
                            dve.wait_ge(state_ready, NJ * h + j + 1)
                            nc.vector.scalar_tensor_tensor(state[:, :], state[:, :], etot[:, j, h:h + 1], dbank[2][:, 0:128],
                                                           ALU.mult, ALU.add).then_inc(state_ready, 1)
                        yield
                    yield
                    dve.wait_ge(o_root, h + 1)
                    mult(flat(xd), dbank[3][:, :], flat(dg)).then_inc(on_ready, 1)
                    yield

            def convolve(c, first_column, taps):
                to, x = cv[:, c % 2, :], raw[:, c % 2, :]
                link(nc.vector.tensor_scalar(to, x[:, first_column:first_column + L], taps[:, 0:1], None, ALU.mult))
                n = taps.shape[1]
                for j in range(1, n):
                    ins = nc.vector.scalar_tensor_tensor(to, x[:, first_column + j:first_column + j + L], taps[:, j:j + 1], to,
                                                         ALU.mult, ALU.add)
                    if j < n - 1:
                        link(ins)
                ins.then_inc(conv_ready, 1)

            def evacuate(n, kind, m):
                p = big[n % 2]
                dve.wait_ge(block_done, n + 1)
                if kind in ("q", "k", "v"):
                    i = ("q", "k", "v").index(kind)
                    c = conv_number(kind, m)
                    dve.wait_ge(raw_ready, 3 * m + i + 1)
                    if c < 2:
                        dve.wait_ge(xlo_ready, KT)
                    elif kind != "k":
                        dve.wait_ge(qkv_ready, 3 * m + (i > 0))
                    convolve(c, 0, sm[:, CQKV + 4 * (8 * i + m):CQKV + 4 * (8 * i + m) + 4])
                if kind == "z":
                    i = gate_number(kind, m)
                    dve.wait_ge(ge_ready, i + 1)
                    link(inverse_of_one_more(egate[:, i % 2, :]))
                    if m >= 2:
                        dve.wait_ge(oglo_ready, m - 1)
                    nc.vector.scalar_tensor_tensor(zs[:, m % 2, :], egate[:, i % 2, :], on_scaled[:, 0:1], p[0][:, :], ALU.mult,
                                                   ALU.mult).then_inc(zs_ready, 1)
                if kind == "u":
                    c = conv_number(kind, m)
                    dve.wait_ge(c_ready, m + 1)
                    if m == 0:
                        dve.wait_ge(zeroed, 1)
                    mult(raw[:, c % 2, 3:3 + HALF], p[0][:, 0:HALF], cbuf[:, 0:HALF])
                    mult(raw[:, c % 2, 3 + HALF:3 + L], p[1][:, 0:HALF], cbuf[:, HALF:L]).then_inc(c_used, 1)
                    dve.wait_ge(c_used, m + 1)
                    dve.wait_ge(qkv_ready, 3 * m + 2)
                    convolve(c, 1, sm[:, CSC + 3 * m:CSC + 3 * m + 3])
                if kind == "b":
                    if m:
                        dve.wait_ge(yblo_ready, m)
                    dve.wait_ge(conv_ready, 4 * m + 4)
                    mult(ybf, p[0][:, :], cv[:, conv_number("u", m) % 2, META:L]).then_inc(yb_ready, 1)
                if kind in ("gb", "ga"):
                    i = gate_number(kind, m)
                    dve.wait_ge(ge_ready, i + 1)
                    inverse_of_one_more(egate[:, i % 2, :]).then_inc(gr_ready, 1)
                if kind == "sc":
                    i = gate_number("gb", m)
                    dve.wait_ge(gr_ready, i - HEADS + 1)
                    mult(mixb[:, m, 0:T], p[0][:, :], egate[:, i % 2, :]).then_inc(mixb_ready, 1)
                if kind == "dn":
                    i = gate_number("ga", m)
                    dve.wait_ge(gr_ready, i - HEADS + 1)
                    dve.wait_ge(yblo_ready, KT + m)
                    mult(ybf, p[0][:, :], egate[:, i % 2, :]).then_inc(dn_gated, 1)
                    dve.wait_ge(dn_gated, m + 1)
                    dve.wait_ge(mixb_ready, m + 1)
                    nc.vector.tensor_tensor(ybf, ybf, mixb[:, m, 0:T], ALU.add).then_inc(yb_ready, 1)
                if kind == "wo":
                    dve.wait_ge(h_again, 16)
                    nc.vector.tensor_tensor(h1[:, m, :], p[0][:, :], h1[:, m, :], ALU.add).then_inc(h1_ready, 1)
                    dve.wait_ge(hnhi_ready, m + 1)
                    nc.vector.scalar_tensor_tensor(og_lo[:, m, :], h1[:, m, :], sm[:, NORM2 + m:NORM2 + m + 1],
                                                   og_hi[:, m, :].bitcast(f32), ALU.mult, ALU.subtract).then_inc(hnlo_ready, 1)
                if kind == "gate":
                    if m == 0:
                        dve.wait_ge(rs2_ready, 1)
                    else:
                        dve.wait_ge(sg_ready, m)
                    mult(tg[:, :], p[0][:, :], rs2[:, :]).then_inc(tg_ready, 1)
                if kind == "up":
                    if m:
                        dve.wait_ge(flo_ready, m)
                    dve.wait_ge(sg2_ready, m + 1)
                    mult(ff[:, :], p[0][:, :], sg[:, :]).then_inc(f_ready, 1)

            def silu_sigmoid(kind, h):
                i = 3 * h + ("q", "k", "v").index(kind)
                dve.wait_ge(ce_ready, i + 1)
                inverse_of_one_more(ebuf[:, :]).then_inc(cr_ready, 1)

            delta = delta_steps()
            for n in range(STREAM + 1):
                if 1 <= n <= MAIN:
                    evacuate(n - 1, *BLOCKS[n - 1])
                for q in range(4):
                    if n >= DELTA_FROM:
                        next(delta, None)
                    if q == 1 and 2 <= n and n - 2 < MAIN and BLOCKS[n - 2][0] in ("q", "k", "v"):
                        silu_sigmoid(*BLOCKS[n - 2])
                if n == 1:
                    token_factors()
                if n == 2:
                    token_decays()
                if n in DOWN_ENDS:
                    m = DOWN_ENDS[n]
                    if FT * (m + 1) % 8 == 0:
                        dve.wait_ge(block_done, n)
                    else:
                        dve.wait_ge(down_done, m + 1 - sum(FT * (i + 1) % 8 == 0 for i in range(m)))
                    nc.vector.tensor_tensor(h1[:, m, :], big[m % 2][0][:, :], h1[:, m, :],
                                            ALU.add).then_inc(h2_ready, 1)
            dve.wait_ge(rs2_ready, 2)
            for m in range(KT):
                nc.vector.scalar_tensor_tensor(h1[:, m, :], h1[:, m, :], sm[:, NORMF + m:NORMF + m + 1], rs2[:, :], ALU.mult,
                                               ALU.mult).then_inc(y_ready, 1)

        @block.tensor
        def _(pe):
            mm = nc.tensor.matmul

            def products(outs, n, k, x_h, x_l, first, last, slot_tile=None):
                t = k if slot_tile is None else slot_tile
                wh = w_hi[:, n % 2, t * 128:(t + 1) * 128]
                wl = w_lo[:, n % 2, t * 128:(t + 1) * 128]
                for w, xs, a in ((wh, x_h, 0), (wh, x_l, 1), (wl, x_h, 2)):
                    for o, x in zip(outs, xs):
                        ins = mm(o, w, x, start=first and a == 0, stop=last and a == 2)
                return ins

            pe.wait_ge(const_in, 16)
            for k in range(KT):
                pe.wait_ge(x_squared, k + 1)
                for s in range(2):
                    ins = mm(big[0][s][:, 0:HALF], ones, sq1[:, k % 2, s * HALF:(s + 1) * HALF], start=k == 0, stop=k == KT - 1)
                ins.then_inc(x_sums, 1)

            def token_projections():
                pe.wait_ge(wba_ready, 1)
                for j in range(NJ + 1):
                    at = slice(0, 128) if j == 0 else slice(META + 128 * (j - 1), META + 128 * j)
                    o = dbank[0][:, 16 * j:16 * j + 16]
                    for k in range(KT):
                        mm(o, x_hi[:, k, at], wba_hi[:, k, :], start=k == 0, stop=False)
                        mm(o, x_hi[:, k, at], wba_lo[:, k, :], start=False, stop=False)
                        ins = mm(o, x_lo[:, k, at], wba_hi[:, k, :], start=False, stop=k == KT - 1)
                ins.then_inc(ba_done, 1)

            def token_sums():
                pe.wait_ge(g_ready, 1)
                gs = g[:, 1:, :].rearrange("p j h -> p (j h)")
                mm(dbank[1][:, 0:32], tri, gs, start=True, stop=True)
                mm(dbank[1][:, 32:64], rev, gs, start=True, stop=True)
                mm(dbank[1][:, 64:96], ones, gs, start=True, stop=True)
                mm(dbank[1][0:META, 96:104], tri[0:META, 0:META], g[0:META, 0, :], start=True, stop=True)
                mm(dbank[1][0:META, 104:112], rev[0:META, 0:META], g[0:META, 0, :], start=True, stop=True).then_inc(cums_done, 1)

            def delta_steps():
                turn = nc.tensor.transpose
                c128 = [slice(128 * j, 128 * (j + 1)) for j in range(NJ)]
                c64 = [slice(64 * j, 64 * (j + 1)) for j in range(NJ)]
                tok = [slice(META + 128 * j, META + 128 * (j + 1)) for j in range(NJ)]
                qh, kh, vh = qkv[:, 0, :], qkv[:, 1, :], qkv[:, 2, :]
                for h in range(HEADS):
                    pe.wait_ge(tokens_ready, 1)
                    pe.wait_ge(qkv_ready, 3 * h + 3)
                    if h:
                        pe.wait_ge(oglo_ready, h)
                    for j in range(NJ):
                        ins = turn(dbank[0][:, c128[j]], vh[:, tok[j]], ident)
                    ins.then_inc(v_turned, 1)
                    yield
                    pe.wait_ge(diag_ready, h + 1)
                    mm(dbank[3][:, :], ones, flat(dg), start=True, stop=True).then_inc(gc_spread, 1)
                    pe.wait_ge(vb_ready, h + 1)
                    pe.wait_ge(qk_squared, h + 1)
                    mm(dbank[0][:, :], ones, flat(xt), start=True, stop=True)
                    mm(dbank[1][:, :], ones, sqk[:, META:L], start=True, stop=True)
                    mm(dbank[2][:, 0:META], ones, sqk[:, 0:META], start=True, stop=True).then_inc(qk_sums, 1)
                    yield
                    pe.wait_ge(k_ready, h + 1)
                    pe.wait_ge(q_root, h + 1)
                    turn(dbank[2][:, 0:128], kh[:, 0:128], ident)
                    turn(dbank[2][:, 128:256], vh[:, 0:128], ident)
                    mm(dbank[2][0:META, 256:272], kh[:, 0:META], kh[:, 0:META], start=True, stop=True)
                    mm(dbank[2][0:META, 272:288], ones[0:META, 0:META], mdg[:, :], start=True, stop=True).then_inc(mpre_done, 1)
                    for j in range(NJ):
                        ins = turn(dbank[0][:, c128[j]], kh[:, tok[j]], ident)
                    ins.then_inc(k_turned, 1)
                    for j in range(NJ):
                        ins = mm(dbank[1][:, c128[j]], kh[:, tok[j]], kh[:, tok[j]], start=True, stop=True)
                    ins.then_inc(kk_done, 1)
                    yield
                    pe.wait_ge(q_ready, h + 1)
                    pe.wait_ge(egc_ready, h + 1)
                    pe.wait_ge(dif_ready, h + 1)
                    for j in range(NJ):
                        ins = mm(dbank[3][:, c128[j]], kh[:, tok[j]], qh[:, tok[j]], start=True, stop=True)
                    ins.then_inc(qk_done, 1)
                    yield
                    pe.wait_ge(t_ready, 2 * h + 2)
                    pe.wait_ge(kd_ready, h + 1)
                    pe.wait_ge(a_ready, h + 1)
                    mm(dbank[1][0:META, 0:META], mt[:, :], ident[0:META, 0:META], start=True, stop=True)
                    for j in range(NJ):
                        ins = turn(dbank[0][:, c128[j]], tm[:, j, :], ident)
                    ins.then_inc(u_turned, 1)
                    yield
                    for l, b in enumerate(LEVELS):
                        done = len(LEVELS) * h + l
                        if l == 0:
                            pe.wait_ge(u_ready, h + 1)
                        else:
                            pe.wait_ge(ut_ready, done)
                        pe.wait_ge(alev_ready, done + 1)
                        if l == META_LEVELS:
                            mm(dbank[1][0:META, 256:384], mu[:, :], mvb[:, :], start=True, stop=True).then_inc(mv_done, 1)
                        if l < META_LEVELS:
                            mm(dbank[1][0:META, 256:264], malev[:, l, :], cols(mu[:, :], b, 1), start=True, stop=True)
                        for j in range(NJ):
                            ins = mm(dbank[1][:, c64[j]], alev[:, l % 2, j, :], cols(um[:, j, :], b, 1), start=True, stop=True)
                        ins.then_inc(p_done, 1)
                        yield
                        pe.wait_ge(pb_ready, done + 1)
                        if l == 0:
                            pe.wait_ge(mkv_ready, h + 1)
                            pe.wait_ge(ma_ready, h + 1)
                            pe.wait_ge(qkt_ready, h + 1)
                        if l == META_LEVELS:
                            pe.wait_ge(mv_ready, h + 1)
                            mm(dbank[2][:, 256:384], mkdec[:, :], mvnew, start=True, stop=True).then_inc(ms_done, 1)
                        if l < META_LEVELS:
                            mm(dbank[2][0:META, 256:264], mt[:, :], cols(mpb[:, l, :], b, 1), start=True, stop=True)
                        if l < META_LEVELS - 1:
                            mm(dbank[3][0:META, 256:264], mpb[:, l, :], cols(mt[:, :], b, 0), start=True, stop=True)
                        for j in range(NJ):
                            ins = mm(dbank[2][:, c64[j]], tm[:, j, :], cols(pb[:, l % 2, j, :], b, 1), start=True, stop=True)
                            if l < len(LEVELS) - 1:
                                ins = mm(dbank[3][:, c64[j]], pb[:, l % 2, j, :], cols(tm[:, j, :], b, 0), start=True, stop=True)
                        ins.then_inc(du_done, 1)
                        yield
                    pe.wait_ge(ut_ready, len(LEVELS) * (h + 1))
                    for j in range(NJ):
                        ins = mm(dbank[0][:, c128[j]], kbe[:, j, :], um[:, j, :], start=True, stop=True)
                    ins.then_inc(w_done, 1)
                    yield
                    for j in range(NJ):
                        if j == 0:
                            pe.wait_ge(nwt_ready, h + 1)
                            pe.wait_ge(qdec_ready, h + 1)
                        pe.wait_ge(state_ready, NJ * h + j + 1)
                        mm(dbank[1][:, 0:128], um[:, j, :], vb[:, j, :], start=True, stop=False)
                        mm(dbank[1][:, 0:128], nwt[:, j, :], state[:, :], start=False, stop=True).then_inc(vn_done, 1)
                        mm(dbank[3][:, c128[j]], state[:, :], qdec[:, j, :], start=True, stop=False)
                        yield
                        pe.wait_ge(vn_ready, NJ * h + j + 1)
                        if j < NJ - 1:
                            mm(dbank[2][:, 0:128], kdec[:, j, :], vnew[:, :], start=True, stop=True).then_inc(ds_done, 1)
                        ins = mm(dbank[3][:, c128[j]], vnew[:, :], xt[:, j, :], start=False, stop=True)
                        if j == NJ - 1:
                            ins.then_inc(o_done, 1)
                        yield
                    yield
                    pe.wait_ge(o_squared, h + 1)
                    mm(dbank[0][:, :], ones, flat(dg), start=True, stop=True).then_inc(o_sums, 1)
                    yield

            delta = delta_steps()
            for n, (kind, m) in enumerate(BLOCKS):
                x_h, x_l = {"sc": (yb_hi, yb_lo), "dn": (og_hi, og_lo), "wo": (yb_hi, yb_lo), "gate": (og_hi, og_lo),
                            "up": (og_hi, og_lo)}.get(kind, (x_hi, x_lo))
                pe.wait_ge(wlo_ready, n + 1)
                if n >= 2:
                    wait_result_read(pe, *BLOCKS[n - 2])
                if kind == "sc":
                    pe.wait_ge(yblo_ready, KT)
                if kind == "dn":
                    pe.wait_ge(oglo_ready, KT)
                if kind == "wo":
                    pe.wait_ge(yblo_ready, 2 * KT)
                if kind in WIDE:
                    parts = [slice(0, HALF), slice(HALF, L)]
                    outs = [big[n % 2][s][:, 0:HALF] for s in range(2)]
                else:
                    off = META if x_h is x_hi else 0
                    parts = [slice(off, off + T)]
                    outs = [big[n % 2][0][:, :]]
                for k in range(KT):
                    if n == 0:
                        pe.wait_ge(xlo_ready, k + 1)
                    if kind == "gate" and m == 0:
                        pe.wait_ge(hnlo_ready, k + 1)
                    ins = products(outs, n, k, [x_h[:, k, s] for s in parts], [x_l[:, k, s] for s in parts], k == 0, k == KT - 1)
                    if k == KT - 1:
                        ins.then_inc(block_done, 1)
                    if k % 2 and n >= DELTA_FROM:
                        next(delta, None)
                if n == 0:
                    token_projections()
                if n == 1:
                    token_sums()
                if kind == "gate" and m == 0:
                    pe.wait_ge(sqa_ready, KT)
                    mm(dbank[0][:, :], ones, sqa[:, :], start=True, stop=True).then_inc(h_sums, 1)
            for d in range(DOWN):
                n = MAIN + d
                pe.wait_ge(wlo_ready, n + 1)
                for i in range(8):
                    m, k = divmod(8 * d + i, FT)
                    if k == 0:
                        if m < 2:
                            wait_result_read(pe, *BLOCKS[MAIN + m - 2])
                        else:
                            pe.wait_ge(h2_ready, m - 1)
                    if m == 0:
                        pe.wait_ge(flo_ready, k + 1)
                    ins = products([big[m % 2][0][:, :]], n, k, [f_hi[:, k, :]], [f_lo[:, k, :]], k == 0, k == FT - 1, i)
                    if i == 7:
                        ins.then_inc(block_done, 1)
                    elif k == FT - 1:
                        ins.then_inc(down_done, 1)
            pe.wait_ge(sqf_ready, KT)
            mm(dbank[0][:, :], ones, sqa[:, :], start=True, stop=True).then_inc(last_sums, 1)


def kernel(x, meta_tokens, norm1, w_in, conv_qkv, a_log, dt_bias, o_norm, w_dn_out, conv_sc, w_sc_out, w_o, norm2,
           w_gate_up, w_down, final_norm):
    import numpy as np
    import concourse.bacc as bacc
    from concourse.bass_utils import run_bass_kernel_spmd

    def tiles(w):
        w = np.asarray(w)
        return w.reshape(w.shape[0] // 128, 128, w.shape[1] // 128, 128).transpose(2, 1, 0, 3).reshape(
            w.shape[1] // 128, 128, w.shape[0])

    def vector(v):
        return np.asarray(v).reshape(-1, 128).T

    win = np.asarray(w_in[0])
    names = ("q", "k", "v", "z", "ba", "c", "u", "b", "ga", "gb")
    widths = [D] * 4 + [2 * HEADS] + [D] * 5
    start = dict(zip(names, np.cumsum([0] + widths[:-1])))
    mats = {k: tiles(win[:, start[k]:start[k] + D]) for k in names if k != "ba"}
    gu = np.asarray(w_gate_up[0])
    mats |= {"sc": tiles(w_sc_out[0]), "dn": tiles(w_dn_out[0]), "wo": tiles(w_o[0]),
             "gate": tiles(gu[:, :FF]), "up": tiles(gu[:, FF:])}
    down = tiles(w_down[0]).reshape(KT, 128, FT, 128).transpose(0, 2, 1, 3).reshape(DOWN, 8, 128, 128)
    down = down.transpose(0, 2, 1, 3).reshape(DOWN, 128, 1024)
    w_stream = np.concatenate([np.stack([mats[k][m] for k, m in BLOCKS]), down])
    w_ba = win[:, start["ba"]:start["ba"] + 16].reshape(KT, 128, 16).transpose(1, 0, 2).reshape(128, KT * 16)
    h_t = np.concatenate([np.asarray(meta_tokens), np.asarray(x[0])]).T.reshape(KT, 128, L).transpose(1, 0, 2)
    cq = np.asarray(conv_qkv[0]).T.reshape(24, 128, 4).transpose(1, 0, 2).reshape(128, 96)
    cs = np.asarray(conv_sc[0]).T.reshape(8, 128, 3).transpose(1, 0, 2).reshape(128, 24)
    small = np.concatenate([vector(norm1[0]), vector(norm2[0]), vector(final_norm), cq, cs, vector(o_norm[0]),
                            np.broadcast_to(np.asarray(a_log[0]), (128, HEADS)),
                            np.broadcast_to(np.asarray(dt_bias[0]), (128, HEADS))], axis=1)
    r = np.arange(128)
    row, col = r[:, None], r[None, :]
    consts = [row == col, (row == col) | True, row <= col, row > col]
    for b in [1] + LEVELS:
        consts.append((row // (2 * b) == col // (2 * b)) & (row // b % 2 == 1) & (col // b % 2 == 0))
    consts = np.stack(consts, axis=1).astype(np.float32)

    arrays = {"h_t": h_t, "w_stream": w_stream, "w_ba": w_ba, "small": small, "consts": consts}
    arrays = {k: np.ascontiguousarray(a) for k, a in arrays.items()}
    nc = bacc.Bacc("TRN2", target_bir_lowering=False, num_devices=1)
    args = [nc.dram_tensor(k, a.shape, mybir.dt.from_np(a.dtype), kind="ExternalInput").ap() for k, a in arrays.items()]
    out = nc.dram_tensor("out", (128, KT, T), mybir.dt.float32, kind="ExternalOutput").ap()
    hybrid_block_kernel(nc, *args, out)
    y = run_bass_kernel_spmd(nc, [arrays], core_ids=[0]).results[0]["out"]
    return np.ascontiguousarray(y.transpose(2, 1, 0).reshape(1, T, D))
```

```python
from contextlib import ExitStack

import concourse.bass as bass
from concourse import mybir

D = 1024
T = 512
META = 16
L = META + T
HALF = L // 2
HEADS = 8
FF = 2816
KT = D // 128
FT = FF // 128
NJ = T // 128
EPS = 1e-6
LEVELS = [2, 4, 8, 16, 32, 64]
META_LEVELS = 3
WARM = 36
MASKED = LEVELS.index(32)

BLOCKS = [(kind, h) for h in range(HEADS) for kind in ("q", "k", "v", "z", "c", "u", "b")]
BLOCKS += [(kind, m) for m in range(KT) for kind in ("gb", "sc")]
BLOCKS += [("ga", 0)] + [x for m in range(KT - 1) for x in (("ga", m + 1), ("dn", m))] + [("dn", KT - 1)]
BLOCKS += [("wo", m) for m in range(KT)]
BLOCKS += [(kind, m) for m in range(FT) for kind in ("gate", "up")]
MAIN = len(BLOCKS)
DOWN = FT * KT // 8
STREAM = MAIN + DOWN
AT = {b: n for n, b in enumerate(BLOCKS)}
WIDE = ("q", "k", "v", "c", "u")
CONV = ("q", "k", "v", "u")
STEPS = 28
PRE = 20
DELTA_FROM = 4
NORM1, NORM2, NORMF = 0, 8, 16
CQKV = 24
CSC = CQKV + 24 * 4
ONORM = CSC + 8 * 3
ALOG = ONORM + 1
DTB = ALOG + 8
NSMALL = DTB + 8
CI, CTRI, CREV, CLEV = 0, 1, 2, 3
NCONST = CLEV + 1 + len(LEVELS)


EXP_LN_FROM = [AT["c", h] for h in range(HEADS)] + [AT["wo", 0], MAIN + 1]
GATES = [b for b in BLOCKS if b[0] in ("gb", "ga")]
DOWN_ENDS = {MAIN + (FT * m + FT - 1) // 8 + 1: m for m in range(KT)}


def conv_number(kind, h):
    return 4 * h + CONV.index(kind)


def level_blocks(b):
    return [(slice(2 * b * i, 2 * b * i + b), slice(2 * b * i + b, 2 * b * i + 2 * b), slice(b * i, b * i + b))
            for i in range(64 // b)]


def gate_number(kind, m):
    return GATES.index((kind, m))


def hybrid_block_kernel(nc, h_t, w_stream, w_ba, small, consts, out):
    f32 = mybir.dt.float32
    f32r = mybir.dt.float32r
    ALU = mybir.AluOpType
    ACT = mybir.ActivationFunctionType

    ctx = ExitStack()
    with ctx:
        def sem(name):
            return ctx.enter_context(nc.semaphore(name))

        def sb(name, shape, dt=f32, where=ctx):
            return where.enter_context(nc.sbuf_tensor(name, shape, dt))

        bank = [ctx.enter_context(nc.psum_tensor(f"bank{i}", [128, 512], f32)) for i in range(8)]
        big = [bank[0:2], bank[2:4]]
        dbank = bank[4:8]

        cst = sb("cst", [128, NCONST, 128])
        ident, tri, rev = (cst[:, c, :] for c in (CI, CTRI, CREV))
        ones_mem = sb("ones_mem", [128, 128])
        ones = ones_mem[:, :]
        sm = sb("sm", [128, NSMALL])
        w_raw = sb("w_raw", [128, 3, 1024])
        w_hi = sb("w_hi", [128, 2, 1024], f32r)
        w_lo = sb("w_lo", [128, 2, 1024], f32r)
        eps = sb("eps", [128, 2])
        og_hi = sb("og_hi", [128, KT, T], f32r)
        og_lo = sb("og_lo", [128, KT, T], f32r)

        mix_mem = ExitStack()
        x_hi = sb("x_hi", [128, KT, L], f32r, mix_mem)
        x_lo = sb("x_lo", [128, KT, L], f32r, mix_mem)
        yb_hi = sb("yb_hi", [128, KT, T], f32r, mix_mem)
        yb_lo = sb("yb_lo", [128, KT, T], f32r, mix_mem)
        h_in = sb("h_in", [128, KT, L], f32, mix_mem)
        raw = sb("raw", [128, 2, 3 + L], f32, mix_mem)
        cv = sb("cv", [128, 2, L], f32, mix_mem)
        cbuf = sb("cbuf", [128, L], f32, mix_mem)
        ybf = cbuf[:, 0:T]
        egate = sb("egate", [128, 2, T], f32, mix_mem)
        eg = egate[:, 1, :].rearrange("p (j c) -> p j c", c=128)
        qkv = sb("qkv", [128, 3, L], f32, mix_mem)
        zs = sb("zs", [128, 2, T], f32, mix_mem)
        tile4 = [128, NJ, 128]
        xt = sb("xt", [128, 2, NJ, 128], f32, mix_mem)
        xd = sb("xd", tile4, f32, mix_mem)
        am = sb("am", tile4, f32, mix_mem)
        alev = sb("alev", [128, MASKED, NJ, 128], f32, mix_mem)
        tm = sb("tm", tile4, f32, mix_mem)
        um = sb("um", tile4, f32, mix_mem)
        pb = h_in[:, KT - 4:KT, :].rearrange("p k l -> p (k l)")[:, 0:MASKED * T].rearrange(
            "p (l j c) -> p l j c", l=MASKED, c=128)
        kbe = sb("kbe", tile4, f32, mix_mem)
        kdec = sb("kdec", tile4, f32, mix_mem)
        dg = kdec
        vb = sb("vb", tile4, f32, mix_mem)
        qdec = sb("qdec", tile4, f32, mix_mem)
        nwt = sb("nwt", tile4, f32, mix_mem)
        osq = nwt
        pbx = nwt
        sqm = sb("sqm", [128, META], f32, mix_mem)
        vnew = sb("vnew", [128, 128], f32, mix_mem)
        state = sb("state", [128, 128], f32, mix_mem)
        g = sb("g", [128, NJ + 1, HEADS], f32, mix_mem)
        ga1 = sb("ga1", [128, NJ + 1, HEADS], f32, mix_mem)
        ga2 = sb("ga2", [128, NJ + 1, HEADS], f32, mix_mem)
        beta = sb("beta", [128, NJ + 1, HEADS], f32, mix_mem)
        gc = sb("gc", [128, NJ + 1, HEADS], f32, mix_mem)
        erev = sb("erev", [128, NJ + 1, HEADS], f32, mix_mem)
        etot = sb("etot", [128, NJ, HEADS], f32, mix_mem)
        be = sb("be", [128, NJ, HEADS], f32, mix_mem)
        nea = sb("nea", [128, HEADS], f32, mix_mem)
        on_scaled = sb("on_scaled", [128, 1], f32, mix_mem)
        wba = sb("wba", [128, KT * 16], f32, mix_mem)
        wba_hi = sb("wba_hi", [128, KT, 16], f32r, mix_mem)
        wba_lo = sb("wba_lo", [128, KT, 16], f32r, mix_mem)
        mdg = sb("mdg", [META, META], f32, mix_mem)
        mx = sb("mx", [META, META], f32, mix_mem)
        ma = sb("ma", [META, META], f32, mix_mem)
        malev = sb("malev", [META, META_LEVELS, META], f32, mix_mem)
        mt = sb("mt", [META, META], f32, mix_mem)
        mu = sb("mu", [META, META], f32, mix_mem)
        mpb = sb("mpb", [META, META_LEVELS, META], f32, mix_mem)
        mkdec = sb("mkdec", [META, 128], f32, mix_mem)
        mvb = sb("mvb", [META, 128], f32, mix_mem)
        mvnew = wba[0:META, :]
        sums1 = qkv[:, 2, :]
        xnf = [cv[:, 0, :], cv[:, 1, :], qkv[:, 0, :], qkv[:, 1, :]]
        rs1 = cbuf
        bat = xt[0:16, :, :, :].rearrange("p a j c -> p (a j c)")[:, 0:L]
        mixb = h_in
        mix_mem.close()

        ffn_mem = ctx.enter_context(ExitStack())
        f_hi = sb("f_hi", [128, FT, T], f32r, ffn_mem)
        f_lo = sb("f_lo", [128, FT, T], f32r, ffn_mem)
        f_pad = sb("f_pad", [128, 3 * T], f32, ffn_mem)
        sqa = sb("sqa", [128, T], f32, ffn_mem)
        sqt = sb("sqt", [128, 2, T], f32, ffn_mem)
        rs2 = sb("rs2", [128, T], f32, ffn_mem)
        tg = sb("tg", [128, T], f32, ffn_mem)
        sg = sb("sg", [128, T], f32, ffn_mem)
        ff = sb("ff", [128, T], f32, ffn_mem)
        h1 = sb("h1", [128, KT, T], f32, ffn_mem)
        del f_pad

        const_in, small_in, ba_in = sem("const_in"), sem("small_in"), sem("ba_in")
        h_loaded = [sem(f"h_loaded{k}") for k in range(4)]
        h_again = sem("h_again")
        w_in = [sem(f"w_in{i}") for i in range(3)]
        stored = sem("stored")
        xlo_even, q_squared, k_squared, km_sums, km_copied, k_sums, q_sums, mt_ready, u_updated, t_updated, mdiag_ready, mt_turned, mu_ready, yblo_last, x_added = (
            sem(n) for n in ("xlo_even", "q_squared", "k_squared", "km_sums", "km_copied", "k_sums", "q_sums", "mt_ready",
                             "u_updated", "t_updated", "mdiag_ready", "mt_turned", "mu_ready", "yblo_last", "x_added"))
        rs1_ready, k_root, q_root, o_root = (sem(n) for n in ("rs1_ready", "k_root", "q_root", "o_root"))
        zs_ready, down_done, mixb_ready, dn_gated = (sem(n) for n in ("zs_ready", "down_done", "mixb_ready", "dn_gated"))
        act_chain, dve_chain, pool_chain = sem("act_chain"), sem("dve_chain"), sem("pool_chain")
        whi_ready, wlo_ready = sem("whi_ready"), sem("wlo_ready")
        block_done = sem("block_done")
        x_squared, x_sums, xn_ready, xhi_ready, xlo_ready = (
            sem(n) for n in ("x_squared", "x_sums", "xn_ready", "xhi_ready", "xlo_ready"))
        zeroed, tm_set, ones_ready, bat_done, bat_copied = (sem(n) for n in ("zeroed", "tm_set", "ones_ready", "bat_done", "bat_copied"))
        wba_hi_ready, wba_ready, ba_done, eb_ready, az_ready, ln_ready, g_ready, cums_done, exps_ready, tokens_ready = (
            sem(n) for n in ("wba_hi_ready", "wba_ready", "ba_done", "eb_ready", "az_ready", "ln_ready", "g_ready",
                             "cums_done", "exps_ready", "tokens_ready"))
        raw_ready, tap_done, conv_ready, qkv_ready = (
            sem(n) for n in ("raw_ready", "tap_done", "conv_ready", "qkv_ready"))
        ge_ready, c_ready, c_used = sem("ge_ready"), sem("c_ready"), sem("c_used")
        yb_ready, ybhi_ready, yblo_ready = sem("yb_ready"), sem("ybhi_ready"), sem("yblo_ready")
        qk_squared, v_turned, diag_ready, vb_ready, qk_sums, gc_spread = (
            sem(n) for n in ("qk_squared", "v_turned", "diag_ready", "vb_ready", "qk_sums", "gc_spread"))
        q_ready, k_ready, egc_ready, dif_ready, xd_ready = (
            sem(n) for n in ("q_ready", "k_ready", "egc_ready", "dif_ready", "xd_ready"))
        k_turned, kk_done, mpre_done, mdif_ready, mx_ready, ma_ready, mkv_ready = (
            sem(n) for n in ("k_turned", "kk_done", "mpre_done", "mdif_ready", "mx_ready", "ma_ready", "mkv_ready"))
        kd_ready, xt_ready, xb_ready, a_ready, t_ready, alev_ready = (
            sem(n) for n in ("kd_ready", "xt_ready", "xb_ready", "a_ready", "t_ready", "alev_ready"))
        qk_done, qkt_ready, qdec_ready, u_turned, u_ready = (
            sem(n) for n in ("qk_done", "qkt_ready", "qdec_ready", "u_turned", "u_ready"))
        p_done, pb_cleared, pb_ready, du_done, ut_ready = (
            sem(n) for n in ("p_done", "pb_cleared", "pb_ready", "du_done", "ut_ready"))
        mv_done, mv_ready, ms_done, w_done, nwt_ready = (
            sem(n) for n in ("mv_done", "mv_ready", "ms_done", "w_done", "nwt_ready"))
        vn_done, vn_ready, ds_done, state_ready, o_done = (
            sem(n) for n in ("vn_done", "vn_ready", "ds_done", "state_ready", "o_done"))
        o_squared, o_sums, on_ready, ogf_ready, oghi_ready, oglo_ready = (
            sem(n) for n in ("o_squared", "o_sums", "on_ready", "ogf_ready", "oghi_ready", "oglo_ready"))
        h1_ready, hnhi_ready, hnlo_ready, sqt_ready, sqa_ready, h_sums, rs2_ready = (
            sem(n) for n in ("h1_ready", "hnhi_ready", "hnlo_ready", "sqt_ready", "sqa_ready", "h_sums", "rs2_ready"))
        tg_ready, sg_ready, sg2_ready, f_ready, fhi_ready, flo_ready = (
            sem(n) for n in ("tg_ready", "sg_ready", "sg2_ready", "f_ready", "fhi_ready", "flo_ready"))
        h2_ready, h2_squared, sqf_ready, last_sums, y_ready = (
            sem(n) for n in ("h2_ready", "h2_squared", "sqf_ready", "last_sums", "y_ready"))

        def cols(ap, b, which):
            return ap.rearrange("p (g two b) -> p g two b", two=2, b=b)[:, :, which, :]

        def compact(t):
            return t[:, 0:256].rearrange("p (j c) -> p j c", c=64)

        def cols4(t, b, which):
            return t.rearrange("p j (g two b) -> p j g two b", two=2, b=b)[:, :, :, which, :]

        def const_cols(m, b, which):
            return cols(m, b, which).unsqueeze(1).broadcast_to([128, NJ, 64 // b, b])

        def flat(t):
            return t[:, :, :].rearrange("p j c -> p (j c)")

        def per_chunk(t, h, first=0, n=NJ):
            return t[:, first:first + n, h].unsqueeze(2).broadcast_to([128, n, 128])

        def all_chunks(m):
            return m.unsqueeze(1).broadcast_to([128, NJ, 128])

        def wait_result_read(engine, kind, m):
            if kind in ("q", "k", "v"):
                engine.wait_ge(raw_ready, 3 * m + ("q", "k", "v").index(kind) + 1)
            elif kind in ("gb", "ga"):
                engine.wait_ge(ge_ready, gate_number(kind, m) + 1)
            else:
                engine.wait_ge({"z": zs_ready, "c": c_ready, "u": c_used, "b": yb_ready, "sc": mixb_ready, "dn": dn_gated,
                                "wo": h1_ready, "gate": tg_ready, "up": f_ready}[kind], m + 1)

        def wait_gate_used(engine, i):
            kind, m = GATES[i]
            engine.wait_ge({"gb": mixb_ready, "ga": dn_gated}[kind], m + 1)

        block = ctx.enter_context(nc.Block())

        @block.sync
        def _(sp):
            for part in range(4):
                sp.dma_start(h_in[:, 2 * part:2 * part + 2, :], h_t[:, 2 * part:2 * part + 2, :]).then_inc(h_loaded[part], 16)
            sp.dma_start(sm[:, :], small[:, :]).then_inc(small_in, 16)
            for n in range(STREAM):
                if n == 2:
                    sp.dma_start(wba[:, :], w_ba[:, :]).then_inc(ba_in, 16)
                    sp.dma_start(cst[:, :, :], consts[:, :, :]).then_inc(const_in, 16)
                if n >= 3:
                    sp.wait_ge(wlo_ready, 2 * (n - 2))
                sp.dma_start(w_raw[:, n % 3, :], w_stream[n, :, :]).then_inc(w_in[n % 3], 16)
            for m in range(KT):
                sp.wait_ge(y_ready, m + 1)
                sp.dma_start(out[:, m, :], h1[:, m, :]).then_inc(stored, 16)
            sp.wait_ge(stored, 16 * KT)


        @block.gpsimd
        def _(pool):
            chain = [0]

            def link(ins):
                chain[0] += 1
                ins.then_inc(pool_chain, 1)
                pool.wait_ge(pool_chain, chain[0])

            def mult(to, a, b):
                return nc.gpsimd.tensor_tensor(to, a, b, ALU.mult)

            nc.gpsimd.memset(ones, 1.0).then_inc(ones_ready, 1)
            nc.gpsimd.memset(raw[:, :, 0:3], 0.0)
            nc.gpsimd.memset(eps[:, 0:1], EPS)
            nc.gpsimd.memset(eps[:, 1:2], 128 * EPS)
            nc.gpsimd.memset(mpb[:, :, :], 0.0)
            nc.gpsimd.memset(alev[:, :, :, :].rearrange("p l j c -> p (l j c)"), 0.0).then_inc(zeroed, 1)

            def split_weights(n, half):
                at = slice(512 * half, 512 * half + 512)
                pool.wait_ge(whi_ready, 2 * n + half + 1)
                if n >= 2:
                    pool.wait_ge(block_done, n - 1)
                nc.gpsimd.tensor_tensor(w_lo[:, n % 2, at], w_raw[:, n % 3, at], w_hi[:, n % 2, at].bitcast(f32),
                                        ALU.subtract).then_inc(wlo_ready, 1)

            split_weights(0, 0)
            split_weights(0, 1)
            for k in range(1, KT, 2):
                pool.wait_ge(xhi_ready, k + 1)
                nc.gpsimd.tensor_tensor(x_lo[:, k, :], xnf[k % 4], x_hi[:, k, :].bitcast(f32),
                                        ALU.subtract).then_inc(xlo_ready, 1)
            nc.gpsimd.memset(pb.rearrange("p l j c -> p (l j c)"), 0.0).then_inc(pb_cleared, 1)

            def level_mask(l):
                b = LEVELS[l]
                mult(cols4(alev[:, l, :, :], b, 0), cols4(am[:, :, :], b, 0),
                     const_cols(cst[:, CLEV + 1 + l, :], b, 0)).then_inc(alev_ready, 1)

            def delta_steps():
                for h in range(-1, HEADS):
                    for step in range(0 if h >= 0 else PRE, STEPS):
                        if step == 0:
                            pool.wait_ge(a_ready, h + 1)
                            level_mask(0)
                        if step == 1:
                            pool.wait_ge(ma_ready, h + 1)
                            link(mult(mt[:, :], ma[:, :], cst[0:META, CLEV, 0:META]))
                            nc.gpsimd.tensor_tensor(mt[:, :], ident[0:META, 0:META], mt[:, :], ALU.subtract)
                            for l in range(META_LEVELS):
                                ins = mult(malev[:, l, :], ma[:, :], cst[0:META, CLEV + 1 + l, 0:META])
                            ins.then_inc(mt_ready, 1)
                        if step == 2:
                            level_mask(1)
                        if step == 3:
                            level_mask(2)
                            pool.wait_ge(q_ready, h + 1)
                            pool.wait_ge(egc_ready, h + 1)
                            mult(flat(qdec), flat(eg), qkv[:, 0, META:L]).then_inc(qdec_ready, 1)
                        if step == 4:
                            level_mask(3)
                        if step == 20 and h + 1 < HEADS:
                            if h < 0:
                                pool.wait_ge(tokens_ready, 1)
                            else:
                                pool.wait_ge(km_sums, h + 1)
                            nc.gpsimd.tensor_tensor(mdg[:, :], ident[0:META, 0:META],
                                                    gc[0:META, 0, h + 1:h + 2].broadcast_to([META, META]),
                                                    ALU.mult).then_inc(mdiag_ready, 1)
                        if step == 22 and h + 1 < HEADS:
                            if h >= 0:
                                pool.wait_ge(ds_done, (NJ - 1) * (h + 1))
                            nc.gpsimd.tensor_tensor(dg[:, :, :], all_chunks(ident), per_chunk(gc, h + 1, 1),
                                                    ALU.mult).then_inc(diag_ready, 1)
                        if step == 27 and h >= 0:
                            pool.wait_ge(oghi_ready, h + 1)
                            nc.gpsimd.tensor_tensor(og_lo[:, h, :], flat(xd), og_hi[:, h, :].bitcast(f32),
                                                    ALU.subtract).then_inc(oglo_ready, 1)
                        yield

            def evacuate(n, kind, m):
                if kind == "b" or kind == "dn" and m < KT - 1:
                    pool.wait_ge(ybhi_ready, (0 if kind == "b" else KT) + m + 1)
                    nc.gpsimd.tensor_tensor(yb_lo[:, m, :], ybf, yb_hi[:, m, :].bitcast(f32), ALU.subtract).then_inc(yblo_ready, 1)
                if kind == "wo":
                    pool.wait_ge(sqt_ready, m + 1)
                    if m == 0:
                        nc.gpsimd.tensor_copy(sqa[:, :], sqt[:, 0, :]).then_inc(sqa_ready, 1)
                    else:
                        pool.wait_ge(sqa_ready, m)
                        nc.gpsimd.tensor_tensor(sqa[:, :], sqa[:, :], sqt[:, m % 2, :], ALU.add).then_inc(sqa_ready, 1)
                if kind == "up":
                    pool.wait_ge(fhi_ready, m + 1)
                    nc.gpsimd.tensor_tensor(f_lo[:, m, :], ff[:, :], f_hi[:, m, :].bitcast(f32), ALU.subtract).then_inc(flo_ready, 1)

            delta = delta_steps()
            for n in range(STREAM + 1):
                for q in range(4):
                    if n >= DELTA_FROM:
                        next(delta, None)
                    if q in (1, 2) and n + 1 < STREAM:
                        split_weights(n + 1, q - 1)
                    if q == 3 and 1 <= n <= MAIN:
                        evacuate(n - 1, *BLOCKS[n - 1])
                if n not in DOWN_ENDS or DOWN_ENDS[n] == KT - 1:
                    continue
                m = DOWN_ENDS[n]
                pool.wait_ge(h2_squared, m + 1)
                if m == 0:
                    nc.gpsimd.tensor_copy(sqa[:, :], sqt[:, 0, :]).then_inc(sqf_ready, 1)
                else:
                    pool.wait_ge(sqf_ready, m)
                    nc.gpsimd.tensor_tensor(sqa[:, :], sqa[:, :], sqt[:, m % 2, :], ALU.add).then_inc(sqf_ready, 1)

        @block.scalar
        def _(act):
            chain = [0]

            def link(ins):
                chain[0] += 1
                ins.then_inc(act_chain, 1)
                act.wait_ge(act_chain, chain[0])

            def copy(to, x):
                return nc.scalar.activation(to, x, ACT.Copy)

            def inverse_root(to, sums, scale, eps_column):
                link(nc.scalar.activation(to, sums, ACT.Ln, scale=scale, bias=eps[:, eps_column:eps_column + 1]))
                return nc.scalar.activation(to, to, ACT.Exp, scale=-0.5)

            nc.scalar.preload_act_table_set("natural_log_exp_and_others")
            for k in range(KT):
                act.wait_ge(h_loaded[k // 2], 16)
                if k >= 4:
                    act.wait_ge(x_added, max(1, k - 4))
                nc.scalar.activation(xnf[k % 4], h_in[:, k, :], ACT.Square).then_inc(x_squared, 1)

            def split_weights(n, half):
                at = slice(512 * half, 512 * half + 512)
                act.wait_ge(w_in[n % 3], 16 * (n // 3 + 1))
                if n >= 2:
                    act.wait_ge(block_done, n - 1)
                copy(w_hi[:, n % 2, at], w_raw[:, n % 3, at]).then_inc(whi_ready, 1)

            split_weights(0, 0)
            split_weights(0, 1)
            act.wait_ge(x_sums, 1)
            act.wait_ge(zeroed, 1)
            halves = [slice(0, HALF), slice(HALF, L)]
            for s in range(2):
                nc.scalar.activation(rs1[:, halves[s]], big[0][s][:, 0:HALF], ACT.Ln, scale=1.0 / D,
                                     bias=eps[:, 0:1]).then_inc(act_chain, 1)
            for s in range(2):
                chain[0] += 1
                act.wait_ge(act_chain, chain[0])
                ins = nc.scalar.activation(rs1[:, halves[s]], rs1[:, halves[s]], ACT.Exp, scale=-0.5)
            ins.then_inc(rs1_ready, 1)
            for k in range(KT):
                act.wait_ge(xn_ready, k + 1)
                copy(x_hi[:, k, :], xnf[k % 4]).then_inc(xhi_ready, 1)
            act.wait_ge(ba_in, 16)
            copy(wba_hi[:, :, :].rearrange("p k c -> p (k c)"), wba[:, :]).then_inc(wba_hi_ready, 1)

            def token_factors():
                act.wait_ge(ba_done, 1)
                ba = dbank[2][:, 0:16 * (NJ + 1)].rearrange("p (j c) -> p j c", c=16)
                nc.scalar.activation(beta[:, :, :], ba[:, :, 0:HEADS], ACT.Exp, scale=-1.0).then_inc(eb_ready, 1)
                act.wait_ge(small_in, 16)
                nc.scalar.activation(nea[:, :], sm[:, ALOG:ALOG + HEADS], ACT.Exp).then_inc(eb_ready, 1)
                act.wait_ge(az_ready, 1)
                link(nc.scalar.activation(ga2[:, :, :], ga1[:, :, :], ACT.Abs))
                link(nc.scalar.activation(ga2[:, :, :], ga2[:, :, :], ACT.Exp, scale=-1.0))
                nc.scalar.activation(ga2[:, :, :], ga2[:, :, :], ACT.Ln, bias=1.0).then_inc(ln_ready, 1)

            def token_decays():
                act.wait_ge(cums_done, 1)
                cums = dbank[1]
                nc.scalar.activation(be[:, :, :], cums[:, 0:32].rearrange("p (j c) -> p j c", c=HEADS), ACT.Exp)
                nc.scalar.activation(erev[:, 1:, :], cums[:, 32:64].rearrange("p (j c) -> p j c", c=HEADS), ACT.Exp)
                nc.scalar.activation(etot[:, :, :], cums[:, 64:96].rearrange("p (j c) -> p j c", c=HEADS), ACT.Exp)
                nc.scalar.activation(gc[:, 1:, :], cums[:, 0:32].rearrange("p (j c) -> p j c", c=HEADS), ACT.Copy)
                nc.scalar.activation(gc[0:META, 0, :], cums[0:META, 96:104], ACT.Copy)
                nc.scalar.activation(erev[0:META, 0, :], cums[0:META, 104:112], ACT.Exp).then_inc(exps_ready, 1)

            def delta_steps():
                for h in range(-1, HEADS):
                    nxt = h + 1
                    for step in range(0 if h >= 0 else PRE, STEPS):
                        if step == 1:
                            act.wait_ge(k_turned, h + 1)
                            for to, factor, first in ((kbe, be, 0), (kdec, erev, 1)):
                                for j in range(NJ):
                                    ins = nc.scalar.activation(to[:, j, :], dbank[0][:, 128 * j:128 * (j + 1)], ACT.Copy,
                                                               scale=factor[:, first + j, h:h + 1])
                            ins.then_inc(kd_ready, 1)
                        if step == 2:
                            act.wait_ge(u_turned, h + 1)
                            copy(flat(um), dbank[1][:, :]).then_inc(u_ready, 1)
                        if step == 4:
                            act.wait_ge(mt_turned, h + 1)
                            copy(mu[:, :], dbank[0][0:META, 0:META]).then_inc(mu_ready, 1)
                        if 3 <= step <= 13 and step % 2:
                            l = (step - 3) // 2
                            b = LEVELS[l]
                            act.wait_ge(p_done, len(LEVELS) * h + l + 1)
                            if 1 <= l <= META_LEVELS:
                                copy(cols(mpb[:, l - 1, :], LEVELS[l - 1], 1), dbank[1][0:META, 256:264])
                            if l < MASKED:
                                act.wait_ge(pb_cleared, 1)
                                ins = copy(cols(pb[:, l, :, :].rearrange("p j c -> p (j c)"), b, 1),
                                           dbank[1][:, 0:256].rearrange("p (g b) -> p g b", b=b))
                            else:
                                for rows, second, at in level_blocks(b):
                                    ins = copy(pbx[rows, :, second], compact(dbank[1])[rows, :, at])
                            ins.then_inc(pb_ready, 1)
                        if step == 4 + 2 * (META_LEVELS + 1):
                            act.wait_ge(mv_done, h + 1)
                            copy(mvnew, dbank[1][0:META, 256:384]).then_inc(mv_ready, 1)
                        if step == 15:
                            act.wait_ge(w_done, h + 1)
                            nc.scalar.activation(flat(nwt), dbank[0][:, :], ACT.Copy, scale=-1.0).then_inc(nwt_ready, 1)
                        if step == 22 and nxt < HEADS:
                            act.wait_ge(km_sums, nxt + 1)
                            copy(mx[:, :], dbank[1][0:META, 272:288])
                            copy(sqm[:, :], dbank[1][:, 256:256 + META]).then_inc(km_copied, 1)
                        if 16 <= step <= 22 and step % 2 == 0 and h >= 0:
                            act.wait_ge(vn_done, NJ * h + (step - 16) // 2 + 1)
                            copy(vnew[:, :], dbank[1][:, 0:128]).then_inc(vn_ready, 1)
                        if nxt < HEADS:
                            if step == 20:
                                if h < 0:
                                    act.wait_ge(const_in, 16)
                                copy(cols4(tm[:, :, :], 1, 1), const_cols(ident, 1, 1)).then_inc(tm_set, 1)
                                act.wait_ge(qkv_ready, 3 * nxt + 1)
                                nc.scalar.activation(flat(xd), qkv[:, 0, META:L], ACT.Square).then_inc(q_squared, 1)
                            if step == 21:
                                act.wait_ge(qkv_ready, 3 * nxt + 2)
                                nc.scalar.activation(sqm[:, :], qkv[:, 1, 0:META], ACT.Square)
                                nc.scalar.activation(flat(am), qkv[:, 1, META:L], ACT.Square).then_inc(k_squared, 1)
                            if step == 22:
                                act.wait_ge(q_sums, nxt + 1)
                                inverse_root(flat(xd), dbank[0][:, :], 1.0, 0).then_inc(q_root, 1)
                            if step == 23:
                                act.wait_ge(k_sums, nxt + 1)
                                act.wait_ge(km_copied, nxt + 1)
                                inverse_root(sqm[:, :], sqm[:, :], 1.0, 0)
                                inverse_root(flat(am), dbank[2][:, :], 1.0, 0).then_inc(k_root, 1)
                            if step == 24:
                                act.wait_ge(mdif_ready, nxt + 1)
                                nc.scalar.activation(mx[:, :], mx[:, :], ACT.Exp, scale=-1.0).then_inc(mx_ready, 1)
                            if step == 25:
                                act.wait_ge(dif_ready, nxt + 1)
                                xtn = flat(xt[:, nxt % 2, :, :])
                                nc.scalar.activation(xtn, xtn, ACT.Exp, scale=-1.0).then_inc(xd_ready, 1)
                                nc.scalar.activation(flat(eg), dbank[1][:, :], ACT.Exp).then_inc(egc_ready, 1)
                        if h >= 0:
                            if step == 24:
                                act.wait_ge(o_done, h + 1)
                                nc.scalar.activation(flat(osq), dbank[3][:, :], ACT.Square).then_inc(o_squared, 1)
                            if step == 26:
                                act.wait_ge(o_sums, h + 1)
                                inverse_root(flat(osq), dbank[2][:, :], 1.0, 1).then_inc(o_root, 1)
                            if step == 27:
                                act.wait_ge(ogf_ready, h + 1)
                                copy(og_hi[:, h, :], flat(xd)).then_inc(oghi_ready, 1)
                        yield

            def evacuate(n, kind, m):
                p = big[n % 2]
                act.wait_ge(block_done, n + 1)
                if kind in ("q", "k", "v"):
                    c = conv_number(kind, m)
                    if c >= 2:
                        act.wait_ge(conv_ready, c - 1)
                    else:
                        act.wait_ge(zeroed, 1)
                    copy(raw[:, c % 2, 3:3 + HALF], p[0][:, 0:HALF])
                    copy(raw[:, c % 2, 3 + HALF:3 + L], p[1][:, 0:HALF]).then_inc(raw_ready, 1)
                if kind == "c":
                    if m:
                        act.wait_ge(yblo_ready, m)
                    copy(cbuf[:, 0:HALF], p[0][:, 0:HALF])
                    copy(cbuf[:, HALF:L], p[1][:, 0:HALF]).then_inc(c_ready, 1)
                if kind == "z":
                    if m >= 2:
                        act.wait_ge(oglo_ready, m - 1)
                    nc.scalar.activation(zs[:, m % 2, :], p[0][:, :], ACT.Silu).then_inc(zs_ready, 1)
                if kind in ("gb", "ga"):
                    i = gate_number(kind, m)
                    if i >= 2:
                        wait_gate_used(act, i - 2)
                    else:
                        act.wait_ge(qdec_ready, HEADS)
                    nc.scalar.activation(egate[:, i % 2, :], p[0][:, :], ACT.Sigmoid).then_inc(ge_ready, 1)
                if kind == "gate" and m == 0:
                    act.wait_ge(h_sums, 1)
                    inverse_root(rs2[:, :], dbank[0][:, :], 1.0 / D, 0).then_inc(rs2_ready, 1)
                yield
                if kind in ("b", "dn"):
                    i = m if kind == "b" else KT + m
                    act.wait_ge(yb_ready, i + 1)
                    copy(yb_hi[:, m, :], ybf).then_inc(ybhi_ready, 1)
                if kind == "wo":
                    act.wait_ge(h1_ready, m + 1)
                    nc.scalar.activation(og_hi[:, m, :], h1[:, m, :], ACT.Copy,
                                         scale=sm[:, NORM2 + m:NORM2 + m + 1]).then_inc(hnhi_ready, 1)
                    if m >= 2:
                        act.wait_ge(sqa_ready, m - 1)
                    nc.scalar.activation(sqt[:, m % 2, :], h1[:, m, :], ACT.Square).then_inc(sqt_ready, 1)
                if kind == "gate":
                    act.wait_ge(tg_ready, m + 1)
                    if m:
                        act.wait_ge(f_ready, m)
                    nc.scalar.activation(sg[:, :], tg[:, :], ACT.Silu).then_inc(sg_ready, 1)
                if kind == "up":
                    act.wait_ge(f_ready, m + 1)
                    copy(f_hi[:, m, :], ff[:, :]).then_inc(fhi_ready, 1)

            def silu(kind, h):
                i = ("q", "k", "v").index(kind)
                c = conv_number(kind, h)
                act.wait_ge(conv_ready, c + 1)
                if h:
                    act.wait_ge(qdec_ready, h)
                    act.wait_ge(qk_done, h)
                nc.scalar.activation(qkv[:, i, :], cv[:, c % 2, :], ACT.Silu).then_inc(qkv_ready, 1)

            delta = delta_steps()
            for n in range(STREAM + 1):
                chores = evacuate(n - 1, *BLOCKS[n - 1]) if 1 <= n <= MAIN else iter(())
                for q in range(4):
                    if n >= DELTA_FROM:
                        next(delta, None)
                    next(chores, None)
                    if q in (1, 2) and n + 1 < STREAM:
                        split_weights(n + 1, q - 1)
                    if q == 0 and 2 <= n and n - 2 < MAIN and BLOCKS[n - 2][0] in ("q", "k", "v"):
                        silu(*BLOCKS[n - 2])
                    if q == 0 and n in EXP_LN_FROM:
                        nc.scalar.preload_act_table_set("natural_log_exp_and_others")
                if n == 1:
                    token_factors()
                if n == 2:
                    token_decays()
                if n == AT["gb", 4]:
                    act.wait_ge(oglo_ready, HEADS)
                    act.dma_start(h1[:, :, :], h_t[:, :, META:L]).then_inc(h_again, 16)
                if n in DOWN_ENDS:
                    m = DOWN_ENDS[n]
                    act.wait_ge(h2_ready, m + 1)
                    if m >= 2:
                        act.wait_ge(sqf_ready, m - 1)
                    nc.scalar.activation(sqt[:, m % 2, :], h1[:, m, :], ACT.Square).then_inc(h2_squared, 1)
            act.wait_ge(last_sums, 1)
            inverse_root(rs2[:, :], dbank[0][:, :], 1.0 / D, 0).then_inc(rs2_ready, 1)

        @block.vector
        def _(dve):
            chain = [0]

            def link(ins):
                chain[0] += 1
                ins.then_inc(dve_chain, 1)
                dve.wait_ge(dve_chain, chain[0])

            def mult(to, a, b):
                return nc.vector.tensor_tensor(to, a, b, ALU.mult)

            for k in range(1, KT):
                dve.wait_ge(x_squared, k + 1)
                if k > 1:
                    dve.wait_ge(x_added, k - 1)
                nc.vector.tensor_tensor(sums1, xnf[0] if k == 1 else sums1, xnf[k % 4], ALU.add).then_inc(x_added, 1)
            dve.wait_ge(small_in, 16)
            link(nc.vector.tensor_scalar(on_scaled[:, :], sm[:, ONORM:ONORM + 1], float(128) ** 0.5, None, ALU.mult))
            dve.wait_ge(rs1_ready, 1)
            for k in range(KT + 2):
                if k < KT:
                    if k >= 4:
                        dve.wait_ge(xlo_ready if k % 2 else xlo_even, k // 2 - 1)
                    nc.vector.scalar_tensor_tensor(xnf[k % 4], h_in[:, k, :], sm[:, NORM1 + k:NORM1 + k + 1], rs1[:, :],
                                                   ALU.mult, ALU.mult).then_inc(xn_ready, 1)
                if k >= 2 and k % 2 == 0:
                    dve.wait_ge(xhi_ready, k - 1)
                    nc.vector.tensor_tensor(x_lo[:, k - 2, :], xnf[(k - 2) % 4], x_hi[:, k - 2, :].bitcast(f32),
                                            ALU.subtract).then_inc(xlo_even, 1)
            dve.wait_ge(wba_hi_ready, 1)
            nc.vector.tensor_tensor(wba_lo[:, :, :].rearrange("p k c -> p (k c)"), wba[:, :],
                                    wba_hi[:, :, :].rearrange("p k c -> p (k c)").bitcast(f32), ALU.subtract).then_inc(wba_ready, 1)

            def token_factors():
                dve.wait_ge(ba_done, 1)
                dve.wait_ge(eb_ready, 1)
                ba = dbank[2][:, 0:16 * (NJ + 1)].rearrange("p (j c) -> p j c", c=16)
                dtb = sm[:, DTB:DTB + HEADS].unsqueeze(1).broadcast_to([128, NJ + 1, HEADS])
                nc.vector.tensor_tensor(ga1[:, :, :], ba[:, :, HEADS:16], dtb, ALU.add).then_inc(az_ready, 1)
                dve.wait_ge(eb_ready, 2)
                link(nc.vector.tensor_scalar(beta[:, :, :], beta[:, :, :], 1.0, None, ALU.add))
                link(nc.vector.reciprocal(beta[:, :, :], beta[:, :, :]))
                link(nc.vector.tensor_scalar(nea[:, :], nea[:, :], -1.0, None, ALU.mult))
                dve.wait_ge(ln_ready, 1)
                link(nc.vector.tensor_scalar(ga1[:, :, :], ga1[:, :, :], 0.0, None, ALU.max))
                link(nc.vector.tensor_tensor(ga1[:, :, :], ga1[:, :, :], ga2[:, :, :], ALU.add))
                mult(g[:, :, :], ga1[:, :, :], nea[:, :].unsqueeze(1).broadcast_to([128, NJ + 1, HEADS])).then_inc(g_ready, 1)

            def token_decays():
                dve.wait_ge(exps_ready, 1)
                mult(be[:, :, :], be[:, :, :], beta[:, 1:, :]).then_inc(tokens_ready, 1)

            def delta_steps():
                def chunks(t):
                    return t[:, :].rearrange("p (j c) -> p j c", c=128)

                mbank = dbank[2]
                for h in range(-1, HEADS):
                    nxt = h + 1
                    for step in range(0 if h >= 0 else PRE, STEPS):
                        if step == 0:
                            dve.wait_ge(kk_done, h + 1)
                            dve.wait_ge(xb_ready, h + 1)
                            mult(flat(am), dbank[1][:, :], flat(am)).then_inc(a_ready, 1)
                            dve.wait_ge(a_ready, h + 1)
                            dve.wait_ge(tm_set, h + 1)
                            t = cols4(tm[:, :, :], 1, 0)
                            link(mult(t, cols4(am[:, :, :], 1, 0), const_cols(cst[:, CLEV, :], 1, 0)))
                            nc.vector.tensor_tensor(t, const_cols(ident, 1, 0), t, ALU.subtract).then_inc(t_ready, 1)
                            dve.wait_ge(mpre_done, h + 1)
                            dve.wait_ge(mx_ready, h + 1)
                            nc.vector.scalar_tensor_tensor(ma[:, :], mbank[0:META, 256:272], beta[0:META, 0, h:h + 1], mx[:, :],
                                                           ALU.mult, ALU.mult).then_inc(ma_ready, 1)
                            nc.vector.tensor_scalar(mkdec[:, :], mbank[0:META, 0:128], erev[0:META, 0, h:h + 1], None, ALU.mult)
                            nc.vector.tensor_scalar(mvb[:, :], mbank[0:META, 128:256], beta[0:META, 0, h:h + 1], None,
                                                    ALU.mult).then_inc(mkv_ready, 1)
                        if step == 2:
                            dve.wait_ge(qk_done, h + 1)
                            dve.wait_ge(xt_ready, h + 1)
                            xth = flat(xt[:, h % 2, :, :])
                            mult(xth, dbank[3][:, :], xth).then_inc(qkt_ready, 1)
                        if 4 <= step <= 14 and step % 2 == 0:
                            l = (step - 4) // 2
                            b = LEVELS[l]
                            dve.wait_ge(du_done, len(LEVELS) * h + l + 1)
                            if l == META_LEVELS + 2:
                                nc.vector.tensor_copy(state[:, :], mbank[:, 256:384]).then_inc(state_ready, 1)
                            if 1 <= l <= META_LEVELS:
                                mb = LEVELS[l - 1]
                                u = cols(mu[:, :], mb, 1)
                                nc.vector.tensor_tensor(u, u, mbank[0:META, 256:264].rearrange("p (g b) -> p g b", b=mb), ALU.subtract)
                            if 1 <= l < META_LEVELS:
                                t = cols(mt[:, :], mb, 0)
                                nc.vector.tensor_tensor(t, t, dbank[3][0:META, 256:264].rearrange("p (g b) -> p g b", b=mb), ALU.subtract)
                            if l >= MASKED:
                                for first, second, at in level_blocks(b):
                                    u = um[first, :, second]
                                    ins = nc.vector.tensor_tensor(u, u, compact(mbank)[first, :, at], ALU.subtract)
                                ins.then_inc(u_updated, 1)
                                if l < len(LEVELS) - 1:
                                    for first, second, at in level_blocks(b):
                                        t = tm[second, :, first]
                                        ins = nc.vector.tensor_tensor(t, t, compact(dbank[3])[second, :, at], ALU.subtract)
                                    ins.then_inc(t_updated, 1)
                            else:
                                u = cols(flat(um), b, 1)
                                nc.vector.tensor_tensor(u, u, mbank[:, 0:256].rearrange("p (g b) -> p g b", b=b),
                                                        ALU.subtract).then_inc(u_updated, 1)
                                t = cols(flat(tm), b, 0)
                                nc.vector.tensor_tensor(t, t, dbank[3][:, 0:256].rearrange("p (g b) -> p g b", b=b),
                                                        ALU.subtract).then_inc(t_updated, 1)
                        if 17 <= step <= 21 and step % 2 and h >= 0:
                            j = (step - 17) // 2
                            dve.wait_ge(ds_done, (NJ - 1) * h + j + 1)
                            dve.wait_ge(state_ready, NJ * h + j + 1)
                            nc.vector.scalar_tensor_tensor(state[:, :], state[:, :], etot[:, j, h:h + 1], mbank[:, 0:128],
                                                           ALU.mult, ALU.add).then_inc(state_ready, 1)
                        if nxt < HEADS:
                            xtn = xt[:, nxt % 2, :, :]
                            if step == 23:
                                dve.wait_ge(km_copied, nxt + 1)
                                link(nc.vector.tensor_tensor(mx[:, :], mx[:, :], gc[0:META, 0, nxt:nxt + 1].broadcast_to([META, META]),
                                                             ALU.subtract))
                                nc.vector.scalar_tensor_tensor(mx[:, :], mx[:, :], -1.0, mx[:, :], ALU.mult,
                                                               ALU.max).then_inc(mdif_ready, 1)
                                dve.wait_ge(q_root, nxt + 1)
                                nc.vector.scalar_tensor_tensor(qkv[:, 0, META:L], qkv[:, 0, META:L], float(128) ** -0.5, flat(xd),
                                                               ALU.mult, ALU.mult).then_inc(q_ready, 1)
                            if step == 24:
                                dve.wait_ge(gc_spread, nxt + 1)
                                link(nc.vector.tensor_tensor(xtn, chunks(dbank[1]), per_chunk(gc, nxt, 1), ALU.subtract))
                                nc.vector.scalar_tensor_tensor(flat(xtn), flat(xtn), -1.0, flat(xtn), ALU.mult,
                                                               ALU.max).then_inc(dif_ready, 1)
                                dve.wait_ge(k_root, nxt + 1)
                                mult(qkv[:, 1, 0:META], qkv[:, 1, 0:META], sqm[:, :])
                                mult(qkv[:, 1, META:L], qkv[:, 1, META:L], flat(am)).then_inc(k_ready, 1)
                            if step == 25:
                                dve.wait_ge(xd_ready, nxt + 1)
                                dve.wait_ge(k_ready, nxt + 1)
                                mult(am[:, :, :], xtn, per_chunk(beta, nxt, 1)).then_inc(xb_ready, 1)
                                mult(xtn, xtn, all_chunks(tri)).then_inc(xt_ready, 1)
                            if step == 26:
                                dve.wait_ge(v_turned, nxt + 1)
                                mult(vb[:, :, :], chunks(dbank[0]), per_chunk(beta, nxt, 1)).then_inc(vb_ready, 1)
                        if step == 27 and h >= 0:
                            if nxt < HEADS:
                                dve.wait_ge(q_ready, nxt + 1)
                            dve.wait_ge(o_root, h + 1)
                            link(nc.vector.scalar_tensor_tensor(flat(xd), dbank[3][:, :], on_scaled[:, 0:1], flat(osq), ALU.mult,
                                                                ALU.mult))
                            dve.wait_ge(zs_ready, h + 1)
                            mult(flat(xd), flat(xd), zs[:, h % 2, :]).then_inc(ogf_ready, 1)
                        yield

            def convolve(c, first_column, taps):
                to, x = cv[:, c % 2, :], raw[:, c % 2, :]
                n = taps.shape[1]
                for j in range(n):
                    xj = x[:, first_column + j:first_column + j + L]
                    if j == 0:
                        ins = nc.vector.tensor_scalar(to, xj, taps[:, 0:1], None, ALU.mult)
                    else:
                        ins = nc.vector.scalar_tensor_tensor(to, xj, taps[:, j:j + 1], to, ALU.mult, ALU.add)
                    if j < n - 1:
                        link(ins)
                        yield
                ins.then_inc(conv_ready, 1)

            def evacuate(n, kind, m):
                p = big[n % 2]
                dve.wait_ge(block_done, n + 1)
                if kind in ("q", "k", "v"):
                    i = ("q", "k", "v").index(kind)
                    c = conv_number(kind, m)
                    dve.wait_ge(raw_ready, 3 * m + i + 1)
                    if c < 2:
                        dve.wait_ge(xlo_ready, KT // 2)
                        dve.wait_ge(xlo_even, KT // 2)
                    elif kind != "k":
                        dve.wait_ge(qkv_ready, 3 * m + (i > 0))
                    yield from convolve(c, 0, sm[:, CQKV + 4 * (8 * i + m):CQKV + 4 * (8 * i + m) + 4])
                if kind == "u":
                    c = conv_number(kind, m)
                    dve.wait_ge(c_ready, m + 1)
                    if m == 0:
                        dve.wait_ge(zeroed, 1)
                    mult(raw[:, c % 2, 3:3 + HALF], p[0][:, 0:HALF], cbuf[:, 0:HALF])
                    mult(raw[:, c % 2, 3 + HALF:3 + L], p[1][:, 0:HALF], cbuf[:, HALF:L]).then_inc(c_used, 1)
                    dve.wait_ge(c_used, m + 1)
                    yield
                    dve.wait_ge(qkv_ready, 3 * m + 2)
                    yield from convolve(c, 1, sm[:, CSC + 3 * m:CSC + 3 * m + 3])
                if kind == "b":
                    if m:
                        dve.wait_ge(yblo_ready, m)
                    dve.wait_ge(conv_ready, 4 * m + 4)
                    mult(ybf, p[0][:, :], cv[:, conv_number("u", m) % 2, META:L]).then_inc(yb_ready, 1)
                if kind == "sc":
                    i = gate_number("gb", m)
                    dve.wait_ge(ge_ready, i + 1)
                    mult(mixb[:, m, 0:T], p[0][:, :], egate[:, i % 2, :]).then_inc(mixb_ready, 1)
                if kind == "dn":
                    i = gate_number("ga", m)
                    dve.wait_ge(ge_ready, i + 1)
                    dve.wait_ge(yblo_ready, KT + m)
                    mult(ybf, p[0][:, :], egate[:, i % 2, :]).then_inc(dn_gated, 1)
                    dve.wait_ge(dn_gated, m + 1)
                    dve.wait_ge(mixb_ready, m + 1)
                    nc.vector.tensor_tensor(ybf, ybf, mixb[:, m, 0:T], ALU.add).then_inc(yb_ready, 1)
                    if m == KT - 1:
                        dve.wait_ge(ybhi_ready, 2 * KT)
                        nc.vector.tensor_tensor(yb_lo[:, m, :], ybf, yb_hi[:, m, :].bitcast(f32), ALU.subtract).then_inc(yblo_last, 1)
                if kind == "wo":
                    dve.wait_ge(h_again, 16)
                    nc.vector.tensor_tensor(h1[:, m, :], p[0][:, :], h1[:, m, :], ALU.add).then_inc(h1_ready, 1)
                    dve.wait_ge(hnhi_ready, m + 1)
                    nc.vector.scalar_tensor_tensor(og_lo[:, m, :], h1[:, m, :], sm[:, NORM2 + m:NORM2 + m + 1],
                                                   og_hi[:, m, :].bitcast(f32), ALU.mult, ALU.subtract).then_inc(hnlo_ready, 1)
                if kind == "gate":
                    if m == 0:
                        dve.wait_ge(rs2_ready, 1)
                    else:
                        dve.wait_ge(sg_ready, m)
                    mult(tg[:, :], p[0][:, :], rs2[:, :]).then_inc(tg_ready, 1)
                    yield
                    dve.wait_ge(sg_ready, m + 1)
                    mult(sg[:, :], sg[:, :], rs2[:, :]).then_inc(sg2_ready, 1)
                if kind == "up":
                    if m:
                        dve.wait_ge(flo_ready, m)
                    dve.wait_ge(sg2_ready, m + 1)
                    mult(ff[:, :], p[0][:, :], sg[:, :]).then_inc(f_ready, 1)

            delta = delta_steps()
            for n in range(STREAM + 1):
                chores = evacuate(n - 1, *BLOCKS[n - 1]) if 1 <= n <= MAIN else iter(())
                for q in range(4):
                    if n >= DELTA_FROM:
                        next(delta, None)
                    next(chores, None)
                next(chores, None)
                if n == 0:
                    dve.wait_ge(bat_done, 1)
                    for s in range(2):
                        ins = nc.vector.tensor_copy(bat[:, s * HALF:(s + 1) * HALF], dbank[s][0:16, 0:HALF])
                    ins.then_inc(bat_copied, 1)
                if n == 1:
                    token_factors()
                if n == 2:
                    token_decays()
                if n in DOWN_ENDS:
                    m = DOWN_ENDS[n]
                    if FT * (m + 1) % 8 == 0:
                        dve.wait_ge(block_done, n)
                    else:
                        dve.wait_ge(down_done, m + 1 - sum(FT * (i + 1) % 8 == 0 for i in range(m)))
                    nc.vector.tensor_tensor(h1[:, m, :], big[m % 2][0][:, :], h1[:, m, :], ALU.add).then_inc(h2_ready, 1)
            dve.wait_ge(rs2_ready, 2)
            for m in range(KT):
                nc.vector.scalar_tensor_tensor(h1[:, m, :], h1[:, m, :], sm[:, NORMF + m:NORMF + m + 1], rs2[:, :], ALU.mult,
                                               ALU.mult).then_inc(y_ready, 1)

        @block.tensor
        def _(pe):
            def mm(o, w, x, start=True, stop=True):
                return nc.tensor.matmul(o, w, x, start=start, stop=stop)

            def products(outs, n, tile, x_h, x_l, first, last):
                wh = w_hi[:, n % 2, tile * 128:(tile + 1) * 128]
                wl = w_lo[:, n % 2, tile * 128:(tile + 1) * 128]
                for w, xs, a in ((wh, x_h, 0), (wh, x_l, 1), (wl, x_h, 2)):
                    for o, x in zip(outs, xs):
                        ins = mm(o, w, x, start=first and a == 0, stop=last and a == 2)
                return ins

            pe.wait_ge(ones_ready, 1)
            for _ in range(WARM):
                mm(dbank[3][:, 0:128], ones, ones)
            pe.wait_ge(x_added, KT - 1)
            for s in range(2):
                ins = mm(big[0][s][:, 0:HALF], ones, sums1[:, s * HALF:(s + 1) * HALF])
            ins.then_inc(x_sums, 1)
            for _ in range(WARM // 3):
                mm(dbank[3][:, 0:128], ones, ones)

            def token_projections():
                pe.wait_ge(wba_ready, 1)
                for k in range(KT):
                    for w, x, a in ((wba_hi, x_hi, 0), (wba_hi, x_lo, 1), (wba_lo, x_hi, 2)):
                        for s in range(2):
                            ins = mm(dbank[s][0:16, 0:HALF], w[:, k, :], x[:, k, s * HALF:(s + 1) * HALF],
                                     start=k == 0 and a == 0, stop=k == KT - 1 and a == 2)
                ins.then_inc(bat_done, 1)

            def turn_token_projections():
                pe.wait_ge(const_in, 16)
                pe.wait_ge(bat_copied, 1)
                for j in range(NJ + 1):
                    at = slice(0, 128) if j == 0 else slice(META + 128 * (j - 1), META + 128 * j)
                    ins = nc.tensor.transpose(dbank[2][:, 16 * j:16 * j + 16], bat[:, at], ident[0:16, 0:16])
                ins.then_inc(ba_done, 1)

            def token_sums():
                pe.wait_ge(g_ready, 1)
                gs = g[:, 1:, :].rearrange("p j h -> p (j h)")
                mm(dbank[1][:, 0:32], tri, gs)
                mm(dbank[1][:, 32:64], rev, gs)
                mm(dbank[1][:, 64:96], ones, gs)
                mm(dbank[1][0:META, 96:104], tri[0:META, 0:META], g[0:META, 0, :])
                mm(dbank[1][0:META, 104:112], rev[0:META, 0:META], g[0:META, 0, :]).then_inc(cums_done, 1)

            def delta_steps():
                turn = nc.tensor.transpose
                c128 = [slice(128 * j, 128 * (j + 1)) for j in range(NJ)]
                c64 = [slice(64 * j, 64 * (j + 1)) for j in range(NJ)]
                tiles32 = [(slice(32 * i, 32 * (i + 1)), slice(16 * i, 16 * (i + 1))) for i in range(4)]
                tok = [slice(META + 128 * j, META + 128 * (j + 1)) for j in range(NJ)]
                qh, kh, vh = qkv[:, 0, :], qkv[:, 1, :], qkv[:, 2, :]
                for h in range(-1, HEADS):
                    nxt = h + 1
                    for step in range(0 if h >= 0 else PRE, STEPS):
                        if step == 0:
                            pe.wait_ge(k_ready, h + 1)
                            pe.wait_ge(egc_ready, h + 1)
                            for j in range(NJ):
                                ins = mm(dbank[1][:, c128[j]], kh[:, tok[j]], kh[:, tok[j]])
                            ins.then_inc(kk_done, 1)
                            if h:
                                pe.wait_ge(o_root, h)
                            turn(dbank[2][:, 0:128], kh[:, 0:128], ident)
                            turn(dbank[2][:, 128:256], vh[:, 0:128], ident)
                            mm(dbank[2][0:META, 256:272], kh[:, 0:META], kh[:, 0:META]).then_inc(mpre_done, 1)
                            pe.wait_ge(vb_ready, h + 1)
                            for j in range(NJ):
                                ins = turn(dbank[0][:, c128[j]], kh[:, tok[j]], ident)
                            ins.then_inc(k_turned, 1)
                        if step == 1:
                            pe.wait_ge(q_ready, h + 1)
                            if h:
                                pe.wait_ge(ogf_ready, h)
                            for j in range(NJ):
                                ins = mm(dbank[3][:, c128[j]], kh[:, tok[j]], qh[:, tok[j]])
                            ins.then_inc(qk_done, 1)
                        if step == 2:
                            pe.wait_ge(t_ready, h + 1)
                            for j in range(NJ):
                                ins = turn(dbank[1][:, c128[j]], tm[:, j, :], ident)
                            ins.then_inc(u_turned, 1)
                        if 3 <= step <= 13 and step % 2:
                            l = (step - 3) // 2
                            b = LEVELS[l]
                            done = len(LEVELS) * h + l
                            if l == 0:
                                pe.wait_ge(u_ready, h + 1)
                            else:
                                pe.wait_ge(u_updated, done)
                            if l < MASKED:
                                pe.wait_ge(alev_ready, MASKED * h + l + 1)
                            if l == META_LEVELS + 2:
                                pe.wait_ge(mv_ready, h + 1)
                            if l == 1:
                                pe.wait_ge(mu_ready, h + 1)
                            if 1 <= l <= META_LEVELS:
                                mm(dbank[1][0:META, 256:264], malev[:, l - 1, :], cols(mu[:, :], LEVELS[l - 1], 1))
                            for j in range(NJ):
                                if l == 0:
                                    ins = mm(dbank[1][:, c64[j]], alev[:, l, j, :], cols(um[:, j, :], b, 1))
                                elif l < MASKED:
                                    for rows, at in tiles32:
                                        ins = mm(compact(dbank[1])[rows, j, at], alev[rows, l, j, rows],
                                                 cols(um[rows, j, rows], b, 1))
                                else:
                                    for first, second, at in level_blocks(b):
                                        ins = mm(compact(dbank[1])[first, j, at], am[second, j, first], um[second, j, second])
                            ins.then_inc(p_done, 1)
                        if 4 <= step <= 14 and step % 2 == 0:
                            l = (step - 4) // 2
                            b = LEVELS[l]
                            done = len(LEVELS) * h + l
                            pe.wait_ge(pb_ready, done + 1)
                            if l == 0:
                                pe.wait_ge(mt_ready, h + 1)
                                pe.wait_ge(kd_ready, h + 1)
                                mm(dbank[0][0:META, 0:META], mt[:, :], ident[0:META, 0:META]).then_inc(mt_turned, 1)
                                pe.wait_ge(mkv_ready, h + 1)
                                pe.wait_ge(qkt_ready, h + 1)
                            else:
                                pe.wait_ge(t_updated, (len(LEVELS) - 1) * h + l)
                            if l == META_LEVELS + 1:
                                mm(dbank[1][0:META, 256:384], mu[:, :], mvb[:, :]).then_inc(mv_done, 1)
                            if l == META_LEVELS + 2:
                                mm(dbank[2][:, 256:384], mkdec[:, :], mvnew)
                            if 1 <= l <= META_LEVELS:
                                mm(dbank[2][0:META, 256:264], mt[:, :], cols(mpb[:, l - 1, :], LEVELS[l - 1], 1))
                            if 1 <= l < META_LEVELS:
                                mm(dbank[3][0:META, 256:264], mpb[:, l - 1, :], cols(mt[:, :], LEVELS[l - 1], 0))
                            for j in range(NJ):
                                if l == 0:
                                    mm(dbank[2][:, c64[j]], tm[:, j, :], cols(pb[:, l, j, :], b, 1))
                                    ins = mm(dbank[3][:, c64[j]], pb[:, l, j, :], cols(tm[:, j, :], b, 0))
                                elif l < MASKED:
                                    for rows, at in tiles32:
                                        mm(compact(dbank[2])[rows, j, at], tm[rows, j, rows], cols(pb[rows, l, j, rows], b, 1))
                                    for rows, at in tiles32:
                                        ins = mm(compact(dbank[3])[rows, j, at], pb[rows, l, j, rows],
                                                 cols(tm[rows, j, rows], b, 0))
                                else:
                                    for first, second, at in level_blocks(b):
                                        ins = mm(compact(dbank[2])[first, j, at], tm[first, j, first], pbx[first, j, second])
                                    if l < len(LEVELS) - 1:
                                        for first, second, at in level_blocks(b):
                                            ins = mm(compact(dbank[3])[second, j, at], pbx[first, j, second],
                                                     tm[first, j, first])
                            ins.then_inc(du_done, 1)
                        if step == 15:
                            pe.wait_ge(u_updated, len(LEVELS) * (h + 1))
                            for j in range(NJ):
                                ins = mm(dbank[0][:, c128[j]], kbe[:, j, :], um[:, j, :])
                            ins.then_inc(w_done, 1)
                        if step == 22 and nxt < HEADS:
                            if h >= 0:
                                pe.wait_ge(state_ready, NJ * (h + 1))
                                pe.wait_ge(vn_ready, NJ * (h + 1) - 1)
                            else:
                                pe.wait_ge(tokens_ready, 1)
                            pe.wait_ge(k_squared, nxt + 1)
                            pe.wait_ge(mdiag_ready, nxt + 1)
                            mm(dbank[1][0:META, 272:288], ones[0:META, 0:META], mdg[:, :])
                            mm(dbank[1][:, 256:256 + META], ones, sqm[:, :]).then_inc(km_sums, 1)
                            mm(dbank[2][:, :], ones, flat(am)).then_inc(k_sums, 1)
                        if 16 <= step <= 22 and step % 2 == 0 and h >= 0:
                            j = (step - 16) // 2
                            if j == 0:
                                pe.wait_ge(nwt_ready, h + 1)
                                pe.wait_ge(qdec_ready, h + 1)
                            if j == NJ - 1 and nxt < HEADS:
                                pe.wait_ge(km_copied, nxt + 1)
                            pe.wait_ge(state_ready, NJ * h + j + 1)
                            mm(dbank[1][:, 0:128], um[:, j, :], vb[:, j, :], stop=False)
                            mm(dbank[1][:, 0:128], nwt[:, j, :], state[:, :], start=False).then_inc(vn_done, 1)
                            mm(dbank[3][:, c128[j]], state[:, :], qdec[:, j, :], stop=False)
                        if 17 <= step <= 23 and step % 2 and h >= 0:
                            j = (step - 17) // 2
                            pe.wait_ge(vn_ready, NJ * h + j + 1)
                            if j < NJ - 1:
                                mm(dbank[2][:, 0:128], kdec[:, j, :], vnew[:, :]).then_inc(ds_done, 1)
                            ins = mm(dbank[3][:, c128[j]], vnew[:, :], xt[:, h % 2, j, :], start=False)
                            if j == NJ - 1:
                                ins.then_inc(o_done, 1)
                        if nxt < HEADS:
                            if step == 21:
                                if h < 0:
                                    pe.wait_ge(tokens_ready, 1)
                                pe.wait_ge(q_squared, nxt + 1)
                                mm(dbank[0][:, :], ones, flat(xd)).then_inc(q_sums, 1)
                            if step == 23:
                                pe.wait_ge(diag_ready, nxt + 1)
                                pe.wait_ge(km_copied, nxt + 1)
                                if h >= 0:
                                    pe.wait_ge(vn_ready, NJ * (h + 1))
                                mm(dbank[1][:, :], ones, flat(dg)).then_inc(gc_spread, 1)
                        if step == 25 and h >= 0:
                            pe.wait_ge(o_squared, h + 1)
                            if nxt < HEADS:
                                pe.wait_ge(k_root, nxt + 1)
                            mm(dbank[2][:, :], ones, flat(osq)).then_inc(o_sums, 1)
                        if step == 24 and nxt < HEADS:
                            pe.wait_ge(q_root, nxt + 1)
                            pe.wait_ge(qkv_ready, 3 * nxt + 3)
                            for j in range(NJ):
                                ins = turn(dbank[0][:, c128[j]], vh[:, tok[j]], ident)
                            ins.then_inc(v_turned, 1)
                        yield

            delta = delta_steps()
            for n, (kind, m) in enumerate(BLOCKS):
                x_h, x_l = {"sc": (yb_hi, yb_lo), "dn": (og_hi, og_lo), "wo": (yb_hi, yb_lo), "gate": (og_hi, og_lo),
                            "up": (og_hi, og_lo)}.get(kind, (x_hi, x_lo))
                if n >= 2:
                    wait_result_read(pe, *BLOCKS[n - 2])
                if kind == "dn":
                    pe.wait_ge(oglo_ready, KT)
                if kind in WIDE:
                    parts = [slice(0, HALF), slice(HALF, L)]
                    outs = [big[n % 2][s][:, 0:HALF] for s in range(2)]
                else:
                    off = META if x_h is x_hi else 0
                    parts = [slice(off, off + T)]
                    outs = [big[n % 2][0][:, :]]
                for k in range(KT):
                    if k % 4 == 0:
                        pe.wait_ge(wlo_ready, 2 * n + k // 4 + 1)
                    if n == 0:
                        pe.wait_ge(xlo_ready if k % 2 else xlo_even, k // 2 + 1)
                    if kind in ("sc", "wo") and m == 0:
                        if kind == "wo" and k == KT - 1:
                            pe.wait_ge(yblo_last, 1)
                        else:
                            pe.wait_ge(yblo_ready, (KT if kind == "wo" else 0) + k + 1)
                    if kind == "gate" and m == 0:
                        pe.wait_ge(hnlo_ready, k + 1)
                    ins = products(outs, n, k, [x_h[:, k, s] for s in parts], [x_l[:, k, s] for s in parts], k == 0, k == KT - 1)
                    if k == KT - 1:
                        ins.then_inc(block_done, 1)
                    if n == 1 and k == 1:
                        turn_token_projections()
                    if kind == "up" and m == 0 and k == 1:
                        pe.wait_ge(sqa_ready, KT)
                        mm(dbank[0][:, :], ones, sqa[:, :]).then_inc(h_sums, 1)
                    if k % 2 and n >= DELTA_FROM:
                        next(delta, None)
                if n == 0:
                    token_projections()
                if n == 2:
                    token_sums()
            for d in range(DOWN):
                n = MAIN + d
                for i in range(8):
                    if i % 4 == 0:
                        pe.wait_ge(wlo_ready, 2 * n + i // 4 + 1)
                    if d == DOWN - 1 and i == 4:
                        pe.wait_ge(sqf_ready, KT - 1)
                        mm(dbank[0][:, :], ones, sqa[:, :], stop=False)
                    m, k = divmod(8 * d + i, FT)
                    if k == 0:
                        if m < 2:
                            wait_result_read(pe, *BLOCKS[MAIN + m - 2])
                        else:
                            pe.wait_ge(h2_ready, m - 1)
                    if m == 0:
                        pe.wait_ge(flo_ready, k + 1)
                    ins = products([big[m % 2][0][:, :]], n, i, [f_hi[:, k, :]], [f_lo[:, k, :]], k == 0, k == FT - 1)
                    if i == 7:
                        ins.then_inc(block_done, 1)
                    elif k == FT - 1:
                        ins.then_inc(down_done, 1)
            pe.wait_ge(h2_squared, KT)
            mm(dbank[0][:, :], ones, sqt[:, (KT - 1) % 2, :], start=False).then_inc(last_sums, 1)


def kernel(x, meta_tokens, norm1, w_in, conv_qkv, a_log, dt_bias, o_norm, w_dn_out, conv_sc, w_sc_out, w_o, norm2,
           w_gate_up, w_down, final_norm):
    import numpy as np
    import concourse.bacc as bacc
    from concourse.bass_utils import run_bass_kernel_spmd

    def tiles(w):
        w = np.asarray(w)
        return w.reshape(w.shape[0] // 128, 128, w.shape[1] // 128, 128).transpose(2, 1, 0, 3).reshape(
            w.shape[1] // 128, 128, w.shape[0])

    def vector(v):
        return np.asarray(v).reshape(-1, 128).T

    win = np.asarray(w_in[0])
    names = ("q", "k", "v", "z", "ba", "c", "u", "b", "ga", "gb")
    widths = [D] * 4 + [2 * HEADS] + [D] * 5
    start = dict(zip(names, np.cumsum([0] + widths[:-1])))
    mats = {k: tiles(win[:, start[k]:start[k] + D]) for k in names if k != "ba"}
    gu = np.asarray(w_gate_up[0])
    mats |= {"sc": tiles(w_sc_out[0]), "dn": tiles(w_dn_out[0]), "wo": tiles(w_o[0]),
             "gate": tiles(gu[:, :FF]), "up": tiles(gu[:, FF:])}
    down = tiles(w_down[0]).reshape(KT, 128, FT, 128).transpose(0, 2, 1, 3).reshape(DOWN, 8, 128, 128)
    down = down.transpose(0, 2, 1, 3).reshape(DOWN, 128, 1024)
    w_stream = np.concatenate([np.stack([mats[k][m] for k, m in BLOCKS]), down])
    w_ba = win[:, start["ba"]:start["ba"] + 16].reshape(KT, 128, 16).transpose(1, 0, 2).reshape(128, KT * 16)
    h_t = np.concatenate([np.asarray(meta_tokens), np.asarray(x[0])]).T.reshape(KT, 128, L).transpose(1, 0, 2)
    cq = np.asarray(conv_qkv[0]).T.reshape(24, 128, 4).transpose(1, 0, 2).reshape(128, 96)
    cs = np.asarray(conv_sc[0]).T.reshape(8, 128, 3).transpose(1, 0, 2).reshape(128, 24)
    small = np.concatenate([vector(norm1[0]), vector(norm2[0]), vector(final_norm), cq, cs, vector(o_norm[0]),
                            np.broadcast_to(np.asarray(a_log[0]), (128, HEADS)),
                            np.broadcast_to(np.asarray(dt_bias[0]), (128, HEADS))], axis=1)
    r = np.arange(128)
    row, col = r[:, None], r[None, :]
    consts = [row == col, row <= col, row > col]
    for b in [1] + LEVELS:
        consts.append((row // (2 * b) == col // (2 * b)) & (row // b % 2 == 1) & (col // b % 2 == 0))
    consts = np.stack(consts, axis=1).astype(np.float32)

    arrays = {"h_t": h_t, "w_stream": w_stream, "w_ba": w_ba, "small": small, "consts": consts}
    arrays = {k: np.ascontiguousarray(a) for k, a in arrays.items()}
    nc = bacc.Bacc("TRN2", target_bir_lowering=False, num_devices=1)
    args = [nc.dram_tensor(k, a.shape, mybir.dt.from_np(a.dtype), kind="ExternalInput").ap() for k, a in arrays.items()]
    out = nc.dram_tensor("out", (128, KT, T), mybir.dt.float32, kind="ExternalOutput").ap()
    hybrid_block_kernel(nc, *args, out)
    y = run_bass_kernel_spmd(nc, [arrays], core_ids=[0]).results[0]["out"]
    return np.ascontiguousarray(y.transpose(2, 1, 0).reshape(1, T, D))
```

```python
from contextlib import ExitStack

import concourse.bass as bass
from concourse import mybir

D = 1024
T = 512
META = 16
L = META + T
HALF = L // 2
HEADS = 8
FF = 2816
KT = D // 128
FT = FF // 128
NJ = T // 128
EPS = 1e-6
LEVELS = [2, 4, 8, 16, 32, 64]
META_LEVELS = 3
WARM = 28
MASKED = LEVELS.index(32)

BLOCKS = [(kind, h) for h in range(HEADS) for kind in ("q", "k", "v", "z", "c", "u", "b")]
BLOCKS += [(kind, m) for m in range(KT) for kind in ("gb", "sc")]
BLOCKS += [("ga", 0)] + [x for m in range(KT - 1) for x in (("ga", m + 1), ("dn", m))] + [("dn", KT - 1)]
BLOCKS += [("wo", m) for m in range(KT)]
BLOCKS += [(kind, m) for m in range(FT) for kind in ("gate", "up")]
MAIN = len(BLOCKS)
DOWN = FT * KT // 8
STREAM = MAIN + DOWN
AT = {b: n for n, b in enumerate(BLOCKS)}
WIDE = ("q", "k", "v", "c", "u")
CONV = ("q", "k", "v", "u")
STEPS = 28
PRE = 20
DELTA_FROM = 4
NORM1, NORM2, NORMF = 0, 8, 16
CQKV = 24
CSC = CQKV + 24 * 4
ONORM = CSC + 8 * 3
ALOG = ONORM + 1
DTB = ALOG + 8
NSMALL = DTB + 8
CI, CTRI, CREV, CLEV = 0, 1, 2, 3
NCONST = CLEV + 1 + MASKED


EXP_LN_FROM = [AT["c", h] for h in range(HEADS)] + [AT["wo", 0], MAIN + 1]
GATES = [b for b in BLOCKS if b[0] in ("gb", "ga")]
DOWN_ENDS = {MAIN + (FT * m + FT - 1) // 8 + 1: m for m in range(KT)}


def conv_number(kind, h):
    return 4 * h + CONV.index(kind)


def level_blocks(b):
    return [(slice(2 * b * i, 2 * b * i + b), slice(2 * b * i + b, 2 * b * i + 2 * b), slice(b * i, b * i + b))
            for i in range(64 // b)]


def gate_number(kind, m):
    return GATES.index((kind, m))


def hybrid_block_kernel(nc, h_t, w_stream, w_ba, small, consts, out):
    f32 = mybir.dt.float32
    f32r = mybir.dt.float32r
    ALU = mybir.AluOpType
    ACT = mybir.ActivationFunctionType

    ctx = ExitStack()
    with ctx:
        def sem(name):
            return ctx.enter_context(nc.semaphore(name))

        def sb(name, shape, dt=f32, where=ctx):
            return where.enter_context(nc.sbuf_tensor(name, shape, dt))

        bank = [ctx.enter_context(nc.psum_tensor(f"bank{i}", [128, 512], f32)) for i in range(8)]
        big = [bank[0:2], bank[2:4]]
        dbank = bank[4:8]

        cst = sb("cst", [128, NCONST, 128])
        ident, tri, rev = (cst[:, c, :] for c in (CI, CTRI, CREV))
        ones_mem = sb("ones_mem", [128, 128])
        ones = ones_mem[:, :]
        ones_r = sb("ones_r", [128, 128], f32r)
        zeros_r = sb("zeros_r", [128, 128], f32r)
        sm = sb("sm", [128, NSMALL])
        w_raw = sb("w_raw", [128, 3, 1024])
        w_hi = sb("w_hi", [128, 2, 1024], f32r)
        w_lo = sb("w_lo", [128, 2, 1024], f32r)
        eps = sb("eps", [128, 2])
        og_hi = sb("og_hi", [128, KT, T], f32r)
        og_lo = sb("og_lo", [128, KT, T], f32r)

        mix_mem = ExitStack()
        x_hi = sb("x_hi", [128, KT, L], f32r, mix_mem)
        x_lo = sb("x_lo", [128, KT, L], f32r, mix_mem)
        yb_hi = sb("yb_hi", [128, KT, T], f32r, mix_mem)
        yb_lo = sb("yb_lo", [128, KT, T], f32r, mix_mem)
        h_in = sb("h_in", [128, KT, L], f32, mix_mem)
        raw = sb("raw", [128, 2, 3 + L], f32, mix_mem)
        cv = sb("cv", [128, 2, L], f32, mix_mem)
        cbuf = sb("cbuf", [128, L], f32, mix_mem)
        ybf = cbuf[:, 0:T]
        egate = sb("egate", [128, 2, T], f32, mix_mem)
        eg = egate[:, 1, :].rearrange("p (j c) -> p j c", c=128)
        qkv = sb("qkv", [128, 3, L], f32, mix_mem)
        zs = sb("zs", [128, 2, T], f32, mix_mem)
        tile4 = [128, NJ, 128]
        xt = sb("xt", [128, 2, NJ, 128], f32, mix_mem)
        xd = sb("xd", tile4, f32, mix_mem)
        am = sb("am", tile4, f32, mix_mem)
        alev = sb("alev", [128, MASKED, NJ, 128], f32, mix_mem)
        tm = sb("tm", tile4, f32, mix_mem)
        um = sb("um", tile4, f32, mix_mem)
        pb = h_in[:, KT - 4:KT, :].rearrange("p k l -> p (k l)")[:, 0:MASKED * T].rearrange(
            "p (l j c) -> p l j c", l=MASKED, c=128)
        kbe = sb("kbe", tile4, f32, mix_mem)
        kdec = sb("kdec", tile4, f32, mix_mem)
        vb = sb("vb", tile4, f32, mix_mem)
        qdec = sb("qdec", tile4, f32, mix_mem)
        nwt = sb("nwt", tile4, f32, mix_mem)
        osq = nwt
        pbx = nwt
        sqm = sb("sqm", [128, META], f32, mix_mem)
        vnew = sb("vnew", [128, 128], f32, mix_mem)
        state = sb("state", [128, 128], f32, mix_mem)
        g = sb("g", [128, NJ + 1, HEADS], f32, mix_mem)
        ga1 = sb("ga1", [128, NJ + 1, HEADS], f32, mix_mem)
        ga2 = sb("ga2", [128, NJ + 1, HEADS], f32, mix_mem)
        beta = sb("beta", [128, NJ + 1, HEADS], f32, mix_mem)
        gc = sb("gc", [128, NJ + 1, HEADS], f32, mix_mem)
        erev = sb("erev", [128, NJ + 1, HEADS], f32, mix_mem)
        etot = sb("etot", [128, NJ, HEADS], f32, mix_mem)
        be = sb("be", [128, NJ, HEADS], f32, mix_mem)
        nea = sb("nea", [128, HEADS], f32, mix_mem)
        on_scaled = sb("on_scaled", [128, 1], f32, mix_mem)
        wba = sb("wba", [128, KT * 16], f32, mix_mem)
        wba_hi = sb("wba_hi", [128, KT, 16], f32r, mix_mem)
        wba_lo = sb("wba_lo", [128, KT, 16], f32r, mix_mem)
        mdg = sb("mdg", [META, META], f32, mix_mem)
        mx = sb("mx", [META, META], f32, mix_mem)
        ma = sb("ma", [META, META], f32, mix_mem)
        malev = sb("malev", [META, META_LEVELS, META], f32, mix_mem)
        mt = sb("mt", [META, META], f32, mix_mem)
        mu = sb("mu", [META, META], f32, mix_mem)
        mpb = sb("mpb", [META, META_LEVELS, META], f32, mix_mem)
        mkdec = sb("mkdec", [META, 128], f32, mix_mem)
        mvb = sb("mvb", [META, 128], f32, mix_mem)
        mvnew = wba[0:META, :]
        sums1 = qkv[:, 2, :]
        xnf = [cv[:, 0, :], cv[:, 1, :], qkv[:, 0, :], qkv[:, 1, :]]
        rs1 = cbuf
        bat = xt[0:16, :, :, :].rearrange("p a j c -> p (a j c)")[:, 0:L]
        mixb = h_in
        mix_mem.close()

        split_mem = ExitStack()
        before_input = 2 * KT * L + 2 * KT * T
        before = before_input + KT * L + 2 * (3 + L) + 2 * L + L + 2 * T + 3 * L + 2 * T
        sb("before_input", [128, before_input], f32, split_mem)
        dg_hi = sb("dg_hi", tile4, f32r, split_mem)
        sb("before_split", [128, before - before_input - T], f32, split_mem)
        dg_lo = sb("dg_lo", [128, 2, NJ, 128], f32r, split_mem)
        q_lo = sb("q_lo", tile4, f32r, split_mem)
        k_lo = sb("k_lo", tile4, f32r, split_mem)
        sb("between_split", [128, MASKED, NJ, 128], f32, split_mem)
        k_hi = sb("k_hi", tile4, f32r, split_mem)
        sb("um_split", tile4, f32, split_mem)
        qo_hi = sb("qo_hi", tile4, f32r, split_mem)
        sb("kdec_split", tile4, f32, split_mem)
        sb("vb_split", tile4, f32, split_mem)
        sb("qdec_split", tile4, f32, split_mem)
        o_lo = sb("o_lo", tile4, f32r, split_mem)
        split_mem.close()

        ffn_mem = ctx.enter_context(ExitStack())
        f_hi = sb("f_hi", [128, FT, T], f32r, ffn_mem)
        f_lo = sb("f_lo", [128, FT, T], f32r, ffn_mem)
        f_pad = sb("f_pad", [128, 3 * T], f32, ffn_mem)
        sqa = sb("sqa", [128, T], f32, ffn_mem)
        sqt = sb("sqt", [128, 2, T], f32, ffn_mem)
        rs2 = sb("rs2", [128, T], f32, ffn_mem)
        tg = sb("tg", [128, T], f32, ffn_mem)
        sg = sb("sg", [128, T], f32, ffn_mem)
        ff = sb("ff", [128, T], f32, ffn_mem)
        h1 = sb("h1", [128, KT, T], f32, ffn_mem)
        del f_pad

        const_in, small_in, ba_in, h_again, stored = (sem(n) for n in ("const_in", "small_in", "ba_in", "h_again", "stored"))
        h_loaded = [sem(f"h_loaded{part}") for part in range(4)]
        w_in = [sem(f"w_in{slot}") for slot in range(3)]
        act_chain, dve_chain, pool_chain = sem("act_chain"), sem("dve_chain"), sem("pool_chain")
        ones_ready, ones_split, zeros_ready, zeroed = (
            sem(n) for n in ("ones_ready", "ones_split", "zeros_ready", "zeroed"))
        whi_ready, wlo_ready, block_done, down_done = (
            sem(n) for n in ("whi_ready", "wlo_ready", "block_done", "down_done"))
        x_squared, x_added, x_sums, rs1_ready, xn_ready, xhi_ready, xlo_even = (
            sem(n) for n in ("x_squared", "x_added", "x_sums", "rs1_ready", "xn_ready", "xhi_ready", "xlo_even"))
        xlo_ready = sem("xlo_ready")
        wba_hi_ready, wba_ready, bat_done, bat_copied, ba_done, eb_ready, az_ready = (
            sem(n) for n in ("wba_hi_ready", "wba_ready", "bat_done", "bat_copied", "ba_done", "eb_ready", "az_ready"))
        ln_ready, g_ready, cums_done, exps_ready, tokens_ready = (
            sem(n) for n in ("ln_ready", "g_ready", "cums_done", "exps_ready", "tokens_ready"))
        raw_ready, conv_ready, qkv_ready, zs_ready, c_ready, c_used, ge_ready = (
            sem(n) for n in ("raw_ready", "conv_ready", "qkv_ready", "zs_ready", "c_ready", "c_used", "ge_ready"))
        yb_ready, ybhi_ready, yblo_ready, yblo_last, mixb_ready, dn_gated = (
            sem(n) for n in ("yb_ready", "ybhi_ready", "yblo_ready", "yblo_last", "mixb_ready", "dn_gated"))
        q_squared, k_squared, km_squared, q_split, k_split, q_sums, k_sums = (
            sem(n) for n in ("q_squared", "k_squared", "km_squared", "q_split", "k_split", "q_sums", "k_sums"))
        km_sums, km_copied, q_root, k_root, q_ready, k_ready, mdiag_ready = (
            sem(n) for n in ("km_sums", "km_copied", "q_root", "k_root", "q_ready", "k_ready", "mdiag_ready"))
        diag_ready, gc_spread, dif_ready, mdif_ready, mx_ready, xd_ready, egc_ready = (
            sem(n) for n in ("diag_ready", "gc_spread", "dif_ready", "mdif_ready", "mx_ready", "xd_ready", "egc_ready"))
        xb_ready, xt_ready, tm_set, v_turned, vb_ready = (
            sem(n) for n in ("xb_ready", "xt_ready", "tm_set", "v_turned", "vb_ready"))
        kk_done, mpre_done, k_turned, kd_ready, a_ready, ma_ready, mkv_ready = (
            sem(n) for n in ("kk_done", "mpre_done", "k_turned", "kd_ready", "a_ready", "ma_ready", "mkv_ready"))
        alev_ready, t_ready, u_ready, mt_ready, mt_turned, mu_ready, qk_done = (
            sem(n) for n in ("alev_ready", "t_ready", "u_ready", "mt_ready", "mt_turned", "mu_ready", "qk_done"))
        qkt_ready, qdec_ready = (
            sem(n) for n in ("qkt_ready", "qdec_ready"))
        p_done, pb_ready, du_done, u_updated, t_updated, mv_done, mv_ready = (
            sem(n) for n in ("p_done", "pb_ready", "du_done", "u_updated", "t_updated", "mv_done", "mv_ready"))
        w_done, nwt_ready, vn_done, vn_ready, ds_done, state_ready, o_done = (
            sem(n) for n in ("w_done", "nwt_ready", "vn_done", "vn_ready", "ds_done", "state_ready", "o_done"))
        o_squared, o_split, o_sums, o_root, ogf_ready, oghi_ready, oglo_ready = (
            sem(n) for n in ("o_squared", "o_split", "o_sums", "o_root", "ogf_ready", "oghi_ready", "oglo_ready"))
        h1_ready, hnhi_ready, hnlo_ready, sqt_ready, sqa_ready, h_sums, rs2_ready = (
            sem(n) for n in ("h1_ready", "hnhi_ready", "hnlo_ready", "sqt_ready", "sqa_ready", "h_sums", "rs2_ready"))
        tg_ready, sg_ready, sg2_ready, f_ready, fhi_ready, flo_ready, h2_ready = (
            sem(n) for n in ("tg_ready", "sg_ready", "sg2_ready", "f_ready", "fhi_ready", "flo_ready", "h2_ready"))
        h2_squared, sqf_ready, last_sums, y_ready = (
            sem(n) for n in ("h2_squared", "sqf_ready", "last_sums", "y_ready"))

        def cols(ap, b, which):
            return ap.rearrange("p (g two b) -> p g two b", two=2, b=b)[:, :, which, :]

        def compact(t):
            return t[:, 0:256].rearrange("p (j c) -> p j c", c=64)

        def cols4(t, b, which):
            return t.rearrange("p j (g two b) -> p j g two b", two=2, b=b)[:, :, :, which, :]

        def const_cols(m, b, which):
            return cols(m, b, which).unsqueeze(1).broadcast_to([128, NJ, 64 // b, b])

        def flat(t):
            return t[:, :, :].rearrange("p j c -> p (j c)")

        def per_chunk(t, h, first=0, n=NJ):
            return t[:, first:first + n, h].unsqueeze(2).broadcast_to([128, n, 128])

        def all_chunks(m):
            return m.unsqueeze(1).broadcast_to([128, NJ, 128])

        def wait_result_read(engine, kind, m):
            if kind in ("q", "k", "v"):
                engine.wait_ge(raw_ready, 3 * m + ("q", "k", "v").index(kind) + 1)
            elif kind in ("gb", "ga"):
                engine.wait_ge(ge_ready, gate_number(kind, m) + 1)
            else:
                engine.wait_ge({"z": zs_ready, "c": c_ready, "u": c_used, "b": yb_ready, "sc": mixb_ready, "dn": dn_gated,
                                "wo": h1_ready, "gate": tg_ready, "up": f_ready}[kind], m + 1)

        def wait_gate_used(engine, i):
            kind, m = GATES[i]
            engine.wait_ge({"gb": mixb_ready, "ga": dn_gated}[kind], m + 1)

        block = ctx.enter_context(nc.Block())

        @block.sync
        def _(sp):
            for part in range(4):
                sp.dma_start(h_in[:, 2 * part:2 * part + 2, :], h_t[:, 2 * part:2 * part + 2, :]).then_inc(h_loaded[part], 16)
            sp.dma_start(sm[:, :], small[:, :]).then_inc(small_in, 16)
            for n in range(STREAM):
                if n == 2:
                    sp.dma_start(wba[:, :], w_ba[:, :]).then_inc(ba_in, 16)
                    sp.dma_start(cst[:, :, :], consts[:, :, :]).then_inc(const_in, 16)
                if n >= 3:
                    sp.wait_ge(wlo_ready, 2 * (n - 2))
                sp.dma_start(w_raw[:, n % 3, :], w_stream[n, :, :]).then_inc(w_in[n % 3], 16)
            for m in range(KT):
                sp.wait_ge(y_ready, m + 1)
                sp.dma_start(out[:, m, :], h1[:, m, :]).then_inc(stored, 16)
            sp.wait_ge(stored, 16 * KT)


        @block.gpsimd
        def _(pool):
            chain = [0]

            def link(ins):
                chain[0] += 1
                ins.then_inc(pool_chain, 1)
                pool.wait_ge(pool_chain, chain[0])

            def mult(to, a, b):
                return nc.gpsimd.tensor_tensor(to, a, b, ALU.mult)

            nc.gpsimd.memset(ones, 1.0).then_inc(ones_ready, 1)
            nc.gpsimd.memset(raw[:, :, 0:3], 0.0)
            nc.gpsimd.memset(eps[:, 0:1], EPS)
            nc.gpsimd.memset(eps[:, 1:2], 128 * EPS)
            nc.gpsimd.memset(mpb[:, :, :], 0.0)
            nc.gpsimd.memset(alev[:, :, :, :].rearrange("p l j c -> p (l j c)"), 0.0).then_inc(zeroed, 1)

            def split_weights(n, half):
                at = slice(512 * half, 512 * half + 512)
                pool.wait_ge(whi_ready, 2 * n + half + 1)
                if n >= 2:
                    pool.wait_ge(block_done, n - 1)
                nc.gpsimd.tensor_tensor(w_lo[:, n % 2, at], w_raw[:, n % 3, at], w_hi[:, n % 2, at].bitcast(f32),
                                        ALU.subtract).then_inc(wlo_ready, 1)

            split_weights(0, 0)
            split_weights(0, 1)
            for k in range(1, KT, 2):
                pool.wait_ge(xhi_ready, k + 1)
                nc.gpsimd.tensor_tensor(x_lo[:, k, :], xnf[k % 4], x_hi[:, k, :].bitcast(f32),
                                        ALU.subtract).then_inc(xlo_ready, 1)

            def level_mask(l):
                b = LEVELS[l]
                mult(cols4(alev[:, l, :, :], b, 0), cols4(am[:, :, :], b, 0),
                     const_cols(cst[:, CLEV + 1 + l, :], b, 0)).then_inc(alev_ready, 1)

            def delta_steps():
                for h in range(-1, HEADS):
                    for step in range(0 if h >= 0 else PRE, STEPS):
                        if step == 0:
                            pool.wait_ge(a_ready, h + 1)
                            level_mask(0)
                        if step == 1:
                            pool.wait_ge(ma_ready, h + 1)
                            link(mult(mt[:, :], ma[:, :], cst[0:META, CLEV, 0:META]))
                            nc.gpsimd.tensor_tensor(mt[:, :], ident[0:META, 0:META], mt[:, :], ALU.subtract)
                            for l in range(META_LEVELS):
                                ins = mult(malev[:, l, :], ma[:, :], cst[0:META, CLEV + 1 + l, 0:META])
                            ins.then_inc(mt_ready, 1)
                        if step == 2:
                            level_mask(1)
                        if step == 3:
                            level_mask(2)
                            pool.wait_ge(q_ready, h + 1)
                            pool.wait_ge(egc_ready, h + 1)
                            mult(flat(qdec), flat(eg), qkv[:, 0, META:L]).then_inc(qdec_ready, 1)
                        if step == 4:
                            level_mask(3)
                        if step == 20 and h + 1 < HEADS:
                            if h < 0:
                                pool.wait_ge(tokens_ready, 1)
                            else:
                                pool.wait_ge(km_sums, h + 1)
                            nc.gpsimd.tensor_tensor(mdg[:, :], ident[0:META, 0:META],
                                                    gc[0:META, 0, h + 1:h + 2].broadcast_to([META, META]),
                                                    ALU.mult).then_inc(mdiag_ready, 1)
                        if step == 21 and h + 1 < HEADS:
                            nc.gpsimd.tensor_tensor(dg_hi[:, :, :], all_chunks(ident), per_chunk(ga1, h + 1, 1), ALU.mult)
                            nc.gpsimd.tensor_tensor(dg_lo[:, (h + 1) % 2, :, :], all_chunks(ident),
                                                    per_chunk(ga2, h + 1, 1), ALU.mult).then_inc(diag_ready, 1)
                        if step == 27 and h >= 0:
                            pool.wait_ge(oghi_ready, h + 1)
                            nc.gpsimd.tensor_tensor(og_lo[:, h, :], flat(xd), og_hi[:, h, :].bitcast(f32),
                                                    ALU.subtract).then_inc(oglo_ready, 1)
                        yield

            def evacuate(n, kind, m):
                if kind == "b" or kind == "dn" and m < KT - 1:
                    pool.wait_ge(ybhi_ready, (0 if kind == "b" else KT) + m + 1)
                    nc.gpsimd.tensor_tensor(yb_lo[:, m, :], ybf, yb_hi[:, m, :].bitcast(f32), ALU.subtract).then_inc(yblo_ready, 1)
                if kind == "wo":
                    pool.wait_ge(sqt_ready, m + 1)
                    if m == 0:
                        nc.gpsimd.tensor_copy(sqa[:, :], sqt[:, 0, :]).then_inc(sqa_ready, 1)
                    else:
                        pool.wait_ge(sqa_ready, m)
                        nc.gpsimd.tensor_tensor(sqa[:, :], sqa[:, :], sqt[:, m % 2, :], ALU.add).then_inc(sqa_ready, 1)
                if kind == "up":
                    pool.wait_ge(fhi_ready, m + 1)
                    nc.gpsimd.tensor_tensor(f_lo[:, m, :], ff[:, :], f_hi[:, m, :].bitcast(f32), ALU.subtract).then_inc(flo_ready, 1)

            delta = delta_steps()
            for n in range(STREAM + 1):
                for q in range(4):
                    if n >= DELTA_FROM:
                        next(delta, None)
                    if q in (1, 2) and n + 1 < STREAM:
                        split_weights(n + 1, q - 1)
                    if q == 3 and 1 <= n <= MAIN:
                        evacuate(n - 1, *BLOCKS[n - 1])
                if n not in DOWN_ENDS or DOWN_ENDS[n] == KT - 1:
                    continue
                m = DOWN_ENDS[n]
                pool.wait_ge(h2_squared, m + 1)
                if m == 0:
                    nc.gpsimd.tensor_copy(sqa[:, :], sqt[:, 0, :]).then_inc(sqf_ready, 1)
                else:
                    pool.wait_ge(sqf_ready, m)
                    nc.gpsimd.tensor_tensor(sqa[:, :], sqa[:, :], sqt[:, m % 2, :], ALU.add).then_inc(sqf_ready, 1)

        @block.scalar
        def _(act):
            chain = [0]

            def link(ins):
                chain[0] += 1
                ins.then_inc(act_chain, 1)
                act.wait_ge(act_chain, chain[0])

            def copy(to, x):
                return nc.scalar.activation(to, x, ACT.Copy)

            def inverse_root(to, sums, scale, eps_column):
                link(nc.scalar.activation(to, sums, ACT.Ln, scale=scale, bias=eps[:, eps_column:eps_column + 1]))
                return nc.scalar.activation(to, to, ACT.Exp, scale=-0.5)

            nc.scalar.preload_act_table_set("natural_log_exp_and_others")
            act.wait_ge(ones_ready, 1)
            copy(ones_r[:, :], ones).then_inc(ones_split, 1)
            nc.scalar.activation(zeros_r[:, :], ones, ACT.Copy, scale=0.0).then_inc(zeros_ready, 1)
            for k in range(KT):
                act.wait_ge(h_loaded[k // 2], 16)
                if k >= 4:
                    act.wait_ge(x_added, max(1, k - 4))
                nc.scalar.activation(xnf[k % 4], h_in[:, k, :], ACT.Square).then_inc(x_squared, 1)

            def split_weights(n, half):
                at = slice(512 * half, 512 * half + 512)
                act.wait_ge(w_in[n % 3], 16 * (n // 3 + 1))
                if n >= 2:
                    act.wait_ge(block_done, n - 1)
                copy(w_hi[:, n % 2, at], w_raw[:, n % 3, at]).then_inc(whi_ready, 1)

            split_weights(0, 0)
            split_weights(0, 1)
            act.wait_ge(x_sums, 1)
            act.wait_ge(zeroed, 1)
            halves = [slice(0, HALF), slice(HALF, L)]
            for s in range(2):
                nc.scalar.activation(rs1[:, halves[s]], big[0][s][:, 0:HALF], ACT.Ln, scale=1.0 / D,
                                     bias=eps[:, 0:1]).then_inc(act_chain, 1)
            for s in range(2):
                chain[0] += 1
                act.wait_ge(act_chain, chain[0])
                ins = nc.scalar.activation(rs1[:, halves[s]], rs1[:, halves[s]], ACT.Exp, scale=-0.5)
            ins.then_inc(rs1_ready, 1)
            for k in range(KT):
                act.wait_ge(xn_ready, k + 1)
                copy(x_hi[:, k, :], xnf[k % 4]).then_inc(xhi_ready, 1)
            act.wait_ge(ba_in, 16)
            copy(wba_hi[:, :, :].rearrange("p k c -> p (k c)"), wba[:, :]).then_inc(wba_hi_ready, 1)

            def token_factors():
                act.wait_ge(ba_done, 1)
                ba = dbank[2][:, 0:16 * (NJ + 1)].rearrange("p (j c) -> p j c", c=16)
                nc.scalar.activation(beta[:, :, :], ba[:, :, 0:HEADS], ACT.Exp, scale=-1.0).then_inc(eb_ready, 1)
                act.wait_ge(small_in, 16)
                nc.scalar.activation(nea[:, :], sm[:, ALOG:ALOG + HEADS], ACT.Exp).then_inc(eb_ready, 1)
                act.wait_ge(az_ready, 1)
                link(nc.scalar.activation(ga2[:, :, :], ga1[:, :, :], ACT.Abs))
                link(nc.scalar.activation(ga2[:, :, :], ga2[:, :, :], ACT.Exp, scale=-1.0))
                nc.scalar.activation(ga2[:, :, :], ga2[:, :, :], ACT.Ln, bias=1.0).then_inc(ln_ready, 1)

            def token_decays():
                act.wait_ge(cums_done, 1)
                cums = dbank[1]
                nc.scalar.activation(be[:, :, :], cums[:, 0:32].rearrange("p (j c) -> p j c", c=HEADS), ACT.Exp)
                nc.scalar.activation(erev[:, 1:, :], cums[:, 32:64].rearrange("p (j c) -> p j c", c=HEADS), ACT.Exp)
                nc.scalar.activation(etot[:, :, :], cums[:, 64:96].rearrange("p (j c) -> p j c", c=HEADS), ACT.Exp)
                nc.scalar.activation(gc[:, 1:, :], cums[:, 0:32].rearrange("p (j c) -> p j c", c=HEADS), ACT.Copy)
                nc.scalar.activation(ga1[:, 1:, :].bitcast(f32r), cums[:, 0:32].rearrange("p (j c) -> p j c", c=HEADS), ACT.Copy)
                nc.scalar.activation(gc[0:META, 0, :], cums[0:META, 96:104], ACT.Copy)
                nc.scalar.activation(erev[0:META, 0, :], cums[0:META, 104:112], ACT.Exp).then_inc(exps_ready, 1)

            def delta_steps():
                for h in range(-1, HEADS):
                    nxt = h + 1
                    for step in range(0 if h >= 0 else PRE, STEPS):
                        if step == 1:
                            act.wait_ge(k_turned, h + 1)
                            for to, factor, first in ((kbe, be, 0), (kdec, erev, 1)):
                                for j in range(NJ):
                                    ins = nc.scalar.activation(to[:, j, :], dbank[0][:, 128 * j:128 * (j + 1)], ACT.Copy,
                                                               scale=factor[:, first + j, h:h + 1])
                            ins.then_inc(kd_ready, 1)
                        if step == 4:
                            act.wait_ge(mt_turned, h + 1)
                            copy(mu[:, :], dbank[0][0:META, 0:META]).then_inc(mu_ready, 1)
                        if 3 <= step <= 13 and step % 2:
                            l = (step - 3) // 2
                            b = LEVELS[l]
                            act.wait_ge(p_done, len(LEVELS) * h + l + 1)
                            if 1 <= l <= META_LEVELS:
                                copy(cols(mpb[:, l - 1, :], LEVELS[l - 1], 1), dbank[1][0:META, 256:264])
                            if l < MASKED:
                                ins = copy(cols(pb[:, l, :, :].rearrange("p j c -> p (j c)"), b, 1),
                                           dbank[1][:, 0:256].rearrange("p (g b) -> p g b", b=b))
                            else:
                                for rows, second, at in level_blocks(b):
                                    ins = copy(pbx[rows, :, second], compact(dbank[1])[rows, :, at])
                            ins.then_inc(pb_ready, 1)
                        if step == 4 + 2 * (META_LEVELS + 1):
                            act.wait_ge(mv_done, h + 1)
                            copy(mvnew, dbank[1][0:META, 256:384]).then_inc(mv_ready, 1)
                        if step == 15:
                            act.wait_ge(w_done, h + 1)
                            nc.scalar.activation(flat(nwt), dbank[0][:, :], ACT.Copy, scale=-1.0).then_inc(nwt_ready, 1)
                        if step == 21 and nxt < HEADS:
                            act.wait_ge(km_sums, nxt + 1)
                            copy(mx[:, :], dbank[1][0:META, 272:288])
                            copy(sqm[:, :], dbank[1][:, 256:256 + META]).then_inc(km_copied, 1)
                        if 16 <= step <= 22 and step % 2 == 0 and h >= 0:
                            act.wait_ge(vn_done, NJ * h + (step - 16) // 2 + 1)
                            copy(vnew[:, :], dbank[1][:, 0:128]).then_inc(vn_ready, 1)
                        if step == 24 and h >= 0:
                            act.wait_ge(o_done, h + 1)
                            link(nc.scalar.activation(flat(osq), dbank[3][:, :], ACT.Square))
                            if nxt < HEADS:
                                act.wait_ge(q_sums, nxt + 1)
                            copy(flat(qo_hi), flat(osq)).then_inc(o_squared, 1)
                        if nxt < HEADS:
                            if step == 20:
                                act.wait_ge(qkv_ready, 3 * nxt + 2)
                                nc.scalar.activation(sqm[:, :], qkv[:, 1, 0:META], ACT.Square).then_inc(km_squared, 1)
                                link(nc.scalar.activation(flat(xd), qkv[:, 0, META:L], ACT.Square))
                                copy(flat(qo_hi), flat(xd)).then_inc(q_squared, 1)
                            if step == 21:
                                act.wait_ge(qkv_ready, 3 * nxt + 2)
                                link(nc.scalar.activation(flat(am), qkv[:, 1, META:L], ACT.Square))
                                copy(flat(k_hi), flat(am)).then_inc(k_squared, 1)
                            if step == 23:
                                act.wait_ge(q_sums, nxt + 1)
                                inverse_root(flat(xd), dbank[0][:, :], 1.0, 0).then_inc(q_root, 1)
                            if step == 24:
                                act.wait_ge(k_sums, nxt + 1)
                                act.wait_ge(km_copied, nxt + 1)
                                inverse_root(sqm[:, :], sqm[:, :], 1.0, 0)
                                inverse_root(flat(am), dbank[2][:, :], 1.0, 0).then_inc(k_root, 1)
                            if step == 24:
                                act.wait_ge(mdif_ready, nxt + 1)
                                nc.scalar.activation(mx[:, :], mx[:, :], ACT.Exp, scale=-1.0).then_inc(mx_ready, 1)
                            if step == 25:
                                copy(cols4(tm[:, :, :], 1, 1), const_cols(ident, 1, 1)).then_inc(tm_set, 1)
                                act.wait_ge(dif_ready, nxt + 1)
                                xtn = flat(xt[:, nxt % 2, :, :])
                                nc.scalar.activation(xtn, xtn, ACT.Exp, scale=-1.0).then_inc(xd_ready, 1)
                                nc.scalar.activation(flat(eg), dbank[1][:, :], ACT.Exp).then_inc(egc_ready, 1)
                        if h >= 0:
                            if step == 27:
                                act.wait_ge(o_sums, h + 1)
                                inverse_root(flat(osq), dbank[2][:, :], 1.0, 1).then_inc(o_root, 1)
                                act.wait_ge(ogf_ready, h + 1)
                                copy(og_hi[:, h, :], flat(xd)).then_inc(oghi_ready, 1)
                        yield

            def evacuate(n, kind, m):
                p = big[n % 2]
                act.wait_ge(block_done, n + 1)
                if kind in ("q", "k", "v"):
                    c = conv_number(kind, m)
                    if c >= 2:
                        act.wait_ge(conv_ready, c - 1)
                    else:
                        act.wait_ge(zeroed, 1)
                    copy(raw[:, c % 2, 3:3 + HALF], p[0][:, 0:HALF])
                    copy(raw[:, c % 2, 3 + HALF:3 + L], p[1][:, 0:HALF]).then_inc(raw_ready, 1)
                if kind == "c":
                    if m:
                        act.wait_ge(yblo_ready, m)
                    copy(cbuf[:, 0:HALF], p[0][:, 0:HALF])
                    copy(cbuf[:, HALF:L], p[1][:, 0:HALF]).then_inc(c_ready, 1)
                if kind == "z":
                    if m >= 2:
                        act.wait_ge(oglo_ready, m - 1)
                    nc.scalar.activation(zs[:, m % 2, :], p[0][:, :], ACT.Silu).then_inc(zs_ready, 1)
                if kind in ("gb", "ga"):
                    i = gate_number(kind, m)
                    if i >= 2:
                        wait_gate_used(act, i - 2)
                    else:
                        act.wait_ge(qdec_ready, HEADS)
                    nc.scalar.activation(egate[:, i % 2, :], p[0][:, :], ACT.Sigmoid).then_inc(ge_ready, 1)
                if kind == "gate" and m == 0:
                    act.wait_ge(h_sums, 1)
                    inverse_root(rs2[:, :], dbank[0][:, :], 1.0 / D, 0).then_inc(rs2_ready, 1)
                yield
                if kind in ("b", "dn"):
                    i = m if kind == "b" else KT + m
                    act.wait_ge(yb_ready, i + 1)
                    copy(yb_hi[:, m, :], ybf).then_inc(ybhi_ready, 1)
                if kind == "wo":
                    act.wait_ge(h1_ready, m + 1)
                    nc.scalar.activation(og_hi[:, m, :], h1[:, m, :], ACT.Copy,
                                         scale=sm[:, NORM2 + m:NORM2 + m + 1]).then_inc(hnhi_ready, 1)
                    if m >= 2:
                        act.wait_ge(sqa_ready, m - 1)
                    nc.scalar.activation(sqt[:, m % 2, :], h1[:, m, :], ACT.Square).then_inc(sqt_ready, 1)
                if kind == "gate":
                    act.wait_ge(tg_ready, m + 1)
                    if m:
                        act.wait_ge(f_ready, m)
                    nc.scalar.activation(sg[:, :], tg[:, :], ACT.Silu).then_inc(sg_ready, 1)
                if kind == "up":
                    act.wait_ge(f_ready, m + 1)
                    copy(f_hi[:, m, :], ff[:, :]).then_inc(fhi_ready, 1)

            def silu(kind, h):
                i = ("q", "k", "v").index(kind)
                c = conv_number(kind, h)
                act.wait_ge(conv_ready, c + 1)
                if h:
                    act.wait_ge(qdec_ready, h)
                    act.wait_ge(qk_done, h)
                nc.scalar.activation(qkv[:, i, :], cv[:, c % 2, :], ACT.Silu).then_inc(qkv_ready, 1)

            delta = delta_steps()
            for n in range(STREAM + 1):
                chores = evacuate(n - 1, *BLOCKS[n - 1]) if 1 <= n <= MAIN else iter(())
                for q in range(4):
                    weights_first = n < MAIN and BLOCKS[n][0] == "u"
                    if q in (1, 2) and weights_first:
                        split_weights(n + 1, q - 1)
                    weights_at_once = n == AT["up", 0]
                    if q == 0 and weights_at_once:
                        split_weights(n + 1, 0)
                        split_weights(n + 1, 1)
                    if n >= DELTA_FROM:
                        next(delta, None)
                    next(chores, None)
                    if q in (1, 2) and n + 1 < STREAM and not weights_first and not weights_at_once:
                        split_weights(n + 1, q - 1)
                    if q == 0 and 2 <= n and n - 2 < MAIN and BLOCKS[n - 2][0] in ("q", "k", "v"):
                        silu(*BLOCKS[n - 2])
                    if q == 2 and n in EXP_LN_FROM:
                        nc.scalar.preload_act_table_set("natural_log_exp_and_others")
                if n == 1:
                    token_factors()
                if n == 2:
                    token_decays()
                if n == AT["gb", 4]:
                    act.wait_ge(oglo_ready, HEADS)
                    act.dma_start(h1[:, :, :], h_t[:, :, META:L]).then_inc(h_again, 16)
                if n in DOWN_ENDS:
                    m = DOWN_ENDS[n]
                    act.wait_ge(h2_ready, m + 1)
                    if m >= 2:
                        act.wait_ge(sqf_ready, m - 1)
                    nc.scalar.activation(sqt[:, m % 2, :], h1[:, m, :], ACT.Square).then_inc(h2_squared, 1)
            act.wait_ge(last_sums, 1)
            inverse_root(rs2[:, :], dbank[0][:, :], 1.0 / D, 0).then_inc(rs2_ready, 1)

        @block.vector
        def _(dve):
            chain = [0]

            def link(ins):
                chain[0] += 1
                ins.then_inc(dve_chain, 1)
                dve.wait_ge(dve_chain, chain[0])

            def mult(to, a, b):
                return nc.vector.tensor_tensor(to, a, b, ALU.mult)

            for k in range(1, KT):
                dve.wait_ge(x_squared, k + 1)
                if k > 1:
                    dve.wait_ge(x_added, k - 1)
                nc.vector.tensor_tensor(sums1, xnf[0] if k == 1 else sums1, xnf[k % 4], ALU.add).then_inc(x_added, 1)
            dve.wait_ge(small_in, 16)
            link(nc.vector.tensor_scalar(on_scaled[:, :], sm[:, ONORM:ONORM + 1], float(128) ** 0.5, None, ALU.mult))
            dve.wait_ge(rs1_ready, 1)
            for k in range(KT + 2):
                if k < KT:
                    if k >= 4:
                        dve.wait_ge(xlo_ready if k % 2 else xlo_even, k // 2 - 1)
                    nc.vector.scalar_tensor_tensor(xnf[k % 4], h_in[:, k, :], sm[:, NORM1 + k:NORM1 + k + 1], rs1[:, :],
                                                   ALU.mult, ALU.mult).then_inc(xn_ready, 1)
                if k >= 2 and k % 2 == 0:
                    dve.wait_ge(xhi_ready, k - 1)
                    nc.vector.tensor_tensor(x_lo[:, k - 2, :], xnf[(k - 2) % 4], x_hi[:, k - 2, :].bitcast(f32),
                                            ALU.subtract).then_inc(xlo_even, 1)
            dve.wait_ge(wba_hi_ready, 1)
            nc.vector.tensor_tensor(wba_lo[:, :, :].rearrange("p k c -> p (k c)"), wba[:, :],
                                    wba_hi[:, :, :].rearrange("p k c -> p (k c)").bitcast(f32), ALU.subtract).then_inc(wba_ready, 1)

            def token_factors():
                dve.wait_ge(ba_done, 1)
                dve.wait_ge(eb_ready, 1)
                ba = dbank[2][:, 0:16 * (NJ + 1)].rearrange("p (j c) -> p j c", c=16)
                dtb = sm[:, DTB:DTB + HEADS].unsqueeze(1).broadcast_to([128, NJ + 1, HEADS])
                nc.vector.tensor_tensor(ga1[:, :, :], ba[:, :, HEADS:16], dtb, ALU.add).then_inc(az_ready, 1)
                dve.wait_ge(eb_ready, 2)
                link(nc.vector.tensor_scalar(beta[:, :, :], beta[:, :, :], 1.0, None, ALU.add))
                link(nc.vector.reciprocal(beta[:, :, :], beta[:, :, :]))
                link(nc.vector.tensor_scalar(nea[:, :], nea[:, :], -1.0, None, ALU.mult))
                dve.wait_ge(ln_ready, 1)
                link(nc.vector.tensor_scalar(ga1[:, :, :], ga1[:, :, :], 0.0, None, ALU.max))
                link(nc.vector.tensor_tensor(ga1[:, :, :], ga1[:, :, :], ga2[:, :, :], ALU.add))
                mult(g[:, :, :], ga1[:, :, :], nea[:, :].unsqueeze(1).broadcast_to([128, NJ + 1, HEADS])).then_inc(g_ready, 1)

            def token_decays():
                dve.wait_ge(exps_ready, 1)
                nc.vector.tensor_tensor(ga2[:, 1:, :].bitcast(f32r), gc[:, 1:, :], ga1[:, 1:, :], ALU.subtract)
                mult(be[:, :, :], be[:, :, :], beta[:, 1:, :]).then_inc(tokens_ready, 1)

            def low_part(low, x, high):
                return nc.vector.tensor_tensor(flat(low), flat(x), flat(high).bitcast(f32), ALU.subtract)

            def delta_steps():
                def chunks(t):
                    return t[:, :].rearrange("p (j c) -> p j c", c=128)

                mbank = dbank[2]
                for h in range(-1, HEADS):
                    nxt = h + 1
                    for step in range(0 if h >= 0 else PRE, STEPS):
                        if step == 0:
                            dve.wait_ge(kk_done, h + 1)
                            dve.wait_ge(xb_ready, h + 1)
                            mult(flat(am), dbank[1][:, :], flat(am)).then_inc(a_ready, 1)
                            dve.wait_ge(a_ready, h + 1)
                            dve.wait_ge(tm_set, h + 1)
                            t = cols4(tm[:, :, :], 1, 0)
                            link(mult(t, cols4(am[:, :, :], 1, 0), const_cols(cst[:, CLEV, :], 1, 0)))
                            nc.vector.tensor_tensor(t, const_cols(ident, 1, 0), t, ALU.subtract).then_inc(t_ready, 1)
                            dve.wait_ge(mpre_done, h + 1)
                            dve.wait_ge(mx_ready, h + 1)
                            nc.vector.scalar_tensor_tensor(ma[:, :], mbank[0:META, 256:272], beta[0:META, 0, h:h + 1], mx[:, :],
                                                           ALU.mult, ALU.mult).then_inc(ma_ready, 1)
                            nc.vector.tensor_scalar(mkdec[:, :], mbank[0:META, 0:128], erev[0:META, 0, h:h + 1], None, ALU.mult)
                            nc.vector.tensor_scalar(mvb[:, :], mbank[0:META, 128:256], beta[0:META, 0, h:h + 1], None,
                                                    ALU.mult).then_inc(mkv_ready, 1)
                        if step == 1:
                            dve.wait_ge(t_ready, h + 1)
                            nc.vector.transpose(flat(um), flat(tm)).then_inc(u_ready, 1)
                        if step == 2:
                            dve.wait_ge(qk_done, h + 1)
                            dve.wait_ge(xt_ready, h + 1)
                            xth = flat(xt[:, h % 2, :, :])
                            mult(xth, dbank[3][:, :], xth).then_inc(qkt_ready, 1)
                        if 4 <= step <= 14 and step % 2 == 0:
                            l = (step - 4) // 2
                            b = LEVELS[l]
                            dve.wait_ge(du_done, len(LEVELS) * h + l + 1)
                            if l == META_LEVELS + 2:
                                nc.vector.tensor_copy(state[:, :], mbank[:, 256:384]).then_inc(state_ready, 1)
                            if 1 <= l <= META_LEVELS:
                                mb = LEVELS[l - 1]
                                u = cols(mu[:, :], mb, 1)
                                nc.vector.tensor_tensor(u, u, mbank[0:META, 256:264].rearrange("p (g b) -> p g b", b=mb), ALU.subtract)
                            if 1 <= l < META_LEVELS:
                                t = cols(mt[:, :], mb, 0)
                                nc.vector.tensor_tensor(t, t, dbank[3][0:META, 256:264].rearrange("p (g b) -> p g b", b=mb), ALU.subtract)
                            if l >= MASKED:
                                for first, second, at in level_blocks(b):
                                    u = um[first, :, second]
                                    ins = nc.vector.tensor_tensor(u, u, compact(mbank)[first, :, at], ALU.subtract)
                                ins.then_inc(u_updated, 1)
                                if l < len(LEVELS) - 1:
                                    for first, second, at in level_blocks(b)[:1]:
                                        t = tm[second, :, first]
                                        ins = nc.vector.tensor_tensor(t, t, compact(dbank[3])[second, :, at], ALU.subtract)
                                    ins.then_inc(t_updated, 1)
                            else:
                                u = cols(flat(um), b, 1)
                                nc.vector.tensor_tensor(u, u, mbank[:, 0:256].rearrange("p (g b) -> p g b", b=b),
                                                        ALU.subtract).then_inc(u_updated, 1)
                                dve.wait_ge(u_updated, len(LEVELS) * h + l + 1)
                                nc.vector.transpose(flat(tm), flat(um)).then_inc(t_updated, 1)
                        if 17 <= step <= 21 and step % 2 and h >= 0:
                            j = (step - 17) // 2
                            dve.wait_ge(ds_done, (NJ - 1) * h + j + 1)
                            dve.wait_ge(state_ready, NJ * h + j + 1)
                            nc.vector.scalar_tensor_tensor(state[:, :], state[:, :], etot[:, j, h:h + 1], mbank[:, 0:128],
                                                           ALU.mult, ALU.add).then_inc(state_ready, 1)
                        if step == 25 and h >= 0:
                            dve.wait_ge(o_squared, h + 1)
                            low_part(o_lo, osq, qo_hi).then_inc(o_split, 1)
                        if nxt < HEADS:
                            xtn = xt[:, nxt % 2, :, :]
                            if step == 21:
                                dve.wait_ge(q_squared, nxt + 1)
                                low_part(q_lo, xd, qo_hi).then_inc(q_split, 1)
                            if step == 22:
                                dve.wait_ge(k_squared, nxt + 1)
                                low_part(k_lo, am, k_hi).then_inc(k_split, 1)
                            if step == 23:
                                dve.wait_ge(km_copied, nxt + 1)
                                link(nc.vector.tensor_tensor(mx[:, :], mx[:, :], gc[0:META, 0, nxt:nxt + 1].broadcast_to([META, META]),
                                                             ALU.subtract))
                                nc.vector.scalar_tensor_tensor(mx[:, :], mx[:, :], -1.0, mx[:, :], ALU.mult,
                                                               ALU.max).then_inc(mdif_ready, 1)
                            if step == 24:
                                dve.wait_ge(q_root, nxt + 1)
                                nc.vector.scalar_tensor_tensor(qkv[:, 0, META:L], qkv[:, 0, META:L], float(128) ** -0.5, flat(xd),
                                                               ALU.mult, ALU.mult).then_inc(q_ready, 1)
                                dve.wait_ge(gc_spread, nxt + 1)
                                link(nc.vector.tensor_tensor(xtn, chunks(dbank[1]), per_chunk(gc, nxt, 1), ALU.subtract))
                                nc.vector.scalar_tensor_tensor(flat(xtn), flat(xtn), -1.0, flat(xtn), ALU.mult,
                                                               ALU.max).then_inc(dif_ready, 1)
                            if step == 25:
                                dve.wait_ge(k_root, nxt + 1)
                                mult(qkv[:, 1, 0:META], qkv[:, 1, 0:META], sqm[:, :])
                                mult(qkv[:, 1, META:L], qkv[:, 1, META:L], flat(am)).then_inc(k_ready, 1)
                                dve.wait_ge(xd_ready, nxt + 1)
                                dve.wait_ge(k_ready, nxt + 1)
                                mult(am[:, :, :], xtn, per_chunk(beta, nxt, 1)).then_inc(xb_ready, 1)
                                mult(xtn, xtn, all_chunks(tri)).then_inc(xt_ready, 1)
                            if step == 26:
                                dve.wait_ge(v_turned, nxt + 1)
                                mult(vb[:, :, :], chunks(dbank[0]), per_chunk(beta, nxt, 1)).then_inc(vb_ready, 1)
                        if step == 27 and h >= 0:
                            if nxt < HEADS:
                                dve.wait_ge(q_ready, nxt + 1)
                            dve.wait_ge(o_root, h + 1)
                            link(nc.vector.scalar_tensor_tensor(flat(xd), dbank[3][:, :], on_scaled[:, 0:1], flat(osq), ALU.mult,
                                                                ALU.mult))
                            dve.wait_ge(zs_ready, h + 1)
                            mult(flat(xd), flat(xd), zs[:, h % 2, :]).then_inc(ogf_ready, 1)
                        yield

            def convolve(c, first_column, taps):
                to, x = cv[:, c % 2, :], raw[:, c % 2, :]
                n = taps.shape[1]
                for j in range(n):
                    xj = x[:, first_column + j:first_column + j + L]
                    if j == 0:
                        ins = nc.vector.tensor_scalar(to, xj, taps[:, 0:1], None, ALU.mult)
                    else:
                        ins = nc.vector.scalar_tensor_tensor(to, xj, taps[:, j:j + 1], to, ALU.mult, ALU.add)
                    if j < n - 1:
                        link(ins)
                        yield
                ins.then_inc(conv_ready, 1)

            def evacuate(n, kind, m):
                p = big[n % 2]
                dve.wait_ge(block_done, n + 1)
                if kind in ("q", "k", "v"):
                    i = ("q", "k", "v").index(kind)
                    c = conv_number(kind, m)
                    dve.wait_ge(raw_ready, 3 * m + i + 1)
                    if c < 2:
                        dve.wait_ge(xlo_ready, KT // 2)
                        dve.wait_ge(xlo_even, KT // 2)
                    elif kind != "k":
                        dve.wait_ge(qkv_ready, 3 * m + (i > 0))
                    yield from convolve(c, 0, sm[:, CQKV + 4 * (8 * i + m):CQKV + 4 * (8 * i + m) + 4])
                if kind == "u":
                    c = conv_number(kind, m)
                    dve.wait_ge(c_ready, m + 1)
                    if m == 0:
                        dve.wait_ge(zeroed, 1)
                    mult(raw[:, c % 2, 3:3 + HALF], p[0][:, 0:HALF], cbuf[:, 0:HALF])
                    mult(raw[:, c % 2, 3 + HALF:3 + L], p[1][:, 0:HALF], cbuf[:, HALF:L]).then_inc(c_used, 1)
                    dve.wait_ge(c_used, m + 1)
                    yield
                    dve.wait_ge(qkv_ready, 3 * m + 2)
                    yield from convolve(c, 1, sm[:, CSC + 3 * m:CSC + 3 * m + 3])
                if kind == "b":
                    if m:
                        dve.wait_ge(yblo_ready, m)
                    dve.wait_ge(conv_ready, 4 * m + 4)
                    mult(ybf, p[0][:, :], cv[:, conv_number("u", m) % 2, META:L]).then_inc(yb_ready, 1)
                if kind == "sc":
                    i = gate_number("gb", m)
                    dve.wait_ge(ge_ready, i + 1)
                    mult(mixb[:, m, 0:T], p[0][:, :], egate[:, i % 2, :]).then_inc(mixb_ready, 1)
                if kind == "dn":
                    i = gate_number("ga", m)
                    dve.wait_ge(ge_ready, i + 1)
                    dve.wait_ge(yblo_ready, KT + m)
                    mult(ybf, p[0][:, :], egate[:, i % 2, :]).then_inc(dn_gated, 1)
                    dve.wait_ge(dn_gated, m + 1)
                    dve.wait_ge(mixb_ready, m + 1)
                    nc.vector.tensor_tensor(ybf, ybf, mixb[:, m, 0:T], ALU.add).then_inc(yb_ready, 1)
                    if m == KT - 1:
                        dve.wait_ge(ybhi_ready, 2 * KT)
                        nc.vector.tensor_tensor(yb_lo[:, m, :], ybf, yb_hi[:, m, :].bitcast(f32), ALU.subtract).then_inc(yblo_last, 1)
                if kind == "wo":
                    dve.wait_ge(h_again, 16)
                    nc.vector.tensor_tensor(h1[:, m, :], p[0][:, :], h1[:, m, :], ALU.add).then_inc(h1_ready, 1)
                    dve.wait_ge(hnhi_ready, m + 1)
                    nc.vector.scalar_tensor_tensor(og_lo[:, m, :], h1[:, m, :], sm[:, NORM2 + m:NORM2 + m + 1],
                                                   og_hi[:, m, :].bitcast(f32), ALU.mult, ALU.subtract).then_inc(hnlo_ready, 1)
                if kind == "gate":
                    if m == 0:
                        dve.wait_ge(rs2_ready, 1)
                    else:
                        dve.wait_ge(sg_ready, m)
                    mult(tg[:, :], p[0][:, :], rs2[:, :]).then_inc(tg_ready, 1)
                    yield
                    dve.wait_ge(sg_ready, m + 1)
                    mult(sg[:, :], sg[:, :], rs2[:, :]).then_inc(sg2_ready, 1)
                if kind == "up":
                    if m:
                        dve.wait_ge(flo_ready, m)
                    dve.wait_ge(sg2_ready, m + 1)
                    mult(ff[:, :], p[0][:, :], sg[:, :]).then_inc(f_ready, 1)

            delta = delta_steps()
            for n in range(STREAM + 1):
                chores = evacuate(n - 1, *BLOCKS[n - 1]) if 1 <= n <= MAIN else iter(())
                for q in range(4):
                    if n >= DELTA_FROM:
                        next(delta, None)
                    next(chores, None)
                next(chores, None)
                if n == 0:
                    dve.wait_ge(bat_done, 1)
                    for s in range(2):
                        ins = nc.vector.tensor_copy(bat[:, s * HALF:(s + 1) * HALF], dbank[s][0:16, 0:HALF])
                    ins.then_inc(bat_copied, 1)
                if n == 1:
                    token_factors()
                if n == 2:
                    token_decays()
                if n in DOWN_ENDS:
                    m = DOWN_ENDS[n]
                    if FT * (m + 1) % 8 == 0:
                        dve.wait_ge(block_done, n)
                    else:
                        dve.wait_ge(down_done, m + 1 - sum(FT * (i + 1) % 8 == 0 for i in range(m)))
                    nc.vector.tensor_tensor(h1[:, m, :], big[m % 2][0][:, :], h1[:, m, :], ALU.add).then_inc(h2_ready, 1)
            dve.wait_ge(rs2_ready, 2)
            for m in range(KT):
                nc.vector.scalar_tensor_tensor(h1[:, m, :], h1[:, m, :], sm[:, NORMF + m:NORMF + m + 1], rs2[:, :], ALU.mult,
                                               ALU.mult).then_inc(y_ready, 1)

        @block.tensor
        def _(pe):
            def mm(o, w, x, start=True, stop=True):
                return nc.tensor.matmul(o, w, x, start=start, stop=stop)

            def products(outs, n, tile, x_h, x_l, first, last):
                wh = w_hi[:, n % 2, tile * 128:(tile + 1) * 128]
                wl = w_lo[:, n % 2, tile * 128:(tile + 1) * 128]
                for w, xs, a in ((wh, x_h, 0), (wh, x_l, 1), (wl, x_h, 2)):
                    for o, x in zip(outs, xs):
                        ins = mm(o, w, x, start=first and a == 0, stop=last and a == 2)
                return ins

            pe.wait_ge(ones_split, 1)
            for _ in range(WARM):
                mm(dbank[3][:, 0:128], ones, ones)
            pe.wait_ge(x_added, KT - 1)
            for s in range(2):
                ins = mm(big[0][s][:, 0:HALF], ones, sums1[:, s * HALF:(s + 1) * HALF])
            ins.then_inc(x_sums, 1)
            for _ in range(WARM // 3):
                mm(dbank[3][:, 0:128], ones, ones)

            def token_projections():
                pe.wait_ge(wba_ready, 1)
                for k in range(KT):
                    for w, x, a in ((wba_hi, x_hi, 0), (wba_hi, x_lo, 1), (wba_lo, x_hi, 2)):
                        for s in range(2):
                            ins = mm(dbank[s][0:16, 0:HALF], w[:, k, :], x[:, k, s * HALF:(s + 1) * HALF],
                                     start=k == 0 and a == 0, stop=k == KT - 1 and a == 2)
                ins.then_inc(bat_done, 1)

            def turn_token_projections():
                pe.wait_ge(const_in, 16)
                pe.wait_ge(bat_copied, 1)
                for j in range(NJ + 1):
                    at = slice(0, 128) if j == 0 else slice(META + 128 * (j - 1), META + 128 * j)
                    ins = nc.tensor.transpose(dbank[2][:, 16 * j:16 * j + 16], bat[:, at], ident[0:16, 0:16])
                ins.then_inc(ba_done, 1)

            def token_sums():
                pe.wait_ge(g_ready, 1)
                gs = g[:, 1:, :].rearrange("p j h -> p (j h)")
                mm(dbank[1][:, 0:32], tri, gs)
                mm(dbank[1][:, 32:64], rev, gs)
                mm(dbank[1][:, 64:96], ones, gs)
                mm(dbank[1][0:META, 96:104], tri[0:META, 0:META], g[0:META, 0, :])
                mm(dbank[1][0:META, 104:112], rev[0:META, 0:META], g[0:META, 0, :]).then_inc(cums_done, 1)

            def spread_sums(o, high, low):
                mm(o[:, :], ones_r[:, :], high, stop=False)
                return mm(o[:, :], ones_r[:, :], low, start=False)

            def clear(o):
                mm(o[:, 0:256].rearrange("p (a c) -> p a c", c=128), zeros_r[:, :],
                   zeros_r[:, :].unsqueeze(1).broadcast_to([128, 2, 128]))

            def delta_steps():
                turn = nc.tensor.transpose
                c128 = [slice(128 * j, 128 * (j + 1)) for j in range(NJ)]
                c64 = [slice(64 * j, 64 * (j + 1)) for j in range(NJ)]
                tiles32 = [(slice(32 * i, 32 * (i + 1)), slice(16 * i, 16 * (i + 1))) for i in range(4)]
                tok = [slice(META + 128 * j, META + 128 * (j + 1)) for j in range(NJ)]
                qh, kh, vh = qkv[:, 0, :], qkv[:, 1, :], qkv[:, 2, :]
                for h in range(-1, HEADS):
                    nxt = h + 1
                    for step in range(0 if h >= 0 else PRE, STEPS):
                        if step == 0:
                            pe.wait_ge(k_ready, h + 1)
                            pe.wait_ge(egc_ready, h + 1)
                            for j in range(NJ):
                                ins = mm(dbank[1][:, c128[j]], kh[:, tok[j]], kh[:, tok[j]])
                            ins.then_inc(kk_done, 1)
                            if h:
                                pe.wait_ge(o_root, h)
                            turn(dbank[2][:, 0:128], kh[:, 0:128], ident)
                            turn(dbank[2][:, 128:256], vh[:, 0:128], ident)
                            mm(dbank[2][0:META, 256:272], kh[:, 0:META], kh[:, 0:META]).then_inc(mpre_done, 1)
                            pe.wait_ge(vb_ready, h + 1)
                            for j in range(NJ):
                                ins = turn(dbank[0][:, c128[j]], kh[:, tok[j]], ident)
                            ins.then_inc(k_turned, 1)
                        if step == 1:
                            pe.wait_ge(q_ready, h + 1)
                            if h:
                                pe.wait_ge(ogf_ready, h)
                            for j in range(NJ):
                                ins = mm(dbank[3][:, c128[j]], kh[:, tok[j]], qh[:, tok[j]])
                            ins.then_inc(qk_done, 1)
                        if step == 4:
                            pe.wait_ge(zeros_ready, 1)
                        if 3 <= step <= 13 and step % 2:
                            l = (step - 3) // 2
                            b = LEVELS[l]
                            done = len(LEVELS) * h + l
                            if l == 0:
                                pe.wait_ge(u_ready, h + 1)
                            else:
                                pe.wait_ge(u_updated, done)
                            if l < MASKED:
                                pe.wait_ge(alev_ready, MASKED * h + l + 1)
                            if l == META_LEVELS + 2:
                                pe.wait_ge(mv_ready, h + 1)
                            if l == 1:
                                pe.wait_ge(mu_ready, h + 1)
                            if 1 <= l <= META_LEVELS:
                                mm(dbank[1][0:META, 256:264], malev[:, l - 1, :], cols(mu[:, :], LEVELS[l - 1], 1))
                            for j in range(NJ):
                                if l < MASKED:
                                    for rows, at in tiles32:
                                        ins = mm(compact(dbank[1])[rows, j, at], alev[rows, l, j, rows],
                                                 cols(um[rows, j, rows], b, 1))
                                else:
                                    for first, second, at in level_blocks(b):
                                        ins = mm(compact(dbank[1])[first, j, at], am[second, j, first], um[second, j, second])
                            ins.then_inc(p_done, 1)
                        if 4 <= step <= 14 and step % 2 == 0:
                            l = (step - 4) // 2
                            b = LEVELS[l]
                            done = len(LEVELS) * h + l
                            pe.wait_ge(pb_ready, done + 1)
                            if l == 0:
                                pe.wait_ge(mt_ready, h + 1)
                                pe.wait_ge(kd_ready, h + 1)
                                mm(dbank[0][0:META, 0:META], mt[:, :], ident[0:META, 0:META]).then_inc(mt_turned, 1)
                                pe.wait_ge(mkv_ready, h + 1)
                                pe.wait_ge(qkt_ready, h + 1)
                            else:
                                pe.wait_ge(t_updated, (len(LEVELS) - 1) * h + l)
                            if l == META_LEVELS + 1:
                                mm(dbank[1][0:META, 256:384], mu[:, :], mvb[:, :]).then_inc(mv_done, 1)
                            if l == META_LEVELS + 2:
                                mm(dbank[2][:, 256:384], mkdec[:, :], mvnew)
                            if 1 <= l <= META_LEVELS:
                                mm(dbank[2][0:META, 256:264], mt[:, :], cols(mpb[:, l - 1, :], LEVELS[l - 1], 1))
                            if 1 <= l < META_LEVELS:
                                mm(dbank[3][0:META, 256:264], mpb[:, l - 1, :], cols(mt[:, :], LEVELS[l - 1], 0))
                            if l == 0:
                                clear(dbank[2])
                            for j in range(NJ):
                                if l < MASKED:
                                    for rows, at in tiles32:
                                        ins = mm(compact(dbank[2])[rows, j, at], tm[rows, j, rows],
                                                 cols(pb[rows, l, j, rows], b, 1))
                                else:
                                    for first, second, at in level_blocks(b):
                                        ins = mm(compact(dbank[2])[first, j, at], tm[first, j, first], pbx[first, j, second])
                                    if l < len(LEVELS) - 1:
                                        for first, second, at in level_blocks(b)[:1]:
                                            ins = mm(compact(dbank[3])[second, j, at], pbx[first, j, second],
                                                     tm[first, j, first])
                            ins.then_inc(du_done, 1)
                        if step == 15:
                            pe.wait_ge(u_updated, len(LEVELS) * (h + 1))
                            for j in range(NJ):
                                ins = mm(dbank[0][:, c128[j]], kbe[:, j, :], um[:, j, :])
                            ins.then_inc(w_done, 1)
                        if step == 22 and nxt < HEADS:
                            if h < 0:
                                pe.wait_ge(tokens_ready, 1)
                            pe.wait_ge(q_split, nxt + 1)
                            spread_sums(dbank[0], flat(qo_hi), flat(q_lo)).then_inc(q_sums, 1)
                        if 16 <= step <= 22 and step % 2 == 0 and h >= 0:
                            j = (step - 16) // 2
                            if j == 0:
                                pe.wait_ge(nwt_ready, h + 1)
                                pe.wait_ge(qdec_ready, h + 1)
                            if j == NJ - 1 and nxt < HEADS:
                                pe.wait_ge(km_copied, nxt + 1)
                            pe.wait_ge(state_ready, NJ * h + j + 1)
                            mm(dbank[1][:, 0:128], um[:, j, :], vb[:, j, :], stop=False)
                            mm(dbank[1][:, 0:128], nwt[:, j, :], state[:, :], start=False).then_inc(vn_done, 1)
                            mm(dbank[3][:, c128[j]], state[:, :], qdec[:, j, :], stop=False)
                        if 17 <= step <= 23 and step % 2 and h >= 0:
                            j = (step - 17) // 2
                            pe.wait_ge(vn_ready, NJ * h + j + 1)
                            if j < NJ - 1:
                                mm(dbank[2][:, 0:128], kdec[:, j, :], vnew[:, :]).then_inc(ds_done, 1)
                            ins = mm(dbank[3][:, c128[j]], vnew[:, :], xt[:, h % 2, j, :], start=False)
                            if j == NJ - 1:
                                ins.then_inc(o_done, 1)
                        if nxt < HEADS:
                            if step == 21:
                                if h >= 0:
                                    pe.wait_ge(vn_ready, NJ * (h + 1) - 1)
                                else:
                                    pe.wait_ge(tokens_ready, 1)
                                pe.wait_ge(km_squared, nxt + 1)
                                pe.wait_ge(mdiag_ready, nxt + 1)
                                mm(dbank[1][0:META, 272:288], ones[0:META, 0:META], mdg[:, :])
                                mm(dbank[1][:, 256:256 + META], ones, sqm[:, :]).then_inc(km_sums, 1)
                            if step == 23:
                                pe.wait_ge(diag_ready, nxt + 1)
                                pe.wait_ge(km_copied, nxt + 1)
                                if h >= 0:
                                    pe.wait_ge(vn_ready, NJ * (h + 1))
                                spread_sums(dbank[1], flat(dg_hi), flat(dg_lo[:, nxt % 2, :, :])).then_inc(gc_spread, 1)
                                pe.wait_ge(k_split, nxt + 1)
                                if h >= 0:
                                    pe.wait_ge(state_ready, NJ * (h + 1))
                                spread_sums(dbank[2], flat(k_hi), flat(k_lo)).then_inc(k_sums, 1)
                        if step == 26 and h >= 0:
                            pe.wait_ge(o_split, h + 1)
                            if nxt < HEADS:
                                pe.wait_ge(k_root, nxt + 1)
                            spread_sums(dbank[2], flat(qo_hi), flat(o_lo)).then_inc(o_sums, 1)
                        if step == 24 and nxt < HEADS:
                            pe.wait_ge(q_root, nxt + 1)
                            pe.wait_ge(qkv_ready, 3 * nxt + 3)
                            for j in range(NJ):
                                ins = turn(dbank[0][:, c128[j]], vh[:, tok[j]], ident)
                            ins.then_inc(v_turned, 1)
                        yield

            delta = delta_steps()
            for n, (kind, m) in enumerate(BLOCKS):
                x_h, x_l = {"sc": (yb_hi, yb_lo), "dn": (og_hi, og_lo), "wo": (yb_hi, yb_lo), "gate": (og_hi, og_lo),
                            "up": (og_hi, og_lo)}.get(kind, (x_hi, x_lo))
                if n >= 2:
                    wait_result_read(pe, *BLOCKS[n - 2])
                if kind == "dn":
                    pe.wait_ge(oglo_ready, KT)
                if kind in WIDE:
                    parts = [slice(0, HALF), slice(HALF, L)]
                    outs = [big[n % 2][s][:, 0:HALF] for s in range(2)]
                else:
                    off = META if x_h is x_hi else 0
                    parts = [slice(off, off + T)]
                    outs = [big[n % 2][0][:, :]]
                for k in range(KT):
                    if k % 4 == 0:
                        pe.wait_ge(wlo_ready, 2 * n + k // 4 + 1)
                    if n == 0:
                        pe.wait_ge(xlo_ready if k % 2 else xlo_even, k // 2 + 1)
                    if kind in ("sc", "wo") and m == 0:
                        if kind == "wo" and k == KT - 1:
                            pe.wait_ge(yblo_last, 1)
                        else:
                            pe.wait_ge(yblo_ready, (KT if kind == "wo" else 0) + k + 1)
                    if kind == "gate" and m == 0:
                        pe.wait_ge(hnlo_ready, k + 1)
                    ins = products(outs, n, k, [x_h[:, k, s] for s in parts], [x_l[:, k, s] for s in parts], k == 0, k == KT - 1)
                    if k == KT - 1:
                        ins.then_inc(block_done, 1)
                    if n == 1 and k == 1:
                        turn_token_projections()
                    if kind == "up" and m == 0 and k == 3:
                        pe.wait_ge(sqa_ready, KT)
                        mm(dbank[0][:, :], ones, sqa[:, :]).then_inc(h_sums, 1)
                    if k % 2 and n >= DELTA_FROM:
                        next(delta, None)
                if n == 0:
                    token_projections()
                if n == 2:
                    token_sums()
            for d in range(DOWN):
                n = MAIN + d
                for i in range(8):
                    if i % 4 == 0:
                        pe.wait_ge(wlo_ready, 2 * n + i // 4 + 1)
                    if d == DOWN - 1 and i == 4:
                        pe.wait_ge(sqf_ready, KT - 1)
                        mm(dbank[0][:, :], ones, sqa[:, :], stop=False)
                    m, k = divmod(8 * d + i, FT)
                    if k == 0:
                        if m < 2:
                            wait_result_read(pe, *BLOCKS[MAIN + m - 2])
                        else:
                            pe.wait_ge(h2_ready, m - 1)
                    if m == 0:
                        pe.wait_ge(flo_ready, k + 1)
                    ins = products([big[m % 2][0][:, :]], n, i, [f_hi[:, k, :]], [f_lo[:, k, :]], k == 0, k == FT - 1)
                    if i == 7:
                        ins.then_inc(block_done, 1)
                    elif k == FT - 1:
                        ins.then_inc(down_done, 1)
            pe.wait_ge(h2_squared, KT)
            mm(dbank[0][:, :], ones, sqt[:, (KT - 1) % 2, :], start=False).then_inc(last_sums, 1)


def kernel(x, meta_tokens, norm1, w_in, conv_qkv, a_log, dt_bias, o_norm, w_dn_out, conv_sc, w_sc_out, w_o, norm2,
           w_gate_up, w_down, final_norm):
    import numpy as np
    import concourse.bacc as bacc
    from concourse.bass_utils import run_bass_kernel_spmd

    def tiles(w):
        w = np.asarray(w)
        return w.reshape(w.shape[0] // 128, 128, w.shape[1] // 128, 128).transpose(2, 1, 0, 3).reshape(
            w.shape[1] // 128, 128, w.shape[0])

    def vector(v):
        return np.asarray(v).reshape(-1, 128).T

    win = np.asarray(w_in[0])
    names = ("q", "k", "v", "z", "ba", "c", "u", "b", "ga", "gb")
    widths = [D] * 4 + [2 * HEADS] + [D] * 5
    start = dict(zip(names, np.cumsum([0] + widths[:-1])))
    mats = {k: tiles(win[:, start[k]:start[k] + D]) for k in names if k != "ba"}
    gu = np.asarray(w_gate_up[0])
    mats |= {"sc": tiles(w_sc_out[0]), "dn": tiles(w_dn_out[0]), "wo": tiles(w_o[0]),
             "gate": tiles(gu[:, :FF]), "up": tiles(gu[:, FF:])}
    down = tiles(w_down[0]).reshape(KT, 128, FT, 128).transpose(0, 2, 1, 3).reshape(DOWN, 8, 128, 128)
    down = down.transpose(0, 2, 1, 3).reshape(DOWN, 128, 1024)
    w_stream = np.concatenate([np.stack([mats[k][m] for k, m in BLOCKS]), down])
    w_ba = win[:, start["ba"]:start["ba"] + 16].reshape(KT, 128, 16).transpose(1, 0, 2).reshape(128, KT * 16)
    h_t = np.concatenate([np.asarray(meta_tokens), np.asarray(x[0])]).T.reshape(KT, 128, L).transpose(1, 0, 2)
    cq = np.asarray(conv_qkv[0]).T.reshape(24, 128, 4).transpose(1, 0, 2).reshape(128, 96)
    cs = np.asarray(conv_sc[0]).T.reshape(8, 128, 3).transpose(1, 0, 2).reshape(128, 24)
    small = np.concatenate([vector(norm1[0]), vector(norm2[0]), vector(final_norm), cq, cs, vector(o_norm[0]),
                            np.broadcast_to(np.asarray(a_log[0]), (128, HEADS)),
                            np.broadcast_to(np.asarray(dt_bias[0]), (128, HEADS))], axis=1)
    r = np.arange(128)
    row, col = r[:, None], r[None, :]
    consts = [row == col, row <= col, row > col]
    for b in [1] + LEVELS[:MASKED]:
        consts.append((row // (2 * b) == col // (2 * b)) & (row // b % 2 == 1) & (col // b % 2 == 0))
    consts = np.stack(consts, axis=1).astype(np.float32)

    arrays = {"h_t": h_t, "w_stream": w_stream, "w_ba": w_ba, "small": small, "consts": consts}
    arrays = {k: np.ascontiguousarray(a) for k, a in arrays.items()}
    nc = bacc.Bacc("TRN2", target_bir_lowering=False, num_devices=1)
    args = [nc.dram_tensor(k, a.shape, mybir.dt.from_np(a.dtype), kind="ExternalInput").ap() for k, a in arrays.items()]
    out = nc.dram_tensor("out", (128, KT, T), mybir.dt.float32, kind="ExternalOutput").ap()
    hybrid_block_kernel(nc, *args, out)
    y = run_bass_kernel_spmd(nc, [arrays], core_ids=[0]).results[0]["out"]
    return np.ascontiguousarray(y.transpose(2, 1, 0).reshape(1, T, D))
```
